# Optimizing a Trainium2 kernel written in Bass

```python
import math
import jax
import jax.numpy as jnp
from jax import lax
import numpy as np

D_MODEL = 1024
BATCH = 1
SEQ = 128
DEPTH = 2
DEC_BATCH = 1
DEC_SEQ = 256
PAST_LEN = 128

GRID_W = 64
EPS = 1e-6
MLA_HEADS = 16
Q_RANK = 384
KV_RANK = 128
NOPE_DIM = 64
ROPE_DIM = 32
V_DIM = 64
ROPE_THETA = 10000.0
Q_BLOCK = 128
SSD_HEADS = 16
SSD_HEAD_DIM = 64
SSD_INNER = SSD_HEADS * SSD_HEAD_DIM
SSD_GROUPS = 2
SSD_STATE = 128
SSD_CONV_W = 5
SSD_CHUNK = 128
SSD_XBC = SSD_INNER + 2 * SSD_GROUPS * SSD_STATE
CONV_CH = 1024
CONV_W = 31
PEER_HEADS = 8
PEER_DQ = 256
N_KEYS = 128
N_EXPERTS = N_KEYS * N_KEYS
PEER_TOPK = 16
PEER_BLOCK = 128
N_BRANCH = 3

OFF_CQ = 0
OFF_CKV = OFF_CQ + Q_RANK
OFF_KR = OFF_CKV + KV_RANK
OFF_Z = OFF_KR + ROPE_DIM
OFF_XBC = OFF_Z + SSD_INNER
OFF_DT = OFF_XBC + SSD_XBC
OFF_GLU = OFF_DT + 2 * SSD_HEADS
N_IN = OFF_GLU + 2 * CONV_CH

kernel_name = "hybrid_mla_ssd_conv_peer_diffusion_step"

def rmsnorm(x, g):
    xf = x.astype(jnp.float32)
    y = xf * lax.rsqrt(jnp.mean(xf * xf, axis=-1, keepdims=True) + EPS)
    return (y * g.astype(jnp.float32)).astype(x.dtype)

def layernorm(x, g, b):
    xf = x.astype(jnp.float32)
    mu = jnp.mean(xf, axis=-1, keepdims=True)
    xc = xf - mu
    y = xc * lax.rsqrt(jnp.mean(xc * xc, axis=-1, keepdims=True) + EPS)
    return (y * g.astype(jnp.float32) + b.astype(jnp.float32)).astype(x.dtype)

def modulation(cvec, w_mod, b_mod):
    m = (jax.nn.silu(cvec) @ w_mod + b_mod)[:, None, :]
    return jnp.split(m, 6, axis=-1)

def dwconv(x, w, b):
    k = w.shape[0]
    y = lax.conv_general_dilated(x, w[:, None, :].astype(x.dtype), (1,), [(k // 2, k // 2)],
                                 dimension_numbers=('NWC', 'WIO', 'NWC'),
                                 feature_group_count=x.shape[-1])
    return y + b

def axial_rope_tables(L):
    rows = L // GRID_W
    row = jnp.repeat(jnp.arange(rows), GRID_W).astype(jnp.float32)
    col = jnp.tile(jnp.arange(GRID_W), rows).astype(jnp.float32)
    nf = ROPE_DIM // 4
    inv = ROPE_THETA ** (-jnp.arange(nf, dtype=jnp.float32) / nf)
    ang = jnp.concatenate([row[:, None] * inv, col[:, None] * inv], axis=-1)
    return jnp.cos(ang), jnp.sin(ang)

def apply_axial_rope(x, cos, sin):
    shp = x.shape
    nf = ROPE_DIM // 4
    xs = x.astype(jnp.float32).reshape(shp[:-1] + (2, 2, nf))
    x1, x2 = xs[..., 0, :], xs[..., 1, :]
    bshape = (shp[1],) + (1,) * (x.ndim - 3) + (2, nf)
    c = cos.reshape(bshape)
    s = sin.reshape(bshape)
    out = jnp.stack([x1 * c - x2 * s, x2 * c + x1 * s], axis=-2)
    return out.reshape(shp).astype(x.dtype)

def mla_queries(cq, g_q_norm, w_uq):
    q = (rmsnorm(cq, g_q_norm) @ w_uq).reshape(cq.shape[:2] + (MLA_HEADS, NOPE_DIM + ROPE_DIM))
    return q[..., :NOPE_DIM], q[..., NOPE_DIM:]

def mla_kv(ckv_n, w_ukv):
    kv = (ckv_n @ w_ukv).reshape(ckv_n.shape[:2] + (MLA_HEADS, NOPE_DIM + V_DIM))
    return kv[..., :NOPE_DIM], kv[..., NOPE_DIM:]

def mla_attention(q_nope, q_rope, k_nope, k_rope, v):
    b, lq, h, _ = q_nope.shape
    nb = lq // Q_BLOCK
    scale = (NOPE_DIM + ROPE_DIM) ** -0.5

    def block(qs):
        qn, qr = qs
        s = (jnp.einsum('bqhd,bkhd->bhqk', qn, k_nope).astype(jnp.float32)
             + jnp.einsum('bqhr,bkr->bhqk', qr, k_rope).astype(jnp.float32))
        p = jax.nn.softmax(s * scale, axis=-1)
        return jnp.einsum('bhqk,bkhd->bqhd', p.astype(v.dtype), v)

    def to_blocks(t):
        return jnp.moveaxis(t.reshape((b, nb, Q_BLOCK) + t.shape[2:]), 1, 0)

    o = lax.map(block, (to_blocks(q_nope), to_blocks(q_rope)))
    return jnp.moveaxis(o, 0, 1).reshape(b, lq, h * V_DIM)

def ssd_chunked(x, dt, A, Bm, Cm, h0):
    f32 = jnp.float32
    b, L, H, P = x.shape
    G, N = Bm.shape[2], Bm.shape[3]
    hg = H // G
    nc = L // SSD_CHUNK
    dt = dt.astype(f32)
    xdt = (x.astype(f32) * dt[..., None]).reshape(b, nc, SSD_CHUNK, G, hg, P)
    a_cum = jnp.cumsum((dt * A.astype(f32)).reshape(b, nc, SSD_CHUNK, G, hg), axis=2)
    Bc = Bm.astype(f32).reshape(b, nc, SSD_CHUNK, G, N)
    Cc = Cm.astype(f32).reshape(b, nc, SSD_CHUNK, G, N)
    tri = jnp.tril(jnp.ones((SSD_CHUNK, SSD_CHUNK), bool))
    seg = a_cum[:, :, :, None] - a_cum[:, :, None, :]
    decay_ls = jnp.exp(jnp.where(tri[:, :, None, None], seg, -jnp.inf))
    cb = jnp.einsum('bclgn,bcsgn->bclsg', Cc, Bc)
    y_diag = jnp.einsum('bclsg,bclsgh,bcsghp->bclghp', cb, decay_ls, xdt)
    decay_end = jnp.exp(a_cum[:, :, -1:] - a_cum)
    chunk_states = jnp.einsum('bclgn,bclgh,bclghp->bcghpn', Bc, decay_end, xdt)
    chunk_decay = jnp.exp(a_cum[:, :, -1])

    def step(s, inp):
        st, dec = inp
        return dec[..., None, None] * s + st, s

    h_final, h_in = lax.scan(step, h0.astype(f32).reshape(b, G, hg, P, N),
                             (jnp.moveaxis(chunk_states, 1, 0), jnp.moveaxis(chunk_decay, 1, 0)))
    h_in = jnp.moveaxis(h_in, 0, 1)
    y_off = jnp.einsum('bclgn,bcghpn,bclgh->bclghp', Cc, h_in, jnp.exp(a_cum))
    return (y_diag + y_off).reshape(b, L, H, P), h_final.reshape(b, H, P, N)

def ssd_bidirectional(xbc_raw, dt_raw, conv_w, conv_b, dt_bias, a_log, d_skip, h0_f, h0_b):
    xbc = jax.nn.silu(dwconv(xbc_raw, conv_w, conv_b))
    b, L, _ = xbc.shape
    gn = SSD_GROUPS * SSD_STATE
    xs = xbc[..., :SSD_INNER].reshape(b, L, SSD_HEADS, SSD_HEAD_DIM)
    Bm = xbc[..., SSD_INNER:SSD_INNER + gn].reshape(b, L, SSD_GROUPS, SSD_STATE)
    Cm = xbc[..., SSD_INNER + gn:].reshape(b, L, SSD_GROUPS, SSD_STATE)
    dt = jax.nn.softplus(dt_raw.astype(jnp.float32).reshape(b, L, 2, SSD_HEADS) + dt_bias.astype(jnp.float32))
    A = -jnp.exp(a_log.astype(jnp.float32))
    y_f, h_f = ssd_chunked(xs, dt[:, :, 0], A[0], Bm, Cm, h0_f)
    flip = lambda t: jnp.flip(t, axis=1)
    y_b, h_b = ssd_chunked(flip(xs), flip(dt[:, :, 1]), A[1], flip(Bm), flip(Cm), h0_b)
    y = y_f + flip(y_b) + d_skip.astype(jnp.float32)[:, None] * xs.astype(jnp.float32)
    return y.reshape(b, L, SSD_INNER), h_f, h_b

def conformer_conv(glu_in, dw_w, dw_b, ln_g, ln_b, w_pw2):
    a, gt = jnp.split(glu_in, 2, axis=-1)
    u = dwconv(a * jax.nn.sigmoid(gt), dw_w, dw_b)
    u = jax.nn.silu(layernorm(u, ln_g, ln_b))
    return u @ w_pw2

def peer(h, w_q, keys, u, v):
    T, D = h.shape

    def block(hb):
        q = (hb @ w_q).reshape(PEER_BLOCK, PEER_HEADS, 2, PEER_DQ // 2)
        s = jnp.einsum('thid,ikd->thik', q, keys).astype(jnp.float32)
        s1, i1 = lax.top_k(s[:, :, 0], PEER_TOPK)
        s2, i2 = lax.top_k(s[:, :, 1], PEER_TOPK)
        cand = (s1[..., :, None] + s2[..., None, :]).reshape(PEER_BLOCK, PEER_HEADS, PEER_TOPK * PEER_TOPK)
        sc, ci = lax.top_k(cand, PEER_TOPK)
        e = (jnp.take_along_axis(i1, ci // PEER_TOPK, axis=-1) * N_KEYS
             + jnp.take_along_axis(i2, ci % PEER_TOPK, axis=-1))
        g = jax.nn.softmax(sc, axis=-1)
        act = jax.nn.gelu(jnp.einsum('thkd,td->thk', u[e], hb).astype(jnp.float32), approximate=False) * g
        return jnp.einsum('thk,thkd->td', act.astype(hb.dtype), v[e])

    out = lax.map(block, h.reshape(T // PEER_BLOCK, PEER_BLOCK, D))
    return out.reshape(T, D)

def trunk_layer(x, cvec, ctx, w_mod, b_mod, g_norm1, g_norm2, w_in, w_gate, b_gate, g_q_norm, w_uq,
                g_kv_norm, w_ukv, w_attn_out, ssd_conv_w, ssd_conv_b, ssd_dt_bias, ssd_a_log, ssd_d,
                g_ssd_norm, w_ssd_out, cv_dw_w, cv_dw_b, cv_ln_g, cv_ln_b, w_cv_pw2, w_out, w_peer_q,
                peer_keys, peer_u, peer_v):
    b, L, _ = x.shape
    sh1, sc1, gt1, sh2, sc2, gt2 = modulation(cvec, w_mod, b_mod)
    h = rmsnorm(x, g_norm1) * (1 + sc1) + sh1
    zin = h @ w_in
    q_nope, q_rope = mla_queries(zin[..., OFF_CQ:OFF_CKV], g_q_norm, w_uq)
    ckv = rmsnorm(zin[..., OFF_CKV:OFF_KR], g_kv_norm)
    k_rope = zin[..., OFF_KR:OFF_Z]
    k_nope, v = mla_kv(ckv, w_ukv)
    if ctx is None:
        h0 = jnp.zeros((b, SSD_HEADS, SSD_HEAD_DIM, SSD_STATE), jnp.float32)
        h0_f, h0_b = h0, h0
        kn_all, kr_all, v_all = k_nope, k_rope, v
    else:
        ckv_c, kr_c, h0_f, h0_b = ctx
        cos, sin = axial_rope_tables(L)
        q_rope = apply_axial_rope(q_rope, cos, sin)
        kn_c, v_c = mla_kv(ckv_c.astype(x.dtype), w_ukv)
        kn_all = jnp.concatenate([kn_c, k_nope], axis=1)
        kr_all = jnp.concatenate([kr_c.astype(x.dtype), apply_axial_rope(k_rope, cos, sin)], axis=1)
        v_all = jnp.concatenate([v_c, v], axis=1)
    o_attn = mla_attention(q_nope, q_rope, kn_all, kr_all, v_all) @ w_attn_out
    y_ssd, h_f, h_b = ssd_bidirectional(zin[..., OFF_XBC:OFF_DT], zin[..., OFF_DT:OFF_GLU], ssd_conv_w, ssd_conv_b,
                                        ssd_dt_bias, ssd_a_log, ssd_d, h0_f, h0_b)
    yz = y_ssd * jax.nn.silu(zin[..., OFF_Z:OFF_XBC].astype(jnp.float32))
    o_ssd = rmsnorm(yz, g_ssd_norm).astype(x.dtype) @ w_ssd_out
    o_conv = conformer_conv(zin[..., OFF_GLU:N_IN], cv_dw_w, cv_dw_b, cv_ln_g, cv_ln_b, w_cv_pw2)
    gates = jax.nn.sigmoid((h @ w_gate + b_gate).astype(jnp.float32)).astype(x.dtype)
    g_a, g_s, g_c = jnp.split(gates, N_BRANCH, axis=-1)
    x = x + gt1 * ((g_a * o_attn + g_s * o_ssd + g_c * o_conv) @ w_out)
    h2 = rmsnorm(x, g_norm2) * (1 + sc2) + sh2
    x = x + gt2 * peer(h2.reshape(b * L, D_MODEL), w_peer_q, peer_keys, peer_u, peer_v).reshape(b, L, D_MODEL)
    if ctx is None:
        return x, (ckv, k_rope, h_f.astype(x.dtype), h_b.astype(x.dtype))
    return x, None

def setup_inputs(seed: int = 0) -> dict:
    key = jax.random.key(seed)
    ks = iter(jax.random.split(key, 64))

    def nrm(shape, s):
        return jax.random.normal(next(ks), shape, jnp.float32) * s

    def gain(shape):
        return 1.0 + nrm(shape, 0.01)

    dt0 = jnp.exp(jax.random.uniform(next(ks), (DEPTH, 2, SSD_HEADS), jnp.float32,
                                     minval=math.log(1e-3), maxval=math.log(1e-1)))
    a0 = jax.random.uniform(next(ks), (DEPTH, 2, SSD_HEADS), jnp.float32, minval=1.0, maxval=16.0)
    return {
        "x_prompt": nrm((BATCH, SEQ, D_MODEL), 1.0),
        "x_sample": nrm((DEC_BATCH, DEC_SEQ, D_MODEL), 1.0),
        "c": nrm((DEC_BATCH, D_MODEL), 1.0),
        "cache_ckv": nrm((DEC_BATCH, DEPTH, PAST_LEN, KV_RANK), 1.0),
        "cache_krope": nrm((DEC_BATCH, DEPTH, PAST_LEN, ROPE_DIM), 1.0),
        "state_ssd_fwd": nrm((DEC_BATCH, DEPTH, SSD_HEADS, SSD_HEAD_DIM, SSD_STATE), 0.1),
        "state_ssd_bwd": nrm((DEC_BATCH, DEPTH, SSD_HEADS, SSD_HEAD_DIM, SSD_STATE), 0.1),
        "c_ctx": nrm((D_MODEL,), 1.0),
        "w_mod": nrm((DEPTH, D_MODEL, 6 * D_MODEL), 0.5 * D_MODEL ** -0.5),
        "b_mod": nrm((DEPTH, 6 * D_MODEL), 0.01),
        "g_norm1": gain((DEPTH, D_MODEL)),
        "g_norm2": gain((DEPTH, D_MODEL)),
        "w_in": nrm((DEPTH, D_MODEL, N_IN), D_MODEL ** -0.5),
        "w_gate": nrm((DEPTH, D_MODEL, N_BRANCH * D_MODEL), D_MODEL ** -0.5),
        "b_gate": nrm((DEPTH, N_BRANCH * D_MODEL), 0.01),
        "g_q_norm": gain((DEPTH, Q_RANK)),
        "w_uq": nrm((DEPTH, Q_RANK, MLA_HEADS * (NOPE_DIM + ROPE_DIM)), Q_RANK ** -0.5),
        "g_kv_norm": gain((DEPTH, KV_RANK)),
        "w_ukv": nrm((DEPTH, KV_RANK, MLA_HEADS * (NOPE_DIM + V_DIM)), KV_RANK ** -0.5),
        "w_attn_out": nrm((DEPTH, MLA_HEADS * V_DIM, D_MODEL), (MLA_HEADS * V_DIM) ** -0.5),
        "ssd_conv_w": nrm((DEPTH, SSD_CONV_W, SSD_XBC), SSD_CONV_W ** -0.5),
        "ssd_conv_b": nrm((DEPTH, SSD_XBC), 0.01),
        "ssd_dt_bias": dt0 + jnp.log(-jnp.expm1(-dt0)),
        "ssd_a_log": jnp.log(a0),
        "ssd_d": gain((DEPTH, SSD_HEADS)),
        "g_ssd_norm": gain((DEPTH, SSD_INNER)),
        "w_ssd_out": nrm((DEPTH, SSD_INNER, D_MODEL), SSD_INNER ** -0.5),
        "cv_dw_w": nrm((DEPTH, CONV_W, CONV_CH), CONV_W ** -0.5),
        "cv_dw_b": nrm((DEPTH, CONV_CH), 0.01),
        "cv_ln_g": gain((DEPTH, CONV_CH)),
        "cv_ln_b": nrm((DEPTH, CONV_CH), 0.01),
        "w_cv_pw2": nrm((DEPTH, CONV_CH, D_MODEL), CONV_CH ** -0.5),
        "w_out": nrm((DEPTH, D_MODEL, D_MODEL), D_MODEL ** -0.5),
        "w_peer_q": nrm((DEPTH, D_MODEL, PEER_HEADS * PEER_DQ), D_MODEL ** -0.5),
        "peer_keys": nrm((DEPTH, 2, N_KEYS, PEER_DQ // 2), (PEER_DQ // 2) ** -0.5),
        "peer_u": nrm((DEPTH, N_EXPERTS, D_MODEL), D_MODEL ** -0.5),
        "peer_v": nrm((DEPTH, N_EXPERTS, D_MODEL), PEER_HEADS ** -0.5),
        "g_final": gain((D_MODEL,)),
    }

def reference(x_prompt, x_sample, c, cache_ckv, cache_krope, state_ssd_fwd, state_ssd_bwd, c_ctx,
              w_mod, b_mod, g_norm1, g_norm2, w_in, w_gate, b_gate, g_q_norm, w_uq, g_kv_norm, w_ukv,
              w_attn_out, ssd_conv_w, ssd_conv_b, ssd_dt_bias, ssd_a_log, ssd_d, g_ssd_norm, w_ssd_out,
              cv_dw_w, cv_dw_b, cv_ln_g, cv_ln_b, w_cv_pw2, w_out, w_peer_q, peer_keys, peer_u, peer_v,
              g_final):
    y_p = x_prompt
    y_s = x_sample
    ckvs, krs, hfs, hbs = [], [], [], []
    for l in range(DEPTH):
        p = dict(w_mod=w_mod[l], b_mod=b_mod[l], g_norm1=g_norm1[l], g_norm2=g_norm2[l], w_in=w_in[l],
                 w_gate=w_gate[l], b_gate=b_gate[l], g_q_norm=g_q_norm[l], w_uq=w_uq[l],
                 g_kv_norm=g_kv_norm[l], w_ukv=w_ukv[l], w_attn_out=w_attn_out[l],
                 ssd_conv_w=ssd_conv_w[l], ssd_conv_b=ssd_conv_b[l], ssd_dt_bias=ssd_dt_bias[l],
                 ssd_a_log=ssd_a_log[l], ssd_d=ssd_d[l], g_ssd_norm=g_ssd_norm[l], w_ssd_out=w_ssd_out[l],
                 cv_dw_w=cv_dw_w[l], cv_dw_b=cv_dw_b[l], cv_ln_g=cv_ln_g[l], cv_ln_b=cv_ln_b[l],
                 w_cv_pw2=w_cv_pw2[l], w_out=w_out[l], w_peer_q=w_peer_q[l], peer_keys=peer_keys[l],
                 peer_u=peer_u[l], peer_v=peer_v[l])
        y_p, ctx_out = trunk_layer(y_p, c_ctx[None, :], None, **p)
        ckv, kr, hf, hb = ctx_out
        ckvs.append(ckv)
        krs.append(kr)
        hfs.append(hf)
        hbs.append(hb)
        y_s, _ = trunk_layer(y_s, c, (cache_ckv[:, l], cache_krope[:, l], state_ssd_fwd[:, l], state_ssd_bwd[:, l]), **p)
    y_prompt = rmsnorm(y_p, g_final)
    y_sample = rmsnorm(y_s, g_final)
    new_ckv = jnp.stack(ckvs, axis=1)
    new_krope = jnp.stack(krs, axis=1)
    new_ssd_fwd = jnp.stack(hfs, axis=1)
    new_ssd_bwd = jnp.stack(hbs, axis=1)
    return (y_prompt, y_sample, new_ckv, new_krope, new_ssd_fwd, new_ssd_bwd)


_drawn_inputs = setup_inputs


def setup_inputs(seed=0):
    import zlib

    import numpy as np

    out = dict(_drawn_inputs(seed))
    spreads = {}
    factors = {'cache_ckv': 4.052,
     'cache_krope': 6.593,
     'state_ssd_bwd': 22.952,
     'g_norm1': 3.385,
     'g_norm2': 6.291,
     'b_gate': 8.0,
     'g_q_norm': 8.0,
     'g_kv_norm': 5.752,
     'ssd_conv_b': 3.129,
     'ssd_d': 200.0,
     'g_ssd_norm': 8.0,
     'cv_dw_b': 8.0,
     'cv_ln_g': 8.0,
     'cv_ln_b': 8.0,
     'g_final': 157.651,
     'state_ssd_fwd': 55.556}
    for name, (base, spread) in spreads.items():
        noise = np.random.default_rng([zlib.crc32(name.encode()), seed]).standard_normal(out[name].shape)
        drawn = base * np.exp(spread * noise) if base else spread * noise
        out[name] = jnp.asarray(drawn.astype(out[name].dtype))
    for name, factor in factors.items():
        out[name] = (out[name] * factor).astype(out[name].dtype)
    return out
```

```python
import math
from contextlib import ExitStack

import numpy as np

import concourse.bass as bass
from concourse import mybir

ALU = mybir.AluOpType
ACT = mybir.ActivationFunctionType
AX = mybir.AxisListType
F32 = mybir.dt.float32
U32 = mybir.dt.uint32

P = 128
D = 1024
KD = D // P
DEPTH = 2
T = 3
TOK = T * P
EPS = 1e-6
HEADS, NOPE, ROPE, VD = 16, 64, 32, 64
QK = NOPE + ROPE
Q_RANK, KV_RANK = 384, 128
KQ = Q_RANK // P
SH, SP_, SN, SG = 16, 64, 128, 2
HG = SH // SG
XC = 12
CW, XW = 31, 5
PH, TOPK, NKEYS = 8, 16, 128
SLOTS = PH * TOPK
NEG = -3.0e38

XIN, XOUT = 2 + P + 2 + 2 * P + 2, P + 2 + 2 * P
UIN, UOUT = 15 + P + 15 + 2 * P + 15, P + 15 + 2 * P

RING = 3
CHUNK = KD * 512
W_MOD, W_CQKV, W_Z, W_XBC, W_GLU = 0, 12, 13, 15, 18
W_BR, W_OUT, W_PQ = 22, 34, 36
N_BIG = 40

V_GQ, V_CW, V_CB, V_UW, V_UB, V_LG, V_LB, V_GS, V_BG = 0, 3, 63, 75, 323, 331, 339, 347, 355
N_VEC = 379
R_GKV, R_DTB, R_ALOG, R_D = 0, 128, 160, 192
R_BASE = 208
N_ROW = 209
C_ID, C_TF, C_TB, C_ONE, C_RC, C_RS, C_IOTA, C_EPS = 0, 128, 256, 384, 512, 576, 640, 656
N_CONST = 658

BANKS = 8


class Groups:

    def __init__(self):
        self.names, self.by = [], []

    def add(self, name, by):
        self.names.append(name)
        self.by.append(by)

    def number(self, name):
        return self.names.index(name)

    def bank(self, name):
        return self.number(name) % BANKS

    def taken(self, name):
        n = self.number(name)
        return self.by[n], sum(b == self.by[n] for b in self.by[:n + 1])

    def reused(self, name):
        n = self.number(name) - BANKS
        return self.names[n] if n >= 0 else None


SSD_UNITS = [(0, 0), (0, 1), (1, 0), (2, 1), (2, 0), (1, 1)]


def attention_order():
    for i in range(HEADS + 3):
        if i < HEADS:
            yield "K", i
            yield "QT", i
        if 0 <= i - 1 < HEADS:
            yield "SA", i - 1
            yield "SB", i - 1
        if 0 <= i - 2 < HEADS:
            yield "PA", i - 2
            yield "PB", i - 2
        if 0 <= i - 3 < HEADS:
            yield "PV", i - 3


def ssd_order():
    units = [(t, d, g) for t, d in SSD_UNITS for g in range(SG)]
    for i in range(len(units) + 1):
        if i < len(units):
            yield "AB0", units[i]
            yield "AB1", units[i]
        if i >= 1:
            u = units[i - 1]
            yield "YD", u
            if u[0] > 0:
                yield "YO", u
            if state_of(u):
                yield "CS", u


def state_of(u):
    t, d, _ = u
    return t == 0 or (t, d) in ((1, 0), (2, 1))


def plan():
    G = Groups()
    chunks, last = [], {}

    def use(chunk, group):
        if chunk not in last:
            chunks.append(chunk)
        last[chunk] = group

    for n in range(12):
        G.add(("mod", n), "dve")
        use(("big", W_MOD + n), ("mod", n))
    for t in range(T):
        for c in range(2):
            G.add(("n1", t, c), "act")
    for t in range(T):
        G.add(("cqkv", t), "act")
        use(("big", W_CQKV), ("cqkv", t))
    for t in range(T):
        G.add(("krdt", t), "act")
        use(("small", 0), ("krdt", t))
    for h in range(2):
        for t in range(T):
            G.add(("z", h, t), "act")
            use(("big", W_Z + h), ("z", h, t))
    for m in range(XC):
        G.add(("xbc", m), "act")
        use(("big", W_XBC + m // 4), ("xbc", m))
    for m in range(KD):
        G.add(("gt", m), "act")
        use(("big", W_GLU + 2 * (m // 4)), ("gt", m))
        G.add(("a", m), "dve")
        use(("big", W_GLU + 2 * (m // 4) + 1), ("a", m))
    for t in range(T):
        G.add(("cqT", t), "act")
    G.add(("kvT", 0), "act")
    G.add(("krT", 0), "dve")
    for c in range(3):
        for t in range(T):
            G.add(("q", c, t), "act")
            use(("uq", c), ("q", c, t))
    for kt in range(4):
        for c in range(2):
            G.add(("v", kt, c), "dve")
            use(("ukv", 0), ("v", kt, c))
    for step, h in attention_order():
        G.add((step, h), {"K": "dve", "QT": "act", "SA": "act", "SB": "act", "PA": "dve", "PB": "act",
                          "PV": "dve"}[step])
        if step == "K":
            use(("ukv", 0), (step, h))
    G.add(("cum", 0), "dve")
    for t in range(T):
        for c in range(2):
            G.add(("xs", t, c), "act")
    G.add(("bt", 0), "act")
    G.add(("bt", 1), "act")
    G.add(("cb", 0), "dve")
    G.add(("cb", 1), "dve")
    for step, u in ssd_order():
        G.add((step, u), "dve")
    for k in range(KD):
        G.add(("oT", k), "act")
    G.add(("mu", 0), "act")
    for k in range(KD):
        G.add(("yT", k), "act")
    G.add(("var", 0), "act")
    for b in range(3):
        for h in range(2):
            for m in range(4):
                G.add(("gate", b, h, m), "act")
                use(("big", W_BR + 4 * b + 2 * h), ("gate", b, h, m))
                G.add(("br", b, h, m), "dve")
                use(("big", W_BR + 4 * b + 2 * h + 1), ("br", b, h, m))
    for h in range(2):
        for t in range(T):
            G.add(("out", h, t), "dve")
            use(("big", W_OUT + h), ("out", h, t))
    for t in range(T):
        for c in range(2):
            G.add(("n2", t, c), "act")
    for m in range(16):
        G.add(("pq", m), "act")
        use(("big", W_PQ + m // 4), ("pq", m))
    for t in range(T):
        for c in range(4):
            G.add(("ps", t, c), "act")
    return G, chunks, last


class Sems:

    def __init__(self, nc, names):
        self.all = {n: nc.alloc_semaphore(n) for n in names}

    def __getitem__(self, name):
        return self.all[name]

    def span(self):
        ids = [s.num for s in self.all.values()]
        assert max(ids) - min(ids) + 1 == len(ids)
        return range(min(ids), max(ids) + 1)


class Steps:

    def __init__(self, sem):
        self.sem, self.n = sem, 0

    def __call__(self, ins):
        ins.then_inc(self.sem, 1)
        self.n += 1
        return self.n


class Kernel:

    def __init__(self, nc, io):
        self.nc, self.io = nc, io
        self.G, self.chunks, self.last = plan()
        self.C = nc.alloc_sbuf_tensor("consts", [P, N_CONST], F32)
        self.x = nc.alloc_sbuf_tensor("x", [P, T, D], F32)
        self.hT = nc.alloc_sbuf_tensor("hT", [P, KD, TOK], F32)
        self.hn = nc.alloc_sbuf_tensor("hn", [P, T, D], F32)
        self.vec = nc.alloc_sbuf_tensor("vec", [P, N_VEC], F32)
        self.row = nc.alloc_sbuf_tensor("row", [P, N_ROW], F32)
        self.st = nc.alloc_sbuf_tensor("st", [P, 64], F32)
        self.pool_n = 30300
        self.ring0 = RING * CHUNK
        self.arena = nc.alloc_sbuf_tensor("arena", [P, self.ring0 + self.pool_n], F32)
        self.ps = [nc.alloc_psum_tensor(f"bank{b}", [P, 512], F32) for b in range(BANKS)]
        self.used = self.ring0
        self.ident = self.C[:, C_ID:C_ID + P]
        self.ones = self.C[:, C_ONE:C_ONE + P]
        self.tri = [self.C[:, C_TF:C_TF + P], self.C[:, C_TB:C_TB + P]]
        self.eps = self.C[:, C_EPS:C_EPS + 1]
        self.one = self.C[:, C_EPS + 1:C_EPS + 2]
        gather = [f"rows_landed{s}" for s in range(8)]
        self.gathered = [nc.alloc_semaphore(n) for n in gather]
        self.S = Sems(nc, NAMES + [f"weights_landed{i}" for i in range(RING)])

    def at(self, off, *shape):
        n = int(np.prod(shape))
        assert off + n <= self.pool_n, (off, shape)
        v = self.arena[:, self.ring0 + off:self.ring0 + off + n]
        if len(shape) == 2:
            v = v.rearrange("p (a b) -> p a b", a=shape[0])
        if len(shape) == 3:
            v = v.rearrange("p (a b c) -> p a b c", a=shape[0], b=shape[1])
        return v

    def slot(self, chunk):
        return self.chunks.index(chunk) % RING

    def weights(self, chunk, k, n):
        s = self.slot(chunk) * CHUNK
        return self.arena[:, s:s + k * n].rearrange("p (k n) -> p k n", k=k)

    def load_weights(self, sp, l, upto):
        io = self.io
        while self.loaded < min(upto, len(self.chunks)):
            n = self.loaded
            kind, i = self.chunks[n]
            if n >= RING:
                sp.wait_ge(self.S["psum_full"], self.G.number(self.last[self.chunks[n - RING]]) + 1)
            src, width = {
                "big": (io["w_big"], CHUNK), "small": (io["w_small"], KD * 64),
                "uq": (io["w_uq"], KQ * 512), "ukv": (io["w_ukv"], 2048)}[kind]
            s = self.slot(self.chunks[n]) * CHUNK
            src = src[bass.ds(l, 1), i].rearrange("a p n -> p (a n)")
            sp.dma_start(self.arena[:, s:s + width], src).then_inc(self.S[f"weights_landed{n % RING}"], 16)
            self.loaded += 1

    def wait_weights(self, pe, chunk):
        n = self.chunks.index(chunk)
        pe.wait_ge(self.S[f"weights_landed{n % RING}"], 16 * (n // RING + 1))

    def bank(self, name):
        return self.ps[self.G.bank(name)]

    def wait_bank(self, pe, name):
        assert self.G.names[self.pe_at] == name, (self.G.names[self.pe_at], name)
        self.pe_at += 1
        old = self.G.reused(name)
        if old is not None:
            self.wait_taken(pe, old)

    def wait_taken(self, eng, name):
        by, n = self.G.taken(name)
        eng.wait_ge(self.S[by + "_took"], n)

    def wait_full(self, eng, name):
        eng.wait_ge(self.S["psum_full"], self.G.number(name) + 1)

    def full(self, ins):
        ins.then_inc(self.S["psum_full"], 1)

    def took(self, ins, name):
        by, n = self.G.taken(name)
        self.takes[by] += 1
        assert self.takes[by] == n, (name, self.takes[by], n)
        ins.then_inc(self.S[by + "_took"], 1)


NAMES = ["psum_full", "act_took", "dve_took", "dve_step", "act_step", "pool_step", "loads", "loads2", "loads3",
         "stores", "mod_scaled", "mod_stored", "stats_sq", "stats_var", "stats_sqrt", "h_ready", "h_read",
         "conv_ready", "u_ready", "sig_ready", "x_conv_done", "x_silu", "u_conv_done", "cq_ready", "kv_ready",
         "kr_ready", "q_roped", "rope_rows", "max_ready", "exp_ready", "o_ready", "dt_abs", "dt_ln", "cum_ready",
         "exps_ready", "seg_ready", "exp_seg", "m_ready", "xdt_ready", "xw_ready", "y_added", "h_next",
         "y_ready", "yn_ready", "uc_ready", "sq_ready", "ln_std", "ln_ready", "uT_ready", "gate_ready",
         "merged", "x_added", "s_ready", "s_read", "soft_in", "soft_exp", "routed", "staged", "dot_done",
         "gelu_done", "weight_done", "slot_done", "zeroed", "pads", "gw_staged", "state_out", "ctx_loads",
         "silu_c", "mean_ready", "lat_var", "dta_ready"]


def modulate_and_norm(K, l):
    nc, S, io, G = K.nc, K.S, K.io, K.G
    rows = K.at(0, 6 * D)
    brow = K.at(6144, 8 * D)
    cT = K.at(14336, KD, 2)
    mrow = K.at(14400, 2, D)
    srow = K.at(16448, 2, D)
    sq = K.at(18496, D)
    steps = Steps(S["dve_step"])
    K.dve_steps = steps
    with nc.Block() as block:
        @block.sync
        def _(sp):
            sp.dma_start(brow[0:2, :], io["mod_rows"][bass.ds(l, 1), :].to_broadcast([2, 8 * D])).then_inc(S["loads"], 16)
            K.load_weights(sp, l, 12)
            sp.dma_start(K.vec[:, :], io["vecs"][bass.ds(l, 1)].rearrange("a p n -> p (a n)")).then_inc(S["loads2"], 16)
            sp.dma_start(K.row[:, :], io["rows"][bass.ds(l, 1), :].to_broadcast([P, N_ROW])).then_inc(S["loads2"], 16)
            sp.wait_ge(S["mod_scaled"], 4)
            K.wait_taken(sp, ("mod", 11))
            sp.dma_start(io["mod_scratch"], rows[0:2, :]).then_inc(S["mod_stored"], 16)
            K.load_weights(sp, l, 15)
            sp.wait_ge(S["mod_stored"], 16)
            for v, dst in ((1, mrow), (0, srow)):
                sp.dma_start(dst, spread(io, v)).then_inc(S["loads3"], 16)

        @block.scalar
        def _(act):
            act.dma_start(cT.rearrange("p a b -> p (a b)"), io["c_rows"]).then_inc(S["ctx_loads"], 16)
            act.wait_ge(S["ctx_loads"], 16)
            act_silu = nc.scalar.activation(cT, cT, ACT.Silu)
            act_silu.then_inc(S["silu_c"], 1)
            norm_act(K, act, sq, "n1", 0)

        @block.tensor
        def _(pe):
            pe.wait_ge(S["silu_c"], 1)
            for n in range(12):
                w = K.weights(("big", W_MOD + n), KD, 512)
                K.wait_weights(pe, ("big", W_MOD + n))
                K.wait_bank(pe, ("mod", n))
                for k in range(KD):
                    mm = nc.tensor.matmul(K.bank(("mod", n))[0:2, :], cT[:, k, :], w[:, k, :],
                                          start=k == 0, stop=k == KD - 1)
                K.full(mm)
            norm_pe(K, pe, "n1", 0)

        @block.vector
        def _(dve):
            norm_stats_dve(K, dve, 0)
            dve.wait_ge(S["loads"], 16)
            for n in range(12):
                v, half = n // 2, n % 2
                r = rows[0:2, n * 512:(n + 1) * 512]
                K.wait_full(dve, ("mod", n))
                K.took(nc.vector.tensor_tensor(r, K.bank(("mod", n))[0:2, :], brow[0:2, n * 512:(n + 1) * 512],
                                               ALU.add), ("mod", n))
                if v in (1, 4):
                    K.wait_taken(dve, ("mod", n))
                    g = 6 * D + (v // 3) * D + half * 512
                    nc.vector.scalar_tensor_tensor(out=r, in0=r, scalar=1.0, in1=brow[0:2, g:g + 512],
                                                   op0=ALU.add, op1=ALU.mult).then_inc(S["mod_scaled"], 1)
            dve.wait_ge(S["loads3"], 32)
            norm_apply_dve(K, dve, mrow, srow, 0)


def spread(io, v):
    t = io["mod_scratch"]
    return bass.AP(tensor=t.tensor, offset=v * D, ap=[[0, P], [6 * D, 2], [1, D]])


def norm_act(K, act, sq, name, which, before=0):
    nc, S = K.nc, K.S
    for t in range(T):
        if t:
            act.wait_ge(S["stats_sq"], 3 * before + t)
        nc.scalar.activation(sq, K.x[:, t, :], ACT.Square,
                             accum_out=K.st[:, 8 * which + t:8 * which + t + 1]).then_inc(S["stats_sq"], 1)
    act.wait_ge(S["stats_var"], before + 1)
    nc.scalar.activation(K.st[:, 8 * which + 3:8 * which + 6], K.st[:, 8 * which:8 * which + 3],
                         ACT.Sqrt).then_inc(S["stats_sqrt"], 1)
    if name is None:
        return
    for t in range(T):
        for c in range(2):
            K.wait_full(act, (name, t, c))
            K.took(nc.scalar.copy(K.hT[:, 4 * c:4 * c + 4, t * P:(t + 1) * P],
                                  K.bank((name, t, c))[:, :].rearrange("p (k n) -> p k n", k=4)), (name, t, c))


def norm_stats_dve(K, dve, which, before=0):
    nc, S = K.nc, K.S
    s = K.st[:, 8 * which:8 * which + 3]
    dve.wait_ge(S["stats_sq"], 3 * before + 3)
    nc.vector.tensor_scalar(s, s, 1.0 / D, EPS, ALU.mult, ALU.add).then_inc(S["stats_var"], 1)
    dve.wait_ge(S["stats_sqrt"], before + 1)
    r = K.st[:, 8 * which + 3:8 * which + 6]
    dve.wait_ge(S["dve_step"], K.dve_steps(nc.vector.reciprocal(r, r)))


def norm_apply_dve(K, dve, mrow, srow, which):
    nc, S = K.nc, K.S
    for t in range(T):
        c = min(t, 1)
        n = K.dve_steps(nc.vector.scalar_tensor_tensor(
            out=K.hn[:, t, :], in0=K.x[:, t, :], scalar=K.st[:, 8 * which + 3 + t:8 * which + 4 + t],
            in1=mrow[:, c, :], op0=ALU.mult, op1=ALU.mult))
        dve.wait_ge(S["dve_step"], n)
        nc.vector.tensor_tensor(K.hn[:, t, :], K.hn[:, t, :], srow[:, c, :], ALU.add).then_inc(S["h_ready"], 1)


def norm_pe(K, pe, name, which):
    nc, S = K.nc, K.S
    for t in range(T):
        pe.wait_ge(S["h_ready"], 3 * which + t + 1)
        for c in range(2):
            K.wait_bank(pe, (name, t, c))
            for k in range(4):
                f = (4 * c + k) * P
                mm = nc.tensor.transpose(K.bank((name, t, c))[:, k * P:(k + 1) * P], K.hn[:, t, f:f + P], K.ident)
            K.full(mm)


A_CQKV, A_KRDT, A_Z, A_XBC, A_UC = 0, 1536, 1728, 4800, 9432
A_FREE = A_UC + KD * UOUT


def tokens(t, pad):
    a = [0, P + pad, 2 * P + pad][t]
    return slice(a, a + P)


def project_in(K, l):
    nc, S, io, G = K.nc, K.S, K.io, K.G
    cqkv, krdt, z = K.at(A_CQKV, T, 512), K.at(A_KRDT, T, 64), K.at(A_Z, T, D)
    xbc, uc = K.at(A_XBC, XC, XOUT), K.at(A_UC, KD, UOUT)
    xin = K.at(A_FREE, 6, XIN)
    uin = K.at(A_FREE + 6 * XIN, KD, UIN)
    sig = K.at(A_FREE + 6 * XIN + KD * UIN, 2, TOK)
    steps = K.dve_steps
    with nc.Block() as block:
        @block.sync
        def _(sp):
            K.load_weights(sp, l, 23 + 3)

        @block.gpsimd
        def _(pool):
            for a, b in ((0, 2), (2 + P, 4 + P), (XIN - 2, XIN)):
                nc.gpsimd.memset(xin[:, :, a:b], 0.0)
            for a, b in ((0, 15), (15 + P, 30 + P), (UIN - 15, UIN)):
                last = nc.gpsimd.memset(uin[:, :, a:b], 0.0)
            last.then_inc(S["pads"], 1)

        @block.tensor
        def _(pe):
            def by_tokens(name, chunk, width, t):
                w = K.weights(chunk, KD, width)
                K.wait_bank(pe, name)
                for k in range(KD):
                    mm = nc.tensor.matmul(K.bank(name)[:, 0:width], K.hT[:, k, t * P:(t + 1) * P], w[:, k, :],
                                          start=k == 0, stop=k == KD - 1)
                K.full(mm)

            def by_features(name, chunk, m):
                w = K.weights(chunk, KD, 512)
                K.wait_weights(pe, chunk)
                K.wait_bank(pe, name)
                for k in range(KD):
                    mm = nc.tensor.matmul(K.bank(name)[:, 0:TOK], w[:, k, m * P:(m + 1) * P], K.hT[:, k, :],
                                          start=k == 0, stop=k == KD - 1)
                K.full(mm)

            K.wait_weights(pe, ("big", W_CQKV))
            for t in range(T):
                by_tokens(("cqkv", t), ("big", W_CQKV), 512, t)
            K.wait_weights(pe, ("small", 0))
            for t in range(T):
                by_tokens(("krdt", t), ("small", 0), 64, t)
            for h in range(2):
                K.wait_weights(pe, ("big", W_Z + h))
                for t in range(T):
                    by_tokens(("z", h, t), ("big", W_Z + h), 512, t)
            for m in range(XC):
                by_features(("xbc", m), ("big", W_XBC + m // 4), m % 4)
            for m in range(KD):
                by_features(("gt", m), ("big", W_GLU + 2 * (m // 4)), m % 4)
                by_features(("a", m), ("big", W_GLU + 2 * (m // 4) + 1), m % 4)

        @block.scalar
        def _(act):
            for t in range(T):
                K.wait_full(act, ("cqkv", t))
                K.took(nc.scalar.copy(cqkv[:, t, :], K.bank(("cqkv", t))[:, :]), ("cqkv", t))
            for t in range(T):
                K.wait_full(act, ("krdt", t))
                K.took(nc.scalar.copy(krdt[:, t, :], K.bank(("krdt", t))[:, 0:64]), ("krdt", t))
            for h in range(2):
                for t in range(T):
                    K.wait_full(act, ("z", h, t))
                    K.took(nc.scalar.activation(z[:, t, h * 512:(h + 1) * 512], K.bank(("z", h, t))[:, :],
                                                ACT.Silu), ("z", h, t))
            act.wait_ge(S["pads"], 1)

            def silu(m):
                act.wait_ge(S["x_conv_done"], m + 1)
                nc.scalar.activation(xbc[:, m, :], xbc[:, m, :], ACT.Silu,
                                     bias=K.vec[:, V_CB + m:V_CB + m + 1]).then_inc(S["x_silu"], 1)

            for m in range(XC):
                if m >= 6:
                    act.wait_ge(S["x_conv_done"], m - 5)
                K.wait_full(act, ("xbc", m))
                b = K.bank(("xbc", m))
                nc.scalar.copy(xin[:, m % 6, 2:2 + P], b[:, 0:P])
                K.took(nc.scalar.copy(xin[:, m % 6, 4 + P:4 + 3 * P], b[:, P:3 * P]), ("xbc", m))
                if m >= 3:
                    silu(m - 3)
            for m in range(XC - 3, XC):
                silu(m)
            for m in range(KD):
                if m >= 2:
                    K.wait_taken(act, ("a", m - 2))
                K.wait_full(act, ("gt", m))
                K.took(nc.scalar.activation(sig[:, m % 2, :], K.bank(("gt", m))[:, 0:TOK], ACT.Sigmoid), ("gt", m))

        @block.vector
        def _(dve):
            def taps(dst, src, wcol, width, length, m, done, ms):
                before = {}
                for k in range(width):
                    for j in ms:
                        o, i = dst[:, j, :], src[:, j % m, k:k + length]
                        w = K.vec[:, wcol + width * j + k:wcol + width * j + k + 1]
                        if k:
                            dve.wait_ge(S["dve_step"], before[j])
                            ins = nc.vector.scalar_tensor_tensor(out=o, in0=i, scalar=w, in1=o, op0=ALU.mult, op1=ALU.add)
                        else:
                            ins = nc.vector.tensor_scalar(o, i, w, None, ALU.mult)
                        if k < width - 1:
                            before[j] = steps(ins)
                        else:
                            ins.then_inc(S[done], 1)

            dve.wait_ge(S["pads"], 1)
            dve.wait_ge(S["loads2"], 32)
            for m in range(0, XC, 2):
                K.wait_taken(dve, ("xbc", m + 1))
                taps(xbc, xin, V_CW, XW, XOUT, 6, "x_conv_done", (m, m + 1))
            for m in range(0, KD, 2):
                for j in (m, m + 1):
                    K.wait_full(dve, ("a", j))
                    K.wait_taken(dve, ("gt", j))
                    b = K.bank(("a", j))
                    n = steps(nc.vector.tensor_tensor(uin[:, j, 15:15 + P], b[:, 0:P], sig[:, j % 2, 0:P], ALU.mult))
                    K.took(nc.vector.tensor_tensor(uin[:, j, 30 + P:30 + 3 * P], b[:, P:3 * P], sig[:, j % 2, P:3 * P],
                                                   ALU.mult), ("a", j))
                K.wait_taken(dve, ("a", m + 1))
                taps(uc, uin, V_UW, CW, UOUT, KD, "u_conv_done", (m, m + 1))


KCOL = [0, 2, 3]


def attention(K, l):
    nc, S, io, G = K.nc, K.S, K.io, K.G
    cqkv, krdt = K.at(A_CQKV, T, 512), K.at(A_KRDT, T, 64)
    o = K.hn
    off = A_FREE
    cqT = K.at(off, KQ, TOK)
    ckvT = K.at(off + 1152, 512)
    krT = K.at(off + 1664, 512)
    q = K.at(off + 2176, T, HEADS * QK)
    v = K.at(off + 6784, 4, HEADS * VD)
    kT = K.at(off + 10880, 4, 512)
    qT = K.at(off + 12928, 2, TOK)
    pr = K.at(off + 13696, 2, 896)
    pT = K.at(off + 15504, 2, 896)
    krp = K.at(off + 10880, T, QK)
    tmp = K.at(off + 10880 + T * QK, HEADS * ROPE)
    mx = K.at(off + 15488, 2, 4)
    sm = K.at(off + 15496, 2, 4)
    steps = K.dve_steps
    st = K.st
    SC = QK ** -0.5
    with nc.Block() as block:
        @block.sync
        def _(sp):
            sp.dma_start(ckvT[:, P:2 * P], io["cache_kvT"][bass.ds(l, 1)].rearrange("a p n -> p (a n)")).then_inc(S["ctx_loads"], 16)
            sp.dma_start(krT[NOPE:QK, P:2 * P], io["cache_krT"][bass.ds(l, 1)].rearrange("a p n -> p (a n)")).then_inc(S["ctx_loads"], 16)
            sp.dma_start(io["new_krope"][bass.ds(l, 1)].rearrange("a p n -> p (a n)"), krdt[:, 0, 0:ROPE]).then_inc(S["stores"], 16)
            sp.wait_ge(S["kv_ready"], 3)
            sp.dma_start(io["new_ckv"][bass.ds(l, 1)].rearrange("a p n -> p (a n)"), cqkv[:, 0, Q_RANK:512]).then_inc(S["stores"], 16)
            K.load_weights(sp, l, 30)
            sp.wait_ge(S["stores"], 32)

        @block.scalar
        def _(act):
            for t in range(T):
                nc.scalar.activation(q[:, t, 0:Q_RANK], cqkv[:, t, 0:Q_RANK], ACT.Square,
                                     accum_out=st[:, 16 + t:17 + t])
                nc.scalar.activation(q[:, t, Q_RANK:512], cqkv[:, t, Q_RANK:512], ACT.Square,
                                     accum_out=st[:, 19 + t:20 + t]).then_inc(S["sq_ready"], 1)
            act.wait_ge(S["lat_var"], 1)
            nc.scalar.activation(st[:, 16:22], st[:, 16:22], ACT.Sqrt).then_inc(S["ln_std"], 1)
            act.wait_ge(S["loads2"], 32)
            for t in range(T):
                K.wait_full(act, ("cqT", t))
                for k in range(KQ):
                    ins = nc.scalar.activation(cqT[:, k, t * P:(t + 1) * P], K.bank(("cqT", t))[:, k * P:(k + 1) * P],
                                               ACT.Copy, scale=K.vec[:, V_GQ + k:V_GQ + k + 1])
                K.took(ins, ("cqT", t))
            K.wait_full(act, ("kvT", 0))
            b = K.bank(("kvT", 0))
            nc.scalar.copy(ckvT[:, 0:P], b[:, 0:P])
            K.took(nc.scalar.copy(ckvT[:, 2 * P:4 * P], b[:, P:3 * P]), ("kvT", 0))
            for c in range(3):
                for t in range(T):
                    K.wait_full(act, ("q", c, t))
                    K.took(nc.scalar.copy(q[:, t, c * 512:(c + 1) * 512], K.bank(("q", c, t))[:, :]), ("q", c, t))
            for step, h in attention_order():
                if step == "QT":
                    if h >= 2:
                        K.wait_full(act, ("SB", h - 2))
                    K.wait_full(act, (step, h))
                    K.took(nc.scalar.copy(qT[0:QK, h % 2, :], K.bank((step, h))[0:QK, 0:TOK]), (step, h))
                if step == "SB":
                    act.wait_ge(S["max_ready"], h + 1)
                    if h >= 2:
                        K.wait_full(act, ("PB", h - 2))
                        K.wait_taken(act, ("PV", h - 2))
                    pieces = [("SA", 0, P, 0), ("SA", P, 512, 1), ("SB", 0, TOK, 2)]
                    for name, a, z, j in pieces:
                        d = 0 if name == "SA" else 512
                        ins = nc.scalar.activation(pr[:, h % 2, d + a:d + z], K.bank((name, h))[:, a:z], ACT.Exp,
                                                   bias=mx[:, h % 2, j:j + 1], scale=SC,
                                                   accum_out=sm[:, h % 2, j:j + 1])
                        if j:
                            K.took(ins, (name, h))
                if step == "PB":
                    if h >= 2:
                        K.wait_full(act, ("PV", h - 2))
                    K.wait_full(act, (step, h))
                    K.took(nc.scalar.copy(pT[:, h % 2, 512:896], K.bank((step, h))[:, 0:TOK]), (step, h))

        @block.tensor
        def _(pe):
            for t in range(T):
                pe.wait_ge(S["cq_ready"], t + 1)
                K.wait_bank(pe, ("cqT", t))
                for k in range(KQ):
                    mm = nc.tensor.transpose(K.bank(("cqT", t))[:, k * P:(k + 1) * P], cqkv[:, t, k * P:(k + 1) * P], K.ident)
                K.full(mm)
            pe.wait_ge(S["kv_ready"], 3)
            K.wait_bank(pe, ("kvT", 0))
            for t in range(T):
                mm = nc.tensor.transpose(K.bank(("kvT", 0))[:, t * P:(t + 1) * P], cqkv[:, t, Q_RANK:512], K.ident)
            K.full(mm)
            pe.wait_ge(S["kr_ready"], 1)
            K.wait_bank(pe, ("krT", 0))
            for t in range(T):
                mm = nc.tensor.transpose(K.bank(("krT", 0))[0:QK, t * P:(t + 1) * P], krp[:, t, :], K.ident)
            K.full(mm)
            K.wait_taken(pe, ("cqT", 2))
            for c in range(3):
                w = K.weights(("uq", c), KQ, 512)
                K.wait_weights(pe, ("uq", c))
                for t in range(T):
                    K.wait_bank(pe, ("q", c, t))
                    for k in range(KQ):
                        mm = nc.tensor.matmul(K.bank(("q", c, t))[:, :], cqT[:, k, t * P:(t + 1) * P], w[:, k, :],
                                              start=k == 0, stop=k == KQ - 1)
                    K.full(mm)
            wv = K.weights(("ukv", 0), HEADS, P)
            K.wait_weights(pe, ("ukv", 0))
            pe.wait_ge(S["ctx_loads"], 48)
            K.wait_taken(pe, ("kvT", 0))
            for kt in range(4):
                for c in range(2):
                    K.wait_bank(pe, ("v", kt, c))
                    K.full(nc.tensor.matmul(K.bank(("v", kt, c))[:, :], ckvT[:, kt * P:(kt + 1) * P],
                                            wv[:, 8 * c:8 * c + 8, NOPE:P], start=True, stop=True))
            for step, h in attention_order():
                b = K.bank((step, h))
                if step == "K":
                    K.wait_bank(pe, (step, h))
                    K.full(nc.tensor.matmul(b[0:NOPE, :], wv[:, h, 0:NOPE], ckvT[:, :], start=True, stop=True))
                if step == "QT":
                    if h == 0:
                        pe.wait_ge(S["q_roped"], 2)
                        K.wait_taken(pe, ("q", 2, 2))
                    K.wait_bank(pe, (step, h))
                    for t in range(T):
                        mm = nc.tensor.transpose(b[0:QK, t * P:(t + 1) * P], q[:, t, h * QK:(h + 1) * QK], K.ident)
                    K.full(mm)
                if step == "SA":
                    K.wait_taken(pe, ("K", h))
                    K.wait_taken(pe, ("QT", h))
                    if h == 0:
                        pe.wait_ge(S["rope_rows"], 1)
                    K.wait_bank(pe, (step, h))
                    nc.tensor.matmul(b[:, 0:P], qT[0:QK, h % 2, 0:P], kT[0:QK, h % 4, 0:P], start=True, stop=True)
                    K.full(nc.tensor.matmul(b[:, P:512], qT[0:QK, h % 2, P:2 * P], kT[0:QK, h % 4, P:512],
                                            start=True, stop=True))
                if step == "SB":
                    K.wait_bank(pe, (step, h))
                    K.full(nc.tensor.matmul(b[:, 0:TOK], qT[0:QK, h % 2, 2 * P:3 * P], kT[0:QK, h % 4, P:512],
                                            start=True, stop=True))
                if step in ("PA", "PB"):
                    K.wait_taken(pe, ("SB", h))
                    K.wait_bank(pe, (step, h))
                    d = 0 if step == "PA" else 512
                    for j in range(4 if step == "PA" else 3):
                        mm = nc.tensor.transpose(b[:, j * P:(j + 1) * P], pr[:, h % 2, d + j * P:d + (j + 1) * P], K.ident)
                    K.full(mm)
                if step == "PV":
                    K.wait_taken(pe, ("PA", h))
                    K.wait_taken(pe, ("PB", h))
                    K.wait_bank(pe, (step, h))
                    vh = v[:, :, h * VD:(h + 1) * VD]
                    nc.tensor.matmul(b[:, 0:VD], pT[:, h % 2, 0:P], vh[:, 0, :], start=True, stop=True)
                    for t in (1, 2):
                        for j in range(3):
                            a = ((1 if t == 1 else 4) + j) * P
                            mm = nc.tensor.matmul(b[:, t * VD:(t + 1) * VD], pT[:, h % 2, a:a + P], vh[:, 1 + j, :],
                                                  start=j == 0, stop=j == 2)
                    K.full(mm)

        @block.vector
        def _(dve):
            dve.wait_ge(S["sq_ready"], 3)
            n = steps(nc.vector.tensor_scalar(st[:, 16:19], st[:, 16:19], 1.0 / Q_RANK, EPS, ALU.mult, ALU.add))
            nc.vector.tensor_scalar(st[:, 19:22], st[:, 19:22], 1.0 / KV_RANK, EPS, ALU.mult, ALU.add).then_inc(S["lat_var"], 1)
            dve.wait_ge(S["ln_std"], 1)
            dve.wait_ge(S["dve_step"], steps(nc.vector.reciprocal(st[:, 16:22], st[:, 16:22])))
            dve.wait_ge(S["loads2"], 32)
            for t in range(T):
                nc.vector.tensor_scalar(cqkv[:, t, 0:Q_RANK], cqkv[:, t, 0:Q_RANK], st[:, 16 + t:17 + t], None,
                                        ALU.mult).then_inc(S["cq_ready"], 1)
                nc.vector.scalar_tensor_tensor(out=cqkv[:, t, Q_RANK:512], in0=cqkv[:, t, Q_RANK:512],
                                               scalar=st[:, 19 + t:20 + t], in1=K.row[:, R_GKV:R_GKV + P],
                                               op0=ALU.mult, op1=ALU.mult).then_inc(S["kv_ready"], 1)

            def rope(src, dst, scratch, heads, t, last=None):
                C = K.C[:, C_RC + 32 * (t - 1):C_RC + 32 * t].rearrange("p (a b n) -> p a b n", a=2, b=2)
                Z = K.C[:, C_RS + 32 * (t - 1):C_RS + 32 * t].rearrange("p (a b n) -> p a b n", a=2, b=2)
                for b in range(2):
                    for a in range(2):
                        s0 = src[:, :, 16 * a + 8 * (1 - b):16 * a + 8 * (1 - b) + 8]
                        o0 = scratch[:, :, 16 * a + 8 * b:16 * a + 8 * b + 8]
                        z0 = Z[:, a, b, :].unsqueeze(1).to_broadcast([P, heads, 8])
                        n = steps(nc.vector.tensor_tensor(o0, s0, z0, ALU.mult))
                cc = K.C[:, C_RC + 32 * (t - 1):C_RC + 32 * t].unsqueeze(1).to_broadcast([P, heads, ROPE])
                dve.wait_ge(S["dve_step"], n)
                n = steps(nc.vector.tensor_tensor(dst, src, cc, ALU.mult))
                dve.wait_ge(S["dve_step"], n)
                ins = nc.vector.tensor_tensor(dst, dst, scratch, ALU.add)
                if last:
                    ins.then_inc(S[last], 1)
                else:
                    steps(ins)

            steps(nc.vector.memset(krp[:, :, 0:NOPE], 0.0))
            steps(nc.vector.tensor_copy(krp[:, 0, NOPE:QK], krdt[:, 0, 0:ROPE]))
            for t in (1, 2):
                rope(krdt[:, t:t + 1, 0:ROPE], krp[:, t:t + 1, NOPE:QK],
                     tmp[:, 32 * t:32 * t + 32].unsqueeze(1), 1, t, "kr_ready" if t == 2 else None)
            K.wait_full(dve, ("krT", 0))
            b = K.bank(("krT", 0))
            steps(nc.vector.tensor_copy(krT[NOPE:QK, 0:P], b[NOPE:QK, 0:P]))
            K.took(nc.vector.tensor_copy(krT[NOPE:QK, 2 * P:4 * P], b[NOPE:QK, P:3 * P]), ("krT", 0))
            for t in (1, 2):
                K.wait_taken(dve, ("q", 2, t))
                if t == 2:
                    dve.wait_ge(S["q_roped"], 1)
                qr = q[:, t, :].rearrange("p (h n) -> p h n", h=HEADS)[:, :, NOPE:QK]
                rope(qr, qr, tmp.rearrange("p (h n) -> p h n", h=HEADS), HEADS, t, "q_roped")
            dve.wait_ge(S["q_roped"], 2)
            dve.wait_ge(S["ctx_loads"], 48)
            K.wait_taken(dve, ("krT", 0))
            nc.vector.tensor_copy(kT[NOPE:QK, :, :], krT[NOPE:QK, :].unsqueeze(1).to_broadcast([ROPE, 4, 512]))\
                .then_inc(S["rope_rows"], 1)
            for kt in range(4):
                for c in range(2):
                    K.wait_full(dve, ("v", kt, c))
                    K.took(nc.vector.tensor_copy(v[:, kt, c * 512:(c + 1) * 512], K.bank(("v", kt, c))[:, :]), ("v", kt, c))
            for step, h in attention_order():
                b = K.bank((step, h))
                if step == "K":
                    if h >= 4:
                        K.wait_full(dve, ("SB", h - 4))
                    K.wait_full(dve, (step, h))
                    K.took(nc.vector.tensor_copy(kT[0:NOPE, h % 4, :], b[0:NOPE, :]), (step, h))
                if step == "SB":
                    K.wait_full(dve, ("SB", h))
                    if h >= 2:
                        K.wait_taken(dve, ("SB", h - 2))
                    sa = K.bank(("SA", h))
                    steps(nc.vector.reduce_max(mx[:, h % 2, 0:1], sa[:, 0:P], AX.X))
                    steps(nc.vector.reduce_max(mx[:, h % 2, 1:2], sa[:, P:512], AX.X))
                    n = steps(nc.vector.reduce_max(mx[:, h % 2, 2:3], b[:, 0:TOK], AX.X))
                    dve.wait_ge(S["dve_step"], n)
                    nc.vector.tensor_scalar(mx[:, h % 2, 0:3], mx[:, h % 2, 0:3], -SC, None, ALU.mult)\
                        .then_inc(S["max_ready"], 1)
                if step == "PA":
                    if h >= 2:
                        K.wait_full(dve, ("PV", h - 2))
                    K.wait_full(dve, (step, h))
                    K.took(nc.vector.tensor_copy(pT[:, h % 2, 0:512], b[:, :]), (step, h))
                if step == "PV":
                    K.wait_taken(dve, ("SB", h))
                    n = steps(nc.vector.reciprocal(sm[:, h % 2, 0:3], sm[:, h % 2, 0:3]))
                    dve.wait_ge(S["dve_step"], n)
                    K.wait_full(dve, (step, h))
                    K.took(nc.vector.tensor_tensor(
                        o[:, :, h * VD:(h + 1) * VD], b[:, 0:T * VD].rearrange("p (t n) -> p t n", t=T),
                        sm[:, h % 2, 0:3].unsqueeze(2).to_broadcast([P, T, VD]), ALU.mult), (step, h))


def ssd(K, l):
    nc, S, io, G = K.nc, K.S, K.io, K.G
    krdt, z = K.at(A_KRDT, T, 64), K.at(A_Z, T, D)
    xbc = K.at(A_XBC, XC, XOUT)
    off = A_FREE
    xs = K.at(off, T, D)
    bt = K.at(off + 3072, T, 2 * SN)
    cbm = K.at(off + 3840, 2, 6 * P)
    y = K.at(off + 5376, T, D)
    H = K.at(off + 8448, 2, D)
    xdt = K.at(off + 10496, 2, 512)
    xw = K.at(off + 11520, 512)
    seg = K.at(off + 12032, 2, 512)
    M = K.at(off + 13056, 2, 512)
    tmp = K.at(off + 14080, 512)
    sm = off + 14592
    raw, dt, aA, ab, acum, tot = [K.at(sm + 96 * i, 96) for i in range(6)]
    ea, dend, etot = [K.at(sm + 96 * i, 96) for i in range(6, 9)]
    A = K.at(A_CQKV, 32)
    outs = K.at(A_CQKV + 64, 2, 512)
    steps = K.dve_steps
    units = [(t, d, g) for t, d in SSD_UNITS for g in range(SG)]

    def heads(a, u):
        t, d, g = u
        c = 32 * t + 16 * d + 8 * g
        return a[:, c:c + 8]

    def spread8(a, u):
        return heads(a, u).unsqueeze(2).to_broadcast([P, HG, SP_])

    def h8(v):
        return v.rearrange("p (h n) -> p h n", h=HG)

    with nc.Block() as block:
        @block.sync
        def _(sp):
            sp.dma_start(H, io["h0T"][bass.ds(l, 1)].rearrange("a p n -> p (a n)").rearrange("p (d n) -> p d n", d=2)).then_inc(S["ctx_loads"], 16)
            for u in units:
                if u[0] == 0:
                    K.wait_taken(sp, ("CS", u))
                    dst = io["new_state"][bass.ds(l, 1), u[1]].rearrange("a p n -> p (a n)")[:, u[2] * 512:(u[2] + 1) * 512]
                    sp.dma_start(dst, outs[:, u[2], :]).then_inc(S["stores"], 16)
            sp.wait_ge(S["stores"], 32 + 64)

        @block.scalar
        def _(act):
            act.wait_ge(S["dt_abs"], 1)
            nc.scalar.activation(ab, ab, ACT.Exp, scale=-1.0).then_inc(S["act_step"], 1)
            nc.scalar.activation(A, K.row[:, R_ALOG:R_ALOG + 32], ACT.Exp).then_inc(S["act_step"], 1)
            act.wait_ge(S["act_step"], 1)
            nc.scalar.activation(ab, ab, ACT.Ln, bias=K.one).then_inc(S["dt_ln"], 1)
            for t in range(T):
                for c in range(2):
                    K.wait_full(act, ("xs", t, c))
                    K.took(nc.scalar.copy(xs[:, t, c * 512:(c + 1) * 512], K.bank(("xs", t, c))[:, :]), ("xs", t, c))
            for g in range(SG):
                K.wait_full(act, ("bt", g))
                K.took(nc.scalar.copy(bt[:, :, g * SN:(g + 1) * SN],
                                      K.bank(("bt", g))[:, 0:TOK].rearrange("p (t n) -> p t n", t=T)), ("bt", g))
            act.wait_ge(S["cum_ready"], 1)
            nc.scalar.activation(ea, acum, ACT.Exp)
            nc.scalar.activation(dend, dend, ACT.Exp)
            nc.scalar.activation(etot, tot, ACT.Exp).then_inc(S["exps_ready"], 1)
            for i in range(2 * len(units)):
                K.wait_taken(act, (f"AB{i % 2}", units[i // 2]))
                if i >= 2:
                    act.wait_ge(S["m_ready"], i - 1)
                nc.scalar.activation(seg[:, i % 2, :], seg[:, i % 2, :], ACT.Exp).then_inc(S["exp_seg"], 1)

        @block.tensor
        def _(pe):
            pe.wait_ge(S["dta_ready"], 1)
            K.wait_bank(pe, ("cum", 0))
            b = K.bank(("cum", 0))
            for t in range(T):
                for d in range(2):
                    c = 32 * t + 16 * d
                    nc.tensor.matmul(b[:, c:c + 16], K.tri[d], aA[:, c:c + 16], start=True, stop=True)
            K.full(nc.tensor.matmul(b[:, 96:192], K.ones, aA, start=True, stop=True))
            for t in range(T):
                for c in range(2):
                    K.wait_bank(pe, ("xs", t, c))
                    for k in range(4):
                        mm = nc.tensor.transpose(K.bank(("xs", t, c))[:, k * P:(k + 1) * P],
                                                 xbc[:, 4 * c + k, tokens(t, 2)], K.ident)
                    K.full(mm)
            for g in range(SG):
                K.wait_bank(pe, ("bt", g))
                for t in range(T):
                    mm = nc.tensor.transpose(K.bank(("bt", g))[:, t * P:(t + 1) * P], xbc[:, 8 + g, tokens(t, 2)], K.ident)
                K.full(mm)
            for j in range(2):
                K.wait_bank(pe, ("cb", j))
                for i in range(4 * j, min(4 * j + 4, 6)):
                    t, g = i // 2, i % 2
                    mm = nc.tensor.matmul(K.bank(("cb", j))[:, (i % 4) * P:(i % 4 + 1) * P], xbc[:, 8 + g, tokens(t, 2)],
                                          xbc[:, 10 + g, tokens(t, 2)], start=True, stop=True)
                K.full(mm)
            n_xw = 0
            pe.wait_ge(S["ctx_loads"], 64)
            for step, u in ssd_order():
                t, d, g = u
                i = units.index(u)
                name = (step, u)
                b = K.bank(name)
                if step in ("AB0", "AB1"):
                    K.wait_bank(pe, name)
                    for j in range(4):
                        c = 32 * t + 16 * d + 8 * g + 4 * (step == "AB1") + j
                        mm = nc.tensor.matmul(b[:, j * P:(j + 1) * P], aA[:, c:c + 1].to_broadcast([P, P]), K.tri[d],
                                              start=True, stop=True)
                    K.full(mm)
                if step == "YD":
                    pe.wait_ge(S["xdt_ready"], i + 1)
                    K.wait_bank(pe, name)
                    for j in range(HG):
                        if j % 4 == 0:
                            pe.wait_ge(S["m_ready"], 2 * i + j // 4 + 1)
                        mm = nc.tensor.matmul(b[:, j * SP_:(j + 1) * SP_], M[:, j // 4, (j % 4) * P:(j % 4 + 1) * P],
                                              xdt[:, i % 2, j * SP_:(j + 1) * SP_], start=True, stop=True)
                    K.full(mm)
                if step == "YO":
                    if (t, d) in ((2, 0), (1, 1)):
                        K.wait_taken(pe, ("CS", (3 - t, d, g)))
                    K.wait_bank(pe, name)
                    K.full(nc.tensor.matmul(b[:, :], xbc[:, 10 + g, tokens(t, 2)], H[:, d, g * 512:(g + 1) * 512],
                                            start=True, stop=True))
                if step == "CS":
                    n_xw += 1
                    pe.wait_ge(S["xw_ready"], n_xw)
                    K.wait_bank(pe, name)
                    K.full(nc.tensor.matmul(b[:, :], bt[:, t, g * SN:(g + 1) * SN], xw, start=True, stop=True))

        @block.vector
        def _(dve):
            r3 = raw.rearrange("p (t n) -> p t n", t=T)
            n = steps(nc.vector.tensor_tensor(r3, krdt[:, :, 32:64],
                                              K.row[:, R_DTB:R_DTB + 32].unsqueeze(1).to_broadcast([P, T, 32]), ALU.add))
            dve.wait_ge(S["dve_step"], n)
            nc.vector.scalar_tensor_tensor(out=ab, in0=raw, scalar=-1.0, in1=raw, op0=ALU.mult, op1=ALU.max).then_inc(S["dt_abs"], 1)
            n = steps(nc.vector.tensor_scalar(dt, raw, 0.0, None, ALU.max))
            dve.wait_ge(S["dve_step"], n)
            dve.wait_ge(S["dt_ln"], 1)
            n = steps(nc.vector.tensor_tensor(dt, dt, ab, ALU.add))
            dve.wait_ge(S["dve_step"], n)
            dve.wait_ge(S["act_step"], 2)
            nc.vector.scalar_tensor_tensor(out=aA.rearrange("p (t n) -> p t n", t=T), in0=dt.rearrange("p (t n) -> p t n", t=T),
                                           scalar=-1.0, in1=A.unsqueeze(1).to_broadcast([P, T, 32]),
                                           op0=ALU.mult, op1=ALU.mult).then_inc(S["dta_ready"], 1)
            K.wait_full(dve, ("cum", 0))
            b = K.bank(("cum", 0))
            steps(nc.vector.tensor_copy(acum, b[:, 0:96]))
            K.took(nc.vector.tensor_copy(tot, b[:, 96:192]), ("cum", 0))
            K.wait_taken(dve, ("cum", 0))
            nc.vector.tensor_tensor(dend, tot, acum, ALU.subtract).then_inc(S["cum_ready"], 1)
            for t in range(T):
                K.wait_taken(dve, ("xs", t, 1))
                n = steps(nc.vector.tensor_tensor(
                    y[:, t, :].rearrange("p (h n) -> p h n", h=SH), xs[:, t, :].rearrange("p (h n) -> p h n", h=SH),
                    K.row[:, R_D:R_D + SH].unsqueeze(2).to_broadcast([P, SH, SP_]), ALU.mult))
            dve.wait_ge(S["dve_step"], n)
            for j in range(2):
                K.wait_full(dve, ("cb", j))
                cnt = 4 if j == 0 else 2
                src = K.bank(("cb", j))[:, 0:cnt * P].rearrange("p (a n) -> p a n", a=cnt)
                for d in range(2):
                    dst = cbm[:, d, 4 * j * P:(4 * j + cnt) * P].rearrange("p (a n) -> p a n", a=cnt)
                    ins = nc.vector.tensor_tensor(dst, src, K.tri[d].unsqueeze(1).to_broadcast([P, cnt, P]), ALU.mult)
                    if d:
                        K.took(ins, ("cb", j))
            K.wait_taken(dve, ("cb", 1))
            dve.wait_ge(S["exps_ready"], 1)
            n_h = n_out = 0
            y_last = {}
            for step, u in ssd_order():
                t, d, g = u
                i = units.index(u)
                name = (step, u)
                b = K.bank(name)
                yv = y[:, t, g * 512:(g + 1) * 512]
                if step == "AB0":
                    if i >= 2:
                        K.wait_full(dve, ("YD", units[i - 2]))
                    nc.vector.tensor_tensor(h8(xdt[:, i % 2, :]), h8(xs[:, t, g * 512:(g + 1) * 512]), spread8(dt, u),
                                            ALU.mult).then_inc(S["xdt_ready"], 1)
                if step in ("AB0", "AB1"):
                    k = 2 * i + (step == "AB1")
                    K.wait_full(dve, name)
                    if k >= 2:
                        dve.wait_ge(S["m_ready"], k - 1)
                    for j in range(4):
                        c = 32 * t + 16 * d + 8 * g + 4 * (step == "AB1") + j
                        ins = nc.vector.tensor_scalar(seg[:, k % 2, j * P:(j + 1) * P], b[:, j * P:(j + 1) * P],
                                                      acum[:, c:c + 1], 0.0, ALU.subtract, ALU.min)
                        if j < 3:
                            steps(ins)
                    K.took(ins, name)
                if step == "AB1":
                    for k in (2 * i, 2 * i + 1):
                        dve.wait_ge(S["exp_seg"], k + 1)
                        if i >= 1:
                            K.wait_full(dve, ("YD", units[i - 1]))
                        cb = cbm[:, d, (2 * t + g) * P:(2 * t + g + 1) * P].unsqueeze(1).to_broadcast([P, 4, P])
                        nc.vector.tensor_tensor(M[:, k % 2, :].rearrange("p (a n) -> p a n", a=4),
                                                seg[:, k % 2, :].rearrange("p (a n) -> p a n", a=4), cb,
                                                ALU.mult).then_inc(S["m_ready"], 1)
                    if state_of(u):
                        prev = [w for w in units[:i] if state_of(w)]
                        if prev:
                            K.wait_full(dve, ("CS", prev[-1]))
                        dve.wait_ge(S["xdt_ready"], i + 1)
                        nc.vector.tensor_tensor(h8(xw), h8(xdt[:, i % 2, :]), spread8(dend, u), ALU.mult).then_inc(S["xw_ready"], 1)
                if step == "YD":
                    if (t, g) in y_last:
                        dve.wait_ge(S["dve_step"], y_last[(t, g)])
                    K.wait_full(dve, name)
                    K.took(nc.vector.tensor_tensor(yv, yv, b[:, :], ALU.add), name)
                    K.wait_taken(dve, name)
                if step == "YO":
                    K.wait_full(dve, name)
                    K.took(nc.vector.tensor_tensor(h8(tmp), h8(b[:, :]), spread8(ea, u), ALU.mult), name)
                    K.wait_taken(dve, name)
                    y_last[(t, g)] = steps(nc.vector.tensor_tensor(yv, yv, tmp, ALU.add))
                if step == "CS":
                    K.wait_full(dve, name)
                    if t == 0:
                        if n_out >= 2:
                            dve.wait_ge(S["stores"], 32 + 32)
                        K.took(nc.vector.tensor_copy(outs[:, g, :], b[:, :]), name)
                        n_out += 1
                    else:
                        if ("YO", u) in G.names:
                            K.wait_full(dve, ("YO", u))
                        dve.wait_ge(S["ctx_loads"], 64)
                        Hs = H[:, d, g * 512:(g + 1) * 512]
                        n = steps(nc.vector.tensor_tensor(h8(Hs), h8(Hs), spread8(etot, u), ALU.mult))
                        dve.wait_ge(S["dve_step"], n)
                        K.took(nc.vector.tensor_tensor(Hs, Hs, b[:, :], ALU.add), name)


def branches(K, l):
    nc, S, io, G = K.nc, K.S, K.io, K.G
    z, uc = K.at(A_Z, T, D), K.at(A_UC, KD, UOUT)
    off = A_FREE
    y = K.at(off + 5376, T, D)
    oT = K.at(off, KD, TOK)
    yT = K.at(A_XBC, KD, TOK)
    uT = K.at(off + 8448, KD, TOK)
    merged = K.at(off + 11520, KD, TOK)
    mean = K.at(A_CQKV, UOUT)
    std = K.at(A_CQKV + 400, UOUT)
    gs = K.at(A_CQKV + 800, 2, TOK)
    tmp = K.at(off + 3072, 2, 512)
    sqt = K.at(off + 4096, D)
    gt = K.at(A_Z, 2, D)
    squ = K.at(off + 11520, KD, UOUT)
    steps = K.dve_steps
    st = K.st
    srcs = [oT, yT, uT]
    with nc.Block() as block:
        @block.sync
        def _(sp):
            sp.wait_ge(S["y_ready"], 3)
            sp.dma_start(gt, spread(io, 2)).then_inc(S["loads3"], 16)
            K.load_weights(sp, l, len(K.chunks) - 1)

        @block.scalar
        def _(act):
            for k in range(KD):
                K.wait_full(act, ("oT", k))
                K.took(nc.scalar.copy(oT[:, k, :], K.bank(("oT", k))[:, 0:TOK]), ("oT", k))
            K.wait_full(act, ("mu", 0))
            K.took(nc.scalar.mul(mean, K.bank(("mu", 0))[:, 0:UOUT], 1.0 / D), ("mu", 0))
            for t in range(T):
                act.wait_ge(S["y_ready"], t + 1)
                act.wait_ge(S["stats_sq"], 3 + t)
                nc.scalar.activation(sqt, y[:, t, :], ACT.Square, accum_out=st[:, 24 + t:25 + t]).then_inc(S["stats_sq"], 1)
            act.wait_ge(S["uc_ready"], 1)
            for m in range(KD):
                nc.scalar.activation(squ[:, m, :], uc[:, m, :], ACT.Square).then_inc(S["u_conv_done"], 1)
            act.wait_ge(S["stats_var"], 2)
            nc.scalar.activation(st[:, 27:30], st[:, 24:27], ACT.Sqrt).then_inc(S["stats_sqrt"], 1)
            for k in range(KD):
                K.wait_full(act, ("yT", k))
                K.took(nc.scalar.activation(yT[:, k, :], K.bank(("yT", k))[:, 0:TOK], ACT.Copy,
                                            scale=K.vec[:, V_GS + k:V_GS + k + 1]), ("yT", k))
            K.wait_full(act, ("var", 0))
            K.took(nc.scalar.activation(std, K.bank(("var", 0))[:, 0:UOUT], ACT.Sqrt, scale=1.0 / D, bias=K.eps), ("var", 0))
            act.wait_ge(S["ln_ready"], 1)
            for m in range(KD):
                for a, z0, b0 in ((0, P, 0), (P + 15, UOUT, P)):
                    ins = nc.scalar.activation(uT[:, m, b0:b0 + z0 - a], uc[:, m, a:z0], ACT.Silu,
                                               scale=K.vec[:, V_LG + m:V_LG + m + 1], bias=K.vec[:, V_LB + m:V_LB + m + 1])
            ins.then_inc(S["uT_ready"], 1)
            i = 0
            for br in range(3):
                for h in range(2):
                    for m in range(4):
                        name = ("gate", br, h, m)
                        if i >= 2:
                            K.wait_taken(act, prev2)
                        K.wait_full(act, name)
                        c = V_BG + 8 * br + 4 * h + m
                        K.took(nc.scalar.activation(gs[:, i % 2, :], K.bank(name)[:, 0:TOK], ACT.Sigmoid,
                                                    bias=K.vec[:, c:c + 1]), name)
                        prev2, prev1 = (prev1 if i else None), ("br", br, h, m)
                        i += 1

        @block.tensor
        def _(pe):
            for k in range(KD):
                K.wait_bank(pe, ("oT", k))
                for t in range(T):
                    mm = nc.tensor.transpose(K.bank(("oT", k))[:, t * P:(t + 1) * P], K.hn[:, t, k * P:(k + 1) * P], K.ident)
                K.full(mm)
            pe.wait_ge(S["mean_ready"], 1)
            K.wait_bank(pe, ("mu", 0))
            for m in range(KD):
                mm = nc.tensor.matmul(K.bank(("mu", 0))[:, 0:UOUT], K.ones, uc[:, m, :], start=m == 0, stop=m == KD - 1)
            K.full(mm)
            for k in range(KD):
                if k == 0:
                    pe.wait_ge(S["yn_ready"], 3)
                K.wait_bank(pe, ("yT", k))
                for t in range(T):
                    mm = nc.tensor.transpose(K.bank(("yT", k))[:, t * P:(t + 1) * P], y[:, t, k * P:(k + 1) * P], K.ident)
                K.full(mm)
            K.wait_bank(pe, ("var", 0))
            for m in range(KD):
                pe.wait_ge(S["u_conv_done"], KD + m + 1)
                mm = nc.tensor.matmul(K.bank(("var", 0))[:, 0:UOUT], K.ones, squ[:, m, :], start=m == 0, stop=m == KD - 1)
            K.full(mm)
            for br in range(3):
                for h in range(2):
                    for m in range(4):
                        for what, name, src in (("g", ("gate", br, h, m), K.hT), ("o", ("br", br, h, m), srcs[br])):
                            chunk = ("big", W_BR + 4 * br + 2 * h + (what == "o"))
                            w = K.weights(chunk, KD, 512)
                            K.wait_weights(pe, chunk)
                            if what == "o" and h == 0 and m == 0:
                                if br == 0:
                                    K.wait_taken(pe, ("oT", KD - 1))
                                if br == 1:
                                    K.wait_taken(pe, ("yT", KD - 1))
                                if br == 2:
                                    pe.wait_ge(S["uT_ready"], 1)
                            K.wait_bank(pe, name)
                            for k in range(KD):
                                mm = nc.tensor.matmul(K.bank(name)[:, 0:TOK], w[:, k, m * P:(m + 1) * P], src[:, k, :],
                                                      start=k == 0, stop=k == KD - 1)
                            K.full(mm)
            for h in range(2):
                w = K.weights(("big", W_OUT + h), KD, 512)
                K.wait_weights(pe, ("big", W_OUT + h))
                for t in range(T):
                    pe.wait_ge(S["merged"], 16)
                    K.wait_bank(pe, ("out", h, t))
                    for k in range(KD):
                        mm = nc.tensor.matmul(K.bank(("out", h, t))[:, :], merged[:, k, t * P:(t + 1) * P], w[:, k, :],
                                              start=k == 0, stop=k == KD - 1)
                    K.full(mm)

        @block.vector
        def _(dve):
            for m in range(KD):
                ins = nc.vector.tensor_scalar(uc[:, m, :], uc[:, m, :], K.vec[:, V_UB + m:V_UB + m + 1], None, ALU.add)
            ins.then_inc(S["mean_ready"], 1)
            for t in range(T):
                nc.vector.tensor_tensor(y[:, t, :], y[:, t, :], z[:, t, :], ALU.mult).then_inc(S["y_ready"], 1)
            K.wait_taken(dve, ("mu", 0))
            dve.wait_ge(S["mean_ready"], 1)
            ub = mean.unsqueeze(1).to_broadcast([P, KD, UOUT])
            nc.vector.tensor_tensor(uc, uc, ub, ALU.subtract).then_inc(S["uc_ready"], 1)
            dve.wait_ge(S["stats_sq"], 6)
            nc.vector.tensor_scalar(st[:, 24:27], st[:, 24:27], 1.0 / D, EPS, ALU.mult, ALU.add).then_inc(S["stats_var"], 1)
            dve.wait_ge(S["stats_sqrt"], 2)
            dve.wait_ge(S["dve_step"], steps(nc.vector.reciprocal(st[:, 27:30], st[:, 27:30])))
            dve.wait_ge(S["y_ready"], 3)
            for t in range(T):
                nc.vector.tensor_scalar(y[:, t, :], y[:, t, :], st[:, 27 + t:28 + t], None, ALU.mult).then_inc(S["yn_ready"], 1)
            K.wait_taken(dve, ("var", 0))
            dve.wait_ge(S["uc_ready"], 1)
            dve.wait_ge(S["dve_step"], steps(nc.vector.reciprocal(std, std)))
            nc.vector.tensor_tensor(uc, uc, std.unsqueeze(1).to_broadcast([P, KD, UOUT]), ALU.mult).then_inc(S["ln_ready"], 1)
            for br in range(3):
                for h in range(2):
                    for m in range(4):
                        mo = merged[:, 4 * h + m, :]
                        name = ("br", br, h, m)
                        K.wait_full(dve, name)
                        K.wait_taken(dve, ("gate", br, h, m))
                        i = (8 * br + 4 * h + m) % 2
                        b = K.bank(name)[:, 0:TOK]
                        if br == 0:
                            K.took(nc.vector.tensor_tensor(mo, b, gs[:, i, :], ALU.mult), name)
                        else:
                            n = 8 * (br - 1) + 4 * h + m
                            if n >= 2:
                                dve.wait_ge(S["merged"], n - 1)
                            K.took(nc.vector.tensor_tensor(tmp[:, i, 0:TOK], b, gs[:, i, :], ALU.mult), name)
                            K.wait_taken(dve, name)
                            if br == 2:
                                dve.wait_ge(S["merged"], 4 * h + m + 1)
                            nc.vector.tensor_tensor(mo, mo, tmp[:, i, 0:TOK], ALU.add).then_inc(S["merged"], 1)
            dve.wait_ge(S["loads3"], 48)
            for h in range(2):
                for t in range(T):
                    i = T * h + t
                    if i >= 2:
                        dve.wait_ge(S["x_added"], i - 1)
                    else:
                        dve.wait_ge(S["merged"], 16)
                    K.wait_full(dve, ("out", h, t))
                    K.took(nc.vector.tensor_tensor(tmp[:, i % 2, :], K.bank(("out", h, t))[:, :], gt[:, min(t, 1), h * 512:(h + 1) * 512],
                                                   ALU.mult), ("out", h, t))
                    K.wait_taken(dve, ("out", h, t))
                    xv = K.x[:, t, h * 512:(h + 1) * 512]
                    nc.vector.tensor_tensor(xv, xv, tmp[:, i % 2, :], ALU.add).then_inc(S["x_added"], 1)


B_GW, B_EI, B_G2 = 0, 384, 768
B_FREE = 768 + 2048


def route(K, l):
    nc, S, io, G = K.nc, K.S, K.io, K.G
    gw, ei = K.at(B_GW, T * SLOTS), K.at(B_EI, T * SLOTS).bitcast(U32)
    g2 = K.at(B_G2, 2, D)
    o = B_FREE
    mrow, srow, sq = K.at(o, 2, D), K.at(o + 2048, 2, D), K.at(o + 4096, D)
    qT = K.at(o + 5120, 16, TOK)
    keys = K.at(o + 11264, 2, P)
    s = K.at(o + 11520, 2, 16 * NKEYS)
    w = o
    s2 = K.at(w, 16, NKEYS)
    cand = K.at(w + 2048, PH, 256)
    o2 = o + 15616
    v1 = K.at(o2, 16, TOPK)
    x1 = K.at(o2 + 256, 16, TOPK).bitcast(U32)
    f1 = K.at(o2 + 512, 16, TOPK)
    v2 = K.at(o2 + 768, PH, TOPK)
    x2 = K.at(o2 + 896, PH, TOPK).bitcast(U32)
    hi = K.at(o2 + 1024, SLOTS).bitcast(U32)
    lo = K.at(o2 + 1152, SLOTS).bitcast(U32)
    hf = K.at(o2 + 1280, SLOTS)
    lf = K.at(o2 + 1408, SLOTS)
    e1 = K.at(o2 + 1536, SLOTS)
    e2 = K.at(o2 + 1664, SLOTS)
    ex = K.at(o2 + 1792, PH, TOPK)
    sm = K.at(o2 + 1920, PH)
    hot = K.at(o2 + 1936, SLOTS, TOPK)
    c2 = K.at(o2 + 3984, PH, 256)
    steps = K.dve_steps
    with nc.Block() as block:
        @block.sync
        def _(sp):
            for v, dst in ((4, mrow), (3, srow), (5, g2)):
                sp.dma_start(dst, spread(io, v)).then_inc(S["loads3"], 16)
            sp.dma_start(keys, io["keysT"][bass.ds(l, 1)].rearrange("a p n -> p (a n)").rearrange("p (d n) -> p d n", d=2)).then_inc(S["loads3"], 16)
            K.load_weights(sp, l, len(K.chunks))

        def soft(act, t):
            act.wait_ge(S["soft_in"], t + 1)
            nc.scalar.activation(ex, ex, ACT.Exp).then_inc(S["soft_exp"], 1)

        @block.scalar
        def _(act):
            norm_act(K, act, sq, "n2", 4, 2)
            for m in range(16):
                K.wait_full(act, ("pq", m))
                K.took(nc.scalar.copy(qT[:, m, :], K.bank(("pq", m))[:, 0:TOK]), ("pq", m))
            for t in range(T):
                if t == 2:
                    act.wait_ge(S["s_read"], 1)
                for c in range(4):
                    K.wait_full(act, ("ps", t, c))
                    K.took(nc.scalar.copy(s[:, t % 2, c * 512:(c + 1) * 512], K.bank(("ps", t, c))[:, :]), ("ps", t, c))
                if t >= 1:
                    soft(act, t - 1)
            soft(act, T - 1)

        @block.tensor
        def _(pe):
            norm_pe(K, pe, "n2", 1)
            for t in range(T):
                K.wait_taken(pe, ("n2", t, 1))
            for m in range(16):
                chunk = ("big", W_PQ + m // 4)
                wt = K.weights(chunk, KD, 512)
                K.wait_weights(pe, chunk)
                K.wait_bank(pe, ("pq", m))
                for k in range(KD):
                    mm = nc.tensor.matmul(K.bank(("pq", m))[:, 0:TOK], wt[:, k, (m % 4) * P:(m % 4 + 1) * P], K.hT[:, k, :],
                                          start=k == 0, stop=k == KD - 1)
                K.full(mm)
            pe.wait_ge(S["loads3"], 112)
            K.wait_taken(pe, ("pq", 15))
            for t in range(T):
                for c in range(4):
                    K.wait_bank(pe, ("ps", t, c))
                    for j in range(4):
                        m = 4 * c + j
                        mm = nc.tensor.matmul(K.bank(("ps", t, c))[:, j * P:(j + 1) * P], qT[:, m, t * P:(t + 1) * P],
                                              keys[:, m % 2, :], start=True, stop=True)
                    K.full(mm)

        @block.vector
        def _(dve):
            norm_stats_dve(K, dve, 4, 2)
            dve.wait_ge(S["loads3"], 112)
            norm_apply_dve(K, dve, mrow, srow, 4)

            def top16(src, scratch, vals, idx, n):
                for j in range(n):
                    k = steps(nc.vector.max(out=vals[:, j, 0:8], in_=src[:, j, :]))
                dve.wait_ge(S["dve_step"], k)
                for j in range(n):
                    steps(nc.vector.max_index(idx[:, j, 0:8], vals[:, j, 0:8], src[:, j, :]))
                    k = steps(nc.vector.match_replace(out=scratch[:, j, :], in_to_replace=vals[:, j, 0:8],
                                                      in_values=src[:, j, :], imm_value=NEG))
                dve.wait_ge(S["dve_step"], k)
                for j in range(n):
                    k = steps(nc.vector.max(out=vals[:, j, 8:16], in_=scratch[:, j, :]))
                dve.wait_ge(S["dve_step"], k)
                for j in range(n):
                    k = steps(nc.vector.max_index(idx[:, j, 8:16], vals[:, j, 8:16], scratch[:, j, :]))
                dve.wait_ge(S["dve_step"], k)

            def chosen(places, ids, out):
                iota = K.C[:, C_IOTA:C_IOTA + TOPK].unsqueeze(1).to_broadcast([P, SLOTS, TOPK])
                k = steps(nc.vector.tensor_tensor(hot, places.unsqueeze(2).to_broadcast([P, SLOTS, TOPK]), iota, ALU.is_equal))
                dve.wait_ge(S["dve_step"], k)
                for h in range(PH):
                    hv = hot[:, h * TOPK:(h + 1) * TOPK, :]
                    k = steps(nc.vector.tensor_tensor(hv, hv, ids[:, 2 * h, :].unsqueeze(1).to_broadcast([P, TOPK, TOPK]), ALU.mult))
                dve.wait_ge(S["dve_step"], k)
                return steps(nc.vector.tensor_reduce(out, hot, AX.X, ALU.add))

            for t in range(T):
                K.wait_taken(dve, ("ps", t, 3))
                sv = s[:, t % 2, :].rearrange("p (m n) -> p m n", m=16)
                top16(sv, s2, v1, x1, 16)
                for h in range(PH):
                    k = steps(nc.vector.tensor_tensor(
                        cand[:, h, :].rearrange("p (a b) -> p a b", a=TOPK),
                        v1[:, 2 * h, :].unsqueeze(2).to_broadcast([P, TOPK, TOPK]),
                        v1[:, 2 * h + 1, :].unsqueeze(1).to_broadcast([P, TOPK, TOPK]), ALU.add))
                nc.vector.tensor_copy(f1, x1).then_inc(S["s_read"], 1)
                dve.wait_ge(S["dve_step"], k)
                top16(cand, c2, v2, x2, PH)
                nc.vector.tensor_tensor(ex, v2, v2[:, :, 0:1].to_broadcast([P, PH, TOPK]), ALU.subtract).then_inc(S["soft_in"], 1)
                xf = x2.rearrange("p a b -> p (a b)")
                steps(nc.vector.tensor_scalar(hi, xf, 4, None, ALU.logical_shift_right))
                k = steps(nc.vector.tensor_scalar(lo, xf, 15, None, ALU.bitwise_and))
                dve.wait_ge(S["dve_step"], k)
                steps(nc.vector.tensor_copy(hf, hi))
                k = steps(nc.vector.tensor_copy(lf, lo))
                dve.wait_ge(S["dve_step"], k)
                dve.wait_ge(S["s_read"], t + 1)
                k = chosen(hf, f1, e1)
                dve.wait_ge(S["dve_step"], k)
                k = chosen(lf, f1[:, 1:16, :], e2)
                dve.wait_ge(S["dve_step"], k)
                k = steps(nc.vector.scalar_tensor_tensor(out=e1, in0=e1, scalar=float(NKEYS), in1=e2, op0=ALU.mult, op1=ALU.add))
                dve.wait_ge(S["dve_step"], k)
                k = steps(nc.vector.tensor_scalar(e1, e1, K.row[:, R_BASE:R_BASE + 1], None, ALU.add))
                dve.wait_ge(S["dve_step"], k)
                steps(nc.vector.tensor_copy(ei[:, t * SLOTS:(t + 1) * SLOTS], e1))
                dve.wait_ge(S["soft_exp"], t + 1)
                k = steps(nc.vector.tensor_reduce(sm, ex, AX.X, ALU.add))
                dve.wait_ge(S["dve_step"], k)
                k = steps(nc.vector.reciprocal(sm, sm))
                dve.wait_ge(S["dve_step"], k)
                k = steps(nc.vector.tensor_tensor(gw[:, t * SLOTS:(t + 1) * SLOTS].rearrange("p (a b) -> p a b", a=PH), ex,
                                                  sm.unsqueeze(2).to_broadcast([P, PH, TOPK]), ALU.mult))
                dve.wait_ge(S["dve_step"], k)


U = 8
TRIPS = SLOTS // (2 * U)


def experts(K, l):
    nc, S, io = K.nc, K.S, K.io
    gw, ei = K.at(B_GW, T * SLOTS), K.at(B_EI, T * SLOTS).bitcast(U32)
    g2 = K.at(B_G2, 2, D)
    o = B_FREE
    rows = K.at(o, U, 2 * D)
    acc = K.at(o + U * 2 * D, D)
    junk = K.at(o + U * 2 * D + D, D)
    o2 = o + U * 2 * D + 2 * D
    stage = K.at(o2, 2, U).bitcast(U32)
    dots, gel, wgt, gws = [K.at(o2 + 16 + 16 * i, 2, U) for i in range(4)]
    tick = K.at(o2 + 80, 1 + 2 * U)
    steps = K.dve_steps
    with nc.Block() as block:
        @block.gpsimd
        def _(pool):
            def pass_wait(n):
                nc.gpsimd.tensor_tensor(tick[:, 1 + n:2 + n], tick[:, 0:1], tick[:, 0:1], ALU.add)

            nc.gpsimd.memset(tick[:, 0:1], 0.0).then_inc(S["pool_step"], 1)
            pool.wait_ge(S["pool_step"], 1)
            for t in range(T):
                with pool.Fori(0, TRIPS) as i:
                    for r in range(2):
                        nc.gpsimd.tensor_copy(stage[:, r, :], ei[:, bass.ds(i * (2 * U) + (t * SLOTS + r * U), U)])\
                            .then_inc(S["staged"], 1)
                        for s in range(U):
                            if s == 0:
                                pool.wait_ge(S["staged"], i * 2 + (2 * t * TRIPS + r + 1))
                            pool.wait_ge(S["slot_done"], i * (2 * U) + (t * SLOTS + r * U + s + 1))
                            pass_wait(r * U + s)
                            nc.gpsimd.indirect_dma_start(rows[:, s, :], None, io["experts"],
                                                         bass.IndirectOffsetOnAxis(ap=stage[:, r, s:s + 1], axis=0))\
                                .then_inc(K.gathered[s], 16)

        @block.scalar
        def _(act):
            for t in range(T):
                with act.Fori(0, TRIPS) as i:
                    nc.scalar.copy(gws.rearrange("p a b -> p (a b)"), gw[:, bass.ds(i * (2 * U) + t * SLOTS, 2 * U)])\
                        .then_inc(S["gw_staged"], 1)
                    act.wait_ge(S["gw_staged"], i + (t * TRIPS + 1))
                    for n in range(2 * U):
                        r, s = n // U, n % U
                        act.wait_ge(S["dot_done"], i * (2 * U) + (t * SLOTS + n + 1))
                        nc.scalar.activation(gel[:, r, s:s + 1], dots[:, r, s:s + 1], ACT.Gelu).then_inc(S["gelu_done"], 1)
                        act.wait_ge(S["gelu_done"], i * (2 * U) + (t * SLOTS + n + 1))
                        nc.scalar.activation(wgt[:, r, s:s + 1], gel[:, r, s:s + 1], ACT.Copy,
                                             scale=gws[:, r, s:s + 1]).then_inc(S["weight_done"], 1)
                    act.wait_ge(S["weight_done"], i * (2 * U) + (t * SLOTS + 2 * U))

        @block.vector
        def _(dve):
            nc.vector.memset(acc, 0.0).then_inc(S["slot_done"], U)
            nc.vector.memset(K.st[:, 61:62], 0.0).then_inc(S["zeroed"], 1)

            def dot(t, i, n):
                r, s = n // U, n % U
                dve.wait_ge(K.gathered[s], (l * (2 * T * TRIPS) + i * 2) * 16 + 16 * (2 * t * TRIPS + r + 1))
                if n:
                    dve.wait_ge(S["dot_done"], i * (2 * U) + (t * SLOTS + n))
                nc.vector.tensor_tensor_reduce(out=junk, in0=rows[:, s, 0:D], in1=K.hn[:, t, :], scale=1.0, scalar=0.0,
                                               op0=ALU.mult, op1=ALU.add, accum_out=dots[:, r, s:s + 1]).then_inc(S["dot_done"], 1)

            def add(t, i, n):
                r, s = n // U, n % U
                dve.wait_ge(S["weight_done"], i * (2 * U) + (t * SLOTS + n + 1))
                dve.wait_ge(S["slot_done"], i * (2 * U) + (t * SLOTS + n + U))
                nc.vector.scalar_tensor_tensor(out=acc, in0=rows[:, s, D:2 * D], scalar=wgt[:, r, s:s + 1], in1=acc,
                                               op0=ALU.mult, op1=ALU.add).then_inc(S["slot_done"], 1)

            for t in range(T):
                with dve.Fori(0, TRIPS) as i:
                    for n in range(2 * U):
                        dot(t, i, n)
                        if n >= 2:
                            add(t, i, n - 2)
                    dve.wait_ge(S["dot_done"], i * (2 * U) + (t * SLOTS + 2 * U))
                    add(t, i, 2 * U - 2)
                    add(t, i, 2 * U - 1)
                dve.wait_ge(S["slot_done"], (t + 1) * SLOTS + U)
                k = steps(nc.vector.tensor_tensor(junk, acc, g2[:, min(t, 1), :], ALU.mult))
                dve.wait_ge(S["dve_step"], k)
                k = steps(nc.vector.tensor_tensor(K.x[:, t, :], K.x[:, t, :], junk, ALU.add))
                if t < T - 1:
                    dve.wait_ge(S["dve_step"], steps(nc.vector.memset(acc, 0.0)))


def trunk_kernel(nc, io):
    K = Kernel(nc, io)
    S = K.S
    with nc.Block() as block:
        @block.sync
        def _(sp):
            sp.dma_start(K.x[:, :, :], io["x"].rearrange("(t p) n -> p t n", p=P)).then_inc(S["loads"], 16)
            sp.dma_start(K.C[:, :], io["consts"]).then_inc(S["loads"], 16)
            sp.wait_ge(S["loads"], 32)
    nc.all_engine_barrier(sems_to_clear=S.span())
    with nc.Fori(0, DEPTH) as l:
        K.loaded, K.pe_at, K.takes = 0, 0, {"act": 0, "dve": 0}
        modulate_and_norm(K, l)
        project_in(K, l)
        attention(K, l)
        ssd(K, l)
        branches(K, l)
        route(K, l)
        experts(K, l)
        assert K.loaded == len(K.chunks) and K.pe_at == len(K.G.names)
        nc.all_engine_barrier(sems_to_clear=S.span())
    final_norm(K)


def final_norm(K):
    nc, S, io = K.nc, K.S, K.io
    gf = K.at(0, D)
    sq = K.at(D, D)
    y = K.at(2 * D, T, D)
    K.dve_steps = Steps(S["dve_step"])
    with nc.Block() as block:
        @block.sync
        def _(sp):
            sp.dma_start(gf, io["g_final"].to_broadcast([P, D])).then_inc(S["loads"], 16)
            for t in range(T):
                sp.wait_ge(S["h_ready"], t + 1)
                sp.dma_start(io["y"][t * P:(t + 1) * P, :], y[:, t, :]).then_inc(S["stores"], 16)
            sp.wait_ge(S["stores"], 16 * T)

        @block.scalar
        def _(act):
            norm_act(K, act, sq, None, 0)

        @block.vector
        def _(dve):
            norm_stats_dve(K, dve, 0)
            dve.wait_ge(S["loads"], 16)
            for t in range(T):
                nc.vector.scalar_tensor_tensor(out=y[:, t, :], in0=K.x[:, t, :], scalar=K.st[:, 3 + t:4 + t], in1=gf,
                                               op0=ALU.mult, op1=ALU.mult).then_inc(S["h_ready"], 1)


def kernel(**a):
    import concourse.bacc as _bacc
    from concourse.bass_utils import run_bass_kernel_spmd as _run

    a = {k: np.ascontiguousarray(v) for k, v in a.items()}
    L = DEPTH

    def big(w, cols):
        w = w[:, :, cols]
        n = w.shape[2] // 512
        return w.reshape(L, KD, P, n, 512).transpose(0, 3, 2, 1, 4).reshape(L, n, P, CHUNK)

    OCQ, OKR, OZ, OX, ODT, OG = 0, 512, 544, 1568, 3104, 3136
    w_in = a["w_in"]
    glu = big(w_in, slice(OG, OG + 2 * D))
    parts = [big(a["w_mod"], slice(None)), big(w_in, slice(0, 512)), big(w_in, slice(OZ, OZ + D)),
             big(w_in, slice(OX, OX + XC * P)), glu[:, 2:3], glu[:, 0:1], glu[:, 3:4], glu[:, 1:2]]
    gate = big(a["w_gate"], slice(None))
    for b, name in enumerate(("w_attn_out", "w_ssd_out", "w_cv_pw2")):
        w = big(a[name], slice(None))
        for h in range(2):
            parts += [gate[:, 2 * b + h:2 * b + h + 1], w[:, h:h + 1]]
    parts += [big(a["w_out"], slice(None)), big(a["w_peer_q"], slice(None))]
    w_big = np.concatenate(parts, axis=1)
    small = np.concatenate([w_in[:, :, OKR:OZ], w_in[:, :, ODT:OG]], axis=2)
    w_small = small.reshape(L, 1, KD, P, 64).transpose(0, 1, 3, 2, 4).reshape(L, 1, P, KD * 64)
    w_uq = a["w_uq"].reshape(L, KQ, P, 3, 512).transpose(0, 3, 2, 1, 4).reshape(L, 3, P, KQ * 512)
    w_ukv = a["w_ukv"].reshape(L, 1, P, 2048)

    def cols(v):
        return v.reshape(L, -1, P).transpose(0, 2, 1)

    def taps(w, n):
        return w.reshape(L, w.shape[1], n, P).transpose(0, 3, 2, 1).reshape(L, P, -1)

    vecs = np.concatenate([cols(a["g_q_norm"]), taps(a["ssd_conv_w"], XC), cols(a["ssd_conv_b"]), taps(a["cv_dw_w"], KD),
                           cols(a["cv_dw_b"]), cols(a["cv_ln_g"]), cols(a["cv_ln_b"]), cols(a["g_ssd_norm"]),
                           cols(a["b_gate"])], axis=2)
    base = (np.arange(L) * NKEYS * NKEYS).astype(np.float32)[:, None]
    rows = np.concatenate([a["g_kv_norm"], a["ssd_dt_bias"].reshape(L, 32), a["ssd_a_log"].reshape(L, 32), a["ssd_d"], base], axis=1)

    consts = np.zeros((P, N_CONST), np.float32)
    i = np.arange(P)
    consts[:, C_ID:C_ID + P] = np.eye(P)
    consts[:, C_TF:C_TF + P] = i[:, None] <= i[None, :]
    consts[:, C_TB:C_TB + P] = i[:, None] >= i[None, :]
    consts[:, C_ONE:C_ONE + P] = 1.0
    inv = (np.float32(10000.0) ** (-np.arange(8, dtype=np.float32) / np.float32(8))).astype(np.float32)
    for t in range(2):
        tok = t * P + i
        for ax, pos in enumerate((tok // 64, tok % 64)):
            ang = pos.astype(np.float32)[:, None] * inv
            for half in range(2):
                c = 32 * t + 16 * ax + 8 * half
                consts[:, C_RC + c:C_RC + c + 8] = np.cos(ang)
                consts[:, C_RS + c:C_RS + c + 8] = np.sin(ang) if half else -np.sin(ang)
    consts[:, C_IOTA:C_IOTA + TOPK] = np.arange(TOPK)
    consts[:, C_EPS] = EPS
    consts[:, C_EPS + 1] = 1.0

    h0 = np.stack([a["state_ssd_fwd"][0], a["state_ssd_bwd"][0]], axis=1)
    arrays = {
        "x": np.concatenate([a["x_prompt"][0], a["x_sample"][0]], axis=0),
        "c_rows": np.stack([a["c_ctx"].reshape(KD, P), a["c"][0].reshape(KD, P)], axis=2).transpose(1, 0, 2).reshape(P, KD * 2),
        "w_big": w_big, "w_small": w_small, "w_uq": w_uq, "w_ukv": w_ukv,
        "mod_rows": np.concatenate([a["b_mod"], a["g_norm1"], a["g_norm2"]], axis=1),
        "vecs": vecs, "rows": rows, "consts": consts,
        "cache_kvT": a["cache_ckv"][0].transpose(0, 2, 1), "cache_krT": a["cache_krope"][0].transpose(0, 2, 1),
        "h0T": h0.transpose(0, 4, 1, 2, 3).reshape(L, P, 2 * D),
        "keysT": a["peer_keys"].transpose(0, 3, 1, 2).reshape(L, P, 2 * P),
        "experts": np.concatenate([a["peer_u"], a["peer_v"]], axis=2).reshape(L * NKEYS * NKEYS, 2 * D),
        "g_final": a["g_final"].reshape(1, D),
    }
    outs = {"y": (TOK, D), "new_ckv": (L, P, KV_RANK), "new_krope": (L, P, ROPE), "new_state": (L, 2, P, D)}
    nc = _bacc.Bacc("TRN2", target_bir_lowering=False, num_devices=1)
    io = {}
    for name in arrays:
        arrays[name] = np.ascontiguousarray(arrays[name])
        io[name] = nc.dram_tensor(f"in_{name}_dram", arrays[name].shape, F32, kind="ExternalInput").ap()
    for name, shape in outs.items():
        io[name] = nc.dram_tensor(f"out_{name}_dram", shape, F32, kind="ExternalOutput").ap()
    io["mod_scratch"] = nc.dram_tensor("mod_scratch", (2, 6 * D), F32, kind="Internal").ap()
    trunk_kernel(nc, io)
    r = _run(nc, [{f"in_{k}_dram": v for k, v in arrays.items()}], core_ids=[0]).results[0]
    y = r["out_y_dram"]
    s = r["out_new_state_dram"].reshape(L, 2, P, SH, SP_).transpose(1, 0, 3, 4, 2)[:, None]
    s = np.ascontiguousarray(s)
    return (y[None, :P], y[None, P:], r["out_new_ckv_dram"][None], r["out_new_krope_dram"][None], s[0], s[1])
```

```python
import math
from contextlib import ExitStack

import numpy as np

import concourse.bass as bass
from concourse import mybir

ALU = mybir.AluOpType
ACT = mybir.ActivationFunctionType
AX = mybir.AxisListType
F32 = mybir.dt.float32
U32 = mybir.dt.uint32

P = 128
D = 1024
KD = D // P
DEPTH = 2
T = 3
TOK = T * P
EPS = 1e-6
HEADS, NOPE, ROPE, VD = 16, 64, 32, 64
QK = NOPE + ROPE
Q_RANK, KV_RANK = 384, 128
KQ = Q_RANK // P
SH, SP_, SN, SG = 16, 64, 128, 2
HG = SH // SG
XC = 12
CW, XW = 31, 5
PH, TOPK, NKEYS = 8, 16, 128
SLOTS = PH * TOPK
NEG = -3.0e38

XIN, XOUT = 2 + P + 2 + 2 * P + 2, P + 2 + 2 * P
UIN, UOUT = 15 + P + 15 + 2 * P + 15, P + 15 + 2 * P

RING = 3
CHUNK = KD * 512
W_MOD, W_CQKV, W_Z, W_XBC, W_GLU = 0, 12, 13, 15, 18
W_BR, W_OUT, W_PQ = 22, 34, 36
N_BIG = 40

V_GQ, V_CW, V_CB, V_UW, V_UB, V_LG, V_LB, V_GS, V_BG = 0, 3, 63, 75, 323, 331, 339, 347, 355
N_VEC = 379
R_GKV, R_DTB, R_ALOG, R_D = 0, 128, 160, 192
R_BASE = 208
N_ROW = 209
C_ID, C_TF, C_TB, C_ONE, C_RC, C_RS, C_IOTA, C_EPS = 0, 128, 256, 384, 512, 576, 640, 656
N_CONST = 658

BANKS = 8


class Groups:

    def __init__(self):
        self.names, self.by = [], []

    def add(self, name, by):
        self.names.append(name)
        self.by.append(by)

    def number(self, name):
        return self.names.index(name)

    def bank(self, name):
        return self.number(name) % BANKS

    def taken(self, name):
        n = self.number(name)
        return self.by[n], sum(b == self.by[n] for b in self.by[:n + 1])

    def reused(self, name):
        n = self.number(name) - BANKS
        return self.names[n] if n >= 0 else None


SSD_UNITS = [(0, 0), (0, 1), (1, 0), (2, 1), (2, 0), (1, 1)]


def attention_order():
    for i in range(HEADS + 3):
        if i < HEADS:
            yield "K", i
            yield "QT", i
        if 0 <= i - 1 < HEADS:
            yield "SA", i - 1
            yield "SB", i - 1
        if 0 <= i - 2 < HEADS:
            yield "PA", i - 2
            yield "PB", i - 2
        if 0 <= i - 3 < HEADS:
            yield "PV", i - 3


def ssd_order():
    units = [(t, d, g) for t, d in SSD_UNITS for g in range(SG)]
    for i in range(len(units) + 1):
        if i < len(units):
            yield "AB0", units[i]
            yield "AB1", units[i]
        if i >= 1:
            u = units[i - 1]
            yield "YD", u
            if u[0] > 0:
                yield "YO", u
            if state_of(u):
                yield "CS", u


def state_of(u):
    t, d, _ = u
    return t == 0 or (t, d) in ((1, 0), (2, 1))


BRANCH_ORDER = [(b, h, m) for b in range(3) for h in range(2) for m in range(4)]
LN_AFTER = {(1, 1, 0): "mu", (1, 1, 2): "var"}


def plan():
    G = Groups()
    chunks, last = [], {}

    def use(chunk, group):
        if chunk not in last:
            chunks.append(chunk)
        last[chunk] = group

    for n in range(12):
        G.add(("mod", n), "dve")
        use(("big", W_MOD + n), ("mod", n))
    for t in range(T):
        for c in range(2):
            G.add(("n1", t, c), "act")
    for t in range(T):
        G.add(("cqkv", t), "act")
        use(("big", W_CQKV), ("cqkv", t))
    for t in range(T):
        G.add(("krdt", t), "act")
        use(("small", 0), ("krdt", t))
    for h in range(2):
        for t in range(T):
            G.add(("z", h, t), "act")
            use(("big", W_Z + h), ("z", h, t))
    for m in range(XC):
        G.add(("xbc", m), "act")
        use(("big", W_XBC + m // 4), ("xbc", m))
    for m in range(KD):
        G.add(("gt", m), "act")
        use(("big", W_GLU + 2 * (m // 4)), ("gt", m))
        G.add(("a", m), "dve")
        use(("big", W_GLU + 2 * (m // 4) + 1), ("a", m))
    for t in range(T):
        G.add(("cqT", t), "act")
    G.add(("kvT", 0), "act")
    G.add(("krT", 0), "dve")
    for c in range(3):
        for t in range(T):
            G.add(("q", c, t), "act")
            use(("uq", c), ("q", c, t))
    for kt in range(4):
        for c in range(2):
            G.add(("v", kt, c), "dve")
            use(("ukv", 0), ("v", kt, c))
    for step, h in attention_order():
        G.add((step, h), {"K": "dve", "QT": "act", "SA": "act", "SB": "act", "PA": "dve", "PB": "act",
                          "PV": "dve"}[step])
        if step == "K":
            use(("ukv", 0), (step, h))
    G.add(("cum", 0), "dve")
    for t in range(T):
        for c in range(2):
            G.add(("xs", t, c), "act")
    G.add(("bt", 0), "act")
    G.add(("bt", 1), "act")
    G.add(("cb", 0), "dve")
    G.add(("cb", 1), "dve")
    for step, u in ssd_order():
        G.add((step, u), "dve")
    for k in range(KD):
        G.add(("oT", k), "act")
    for k in range(KD):
        G.add(("yT", k), "act")
    for b, h, m in BRANCH_ORDER:
        G.add(("gate", b, h, m), "act")
        use(("big", W_BR + 4 * b + 2 * h), ("gate", b, h, m))
        G.add(("br", b, h, m), "dve")
        use(("big", W_BR + 4 * b + 2 * h + 1), ("br", b, h, m))
        if (b, h, m) in LN_AFTER:
            G.add((LN_AFTER[b, h, m], 0), "act")
    for h in range(2):
        for t in range(T):
            G.add(("out", h, t), "dve")
            use(("big", W_OUT + h), ("out", h, t))
    for t in range(T):
        for c in range(2):
            G.add(("n2", t, c), "act")
    for c in range(4):
        G.add(("pq0", c), "act")
        use(("big", W_PQ + c), ("pq0", c))
    for c in range(4):
        G.add(("ps", 0, c), "act")
    for m in range(16):
        G.add(("pq", m), "act")
        use(("big", W_PQ + m // 4), ("pq", m))
    for t in (1, 2):
        for c in range(4):
            G.add(("ps", t, c), "act")
    return G, chunks, last


class Sems:

    def __init__(self, nc, names):
        self.all = {n: nc.alloc_semaphore(n) for n in names}

    def __getitem__(self, name):
        return self.all[name]

    def span(self):
        ids = [s.num for s in self.all.values()]
        assert max(ids) - min(ids) + 1 == len(ids)
        return range(min(ids), max(ids) + 1)


class Steps:

    def __init__(self, sem):
        self.sem, self.n = sem, 0

    def __call__(self, ins):
        ins.then_inc(self.sem, 1)
        self.n += 1
        return self.n


class Kernel:

    def __init__(self, nc, io):
        self.nc, self.io = nc, io
        self.G, self.chunks, self.last = plan()
        self.C = nc.alloc_sbuf_tensor("consts", [P, N_CONST], F32)
        self.x = nc.alloc_sbuf_tensor("x", [P, T, D], F32)
        self.hT = nc.alloc_sbuf_tensor("hT", [P, KD, TOK], F32)
        self.hn = nc.alloc_sbuf_tensor("hn", [P, T, D], F32)
        self.vec = nc.alloc_sbuf_tensor("vec", [P, N_VEC], F32)
        self.row = nc.alloc_sbuf_tensor("row", [P, N_ROW], F32)
        self.st = nc.alloc_sbuf_tensor("st", [P, 64], F32)
        self.pool_n = 30300
        self.ring0 = RING * CHUNK
        self.arena = nc.alloc_sbuf_tensor("arena", [P, self.ring0 + self.pool_n], F32)
        self.ps = [nc.alloc_psum_tensor(f"bank{b}", [P, 512], F32) for b in range(BANKS)]
        self.used = self.ring0
        self.ident = self.C[:, C_ID:C_ID + P]
        self.ones = self.C[:, C_ONE:C_ONE + P]
        self.tri = [self.C[:, C_TF:C_TF + P], self.C[:, C_TB:C_TB + P]]
        self.eps = self.C[:, C_EPS:C_EPS + 1]
        self.one = self.C[:, C_EPS + 1:C_EPS + 2]
        gather = [f"rows_landed{s}" for s in range(8)]
        self.gathered = [nc.alloc_semaphore(n) for n in gather]
        self.S = Sems(nc, NAMES + [f"weights_landed{i}" for i in range(RING)])

    def at(self, off, *shape):
        n = int(np.prod(shape))
        assert off + n <= self.pool_n, (off, shape)
        v = self.arena[:, self.ring0 + off:self.ring0 + off + n]
        if len(shape) == 2:
            v = v.rearrange("p (a b) -> p a b", a=shape[0])
        if len(shape) == 3:
            v = v.rearrange("p (a b c) -> p a b c", a=shape[0], b=shape[1])
        return v

    def place(self, chunk):
        n = self.chunks.index(chunk)
        return (n % RING if n < len(self.chunks) - 1 else RING) * CHUNK

    def weights(self, chunk, k, n):
        s = self.place(chunk)
        return self.arena[:, s:s + k * n].rearrange("p (k n) -> p k n", k=k)

    def load_weights(self, sp, l, upto):
        io = self.io
        while self.loaded < min(upto, len(self.chunks)):
            n = self.loaded
            kind, i = self.chunks[n]
            if n >= RING and n < len(self.chunks) - 1:
                sp.wait_ge(self.S["psum_full"], self.G.number(self.last[self.chunks[n - RING]]) + 1)
            src, width = {
                "big": (io["w_big"], CHUNK), "small": (io["w_small"], KD * 64),
                "uq": (io["w_uq"], KQ * 512), "ukv": (io["w_ukv"], 2048)}[kind]
            s = self.place(self.chunks[n])
            src = src[bass.ds(l, 1), i].rearrange("a p n -> p (a n)")
            sp.dma_start(self.arena[:, s:s + width], src).then_inc(self.S[f"weights_landed{n % RING}"], 16)
            self.loaded += 1

    def wait_weights(self, pe, chunk):
        n = self.chunks.index(chunk)
        pe.wait_ge(self.S[f"weights_landed{n % RING}"], 16 * (n // RING + 1))

    def bank(self, name):
        return self.ps[self.G.bank(name)]

    def wait_bank(self, pe, name):
        assert self.G.names[self.pe_at] == name, (self.G.names[self.pe_at], name)
        self.pe_at += 1
        old = self.G.reused(name)
        if old is not None:
            self.wait_taken(pe, old)

    def wait_taken(self, eng, name):
        by, n = self.G.taken(name)
        eng.wait_ge(self.S[by + "_took"], n)

    def wait_full(self, eng, name):
        eng.wait_ge(self.S["psum_full"], self.G.number(name) + 1)

    def full(self, ins):
        ins.then_inc(self.S["psum_full"], 1)

    def took(self, ins, name):
        by, n = self.G.taken(name)
        self.takes[by] += 1
        assert self.takes[by] == n, (name, self.takes[by], n)
        ins.then_inc(self.S[by + "_took"], 1)


NAMES = ["psum_full", "act_took", "dve_took", "dve_step", "act_step", "pool_step", "loads", "loads2", "loads3",
         "stores", "mod_scaled", "mod_stored", "stats_sq", "stats_var", "stats_sqrt", "h_ready", "h_read",
         "conv_ready", "u_ready", "sig_ready", "x_conv_done", "x_silu", "u_conv_done", "cq_ready", "kv_ready",
         "kr_ready", "q_roped", "rope_rows", "max_ready", "exp_ready", "o_ready", "dt_abs", "dt_ln", "cum_ready",
         "exps_ready", "seg_ready", "exp_seg", "m_ready", "xdt_ready", "xw_ready", "y_added", "h_next",
         "y_ready", "yn_ready", "uc_ready", "sq_ready", "ln_std", "ln_ready", "uT_ready", "gate_ready",
         "merged", "x_added", "s_ready", "s_read", "soft_in", "soft_exp", "routed", "staged", "dot_done",
         "gelu_done", "weight_done", "slot_done", "zeroed", "pads", "gw_staged", "state_out", "ctx_loads",
         "silu_c", "mean_ready", "lat_var", "dta_ready", "key_loads", "gates_ready", "squares"]


def modulate_and_norm(K, l):
    nc, S, io, G = K.nc, K.S, K.io, K.G
    rows = K.at(0, 6 * D)
    brow = K.at(6144, 8 * D)
    cT = K.at(14336, KD, 2)
    mrow = K.at(14400, 2, D)
    srow = K.at(16448, 2, D)
    sq = K.at(18496, D)
    steps = Steps(S["dve_step"])
    K.dve_steps = steps
    with nc.Block() as block:
        @block.sync
        def _(sp):
            sp.dma_start(brow[0:2, :], io["mod_rows"][bass.ds(l, 1), :].to_broadcast([2, 8 * D])).then_inc(S["loads"], 16)
            K.load_weights(sp, l, 12)
            sp.dma_start(K.vec[:, :], io["vecs"][bass.ds(l, 1)].rearrange("a p n -> p (a n)")).then_inc(S["loads2"], 16)
            sp.dma_start(K.row[:, :], io["rows"][bass.ds(l, 1), :].to_broadcast([P, N_ROW])).then_inc(S["loads2"], 16)
            K.load_weights(sp, l, 15)

        @block.scalar
        def _(act):
            act.dma_start(cT.rearrange("p a b -> p (a b)"), io["c_rows"]).then_inc(S["ctx_loads"], 16)
            act.wait_ge(S["ctx_loads"], 16)
            act_silu = nc.scalar.activation(cT, cT, ACT.Silu)
            act_silu.then_inc(S["silu_c"], 1)
            norm_act_stats(K, act, sq, 0)
            act.wait_ge(S["mod_scaled"], 2)
            K.wait_taken(act, ("mod", 3))
            act.dma_start(io["mod_scratch"][:, 0:2 * D], rows[0:2, 0:2 * D]).then_inc(S["mod_stored"], 16)
            act.wait_ge(S["mod_stored"], 16)
            for v, dst in ((1, mrow), (0, srow)):
                act.dma_start(dst, spread(io, v)).then_inc(S["loads3"], 16)
            act.wait_ge(S["mod_scaled"], 4)
            K.wait_taken(act, ("mod", 11))
            act.dma_start(io["mod_scratch"][:, 2 * D:6 * D], rows[0:2, 2 * D:6 * D]).then_inc(S["mod_stored"], 16)
            norm_act_take(K, act, "n1")
            act.wait_ge(S["mod_stored"], 32)

        @block.tensor
        def _(pe):
            pe.wait_ge(S["silu_c"], 1)
            for n in range(12):
                w = K.weights(("big", W_MOD + n), KD, 512)
                K.wait_weights(pe, ("big", W_MOD + n))
                K.wait_bank(pe, ("mod", n))
                for k in range(KD):
                    mm = nc.tensor.matmul(K.bank(("mod", n))[0:2, :], cT[:, k, :], w[:, k, :],
                                          start=k == 0, stop=k == KD - 1)
                K.full(mm)
            norm_pe(K, pe, "n1", 0)

        @block.vector
        def _(dve):
            norm_stats_dve(K, dve, 0)
            dve.wait_ge(S["loads"], 16)
            for n in range(12):
                v, half = n // 2, n % 2
                r = rows[0:2, n * 512:(n + 1) * 512]
                K.wait_full(dve, ("mod", n))
                K.took(nc.vector.tensor_tensor(r, K.bank(("mod", n))[0:2, :], brow[0:2, n * 512:(n + 1) * 512],
                                               ALU.add), ("mod", n))
                if v in (1, 4):
                    K.wait_taken(dve, ("mod", n))
                    g = 6 * D + (v // 3) * D + half * 512
                    nc.vector.scalar_tensor_tensor(out=r, in0=r, scalar=1.0, in1=brow[0:2, g:g + 512],
                                                   op0=ALU.add, op1=ALU.mult).then_inc(S["mod_scaled"], 1)
                if n == 7:
                    dve.wait_ge(S["loads3"], 32)
                    norm_apply_dve(K, dve, mrow, srow, 0)


def spread(io, v):
    t = io["mod_scratch"]
    return bass.AP(tensor=t.tensor, offset=v * D, ap=[[0, P], [6 * D, 2], [1, D]])


def norm_act_stats(K, act, sq, which, before=0):
    nc, S = K.nc, K.S
    for t in range(T):
        if t:
            act.wait_ge(S["stats_sq"], 3 * before + t)
        nc.scalar.activation(sq, K.x[:, t, :], ACT.Square,
                             accum_out=K.st[:, 8 * which + t:8 * which + t + 1]).then_inc(S["stats_sq"], 1)
    act.wait_ge(S["stats_var"], before + 1)
    nc.scalar.activation(K.st[:, 8 * which + 3:8 * which + 6], K.st[:, 8 * which:8 * which + 3],
                         ACT.Sqrt).then_inc(S["stats_sqrt"], 1)


def norm_act_take(K, act, name):
    nc = K.nc
    for t in range(T):
        for c in range(2):
            K.wait_full(act, (name, t, c))
            K.took(nc.scalar.copy(K.hT[:, 4 * c:4 * c + 4, t * P:(t + 1) * P],
                                  K.bank((name, t, c))[:, :].rearrange("p (k n) -> p k n", k=4)), (name, t, c))


def norm_stats_dve(K, dve, which, before=0):
    nc, S = K.nc, K.S
    s = K.st[:, 8 * which:8 * which + 3]
    dve.wait_ge(S["stats_sq"], 3 * before + 3)
    nc.vector.tensor_scalar(s, s, 1.0 / D, EPS, ALU.mult, ALU.add).then_inc(S["stats_var"], 1)
    dve.wait_ge(S["stats_sqrt"], before + 1)
    r = K.st[:, 8 * which + 3:8 * which + 6]
    dve.wait_ge(S["dve_step"], K.dve_steps(nc.vector.reciprocal(r, r)))


def norm_apply_dve(K, dve, mrow, srow, which):
    nc, S = K.nc, K.S
    for t in range(T):
        c = min(t, 1)
        n = K.dve_steps(nc.vector.scalar_tensor_tensor(
            out=K.hn[:, t, :], in0=K.x[:, t, :], scalar=K.st[:, 8 * which + 3 + t:8 * which + 4 + t],
            in1=mrow[:, c, :], op0=ALU.mult, op1=ALU.mult))
        dve.wait_ge(S["dve_step"], n)
        nc.vector.tensor_tensor(K.hn[:, t, :], K.hn[:, t, :], srow[:, c, :], ALU.add).then_inc(S["h_ready"], 1)


def norm_pe(K, pe, name, which):
    nc, S = K.nc, K.S
    for t in range(T):
        pe.wait_ge(S["h_ready"], 3 * which + t + 1)
        for c in range(2):
            K.wait_bank(pe, (name, t, c))
            for k in range(4):
                f = (4 * c + k) * P
                mm = nc.tensor.transpose(K.bank((name, t, c))[:, k * P:(k + 1) * P], K.hn[:, t, f:f + P], K.ident)
            K.full(mm)


A_CQKV, A_KRDT, A_Z, A_XBC, A_UIN = 0, 1536, 1728, 4800, 9432
A_FREE = A_UIN + KD * UIN


def tokens(t, pad):
    a = [0, P + pad, 2 * P + pad][t]
    return slice(a, a + P)


def taps(K, dve, dst, src, wcol, bcol, width, length, m, done, ms):
    nc, S = K.nc, K.S
    before = {}
    for k in range(width):
        for j in ms:
            o, i = dst[:, j, :], src[:, j % m, k:k + length]
            w = K.vec[:, wcol + width * j + k:wcol + width * j + k + 1]
            if k:
                dve.wait_ge(S["dve_step"], before[j])
                ins = nc.vector.scalar_tensor_tensor(out=o, in0=i, scalar=w, in1=o, op0=ALU.mult, op1=ALU.add)
            elif bcol is None:
                ins = nc.vector.tensor_scalar(o, i, w, None, ALU.mult)
            else:
                ins = nc.vector.tensor_scalar(o, i, w, K.vec[:, bcol + j:bcol + j + 1], ALU.mult, ALU.add)
            if k < width - 1:
                before[j] = K.dve_steps(ins)
            else:
                ins.then_inc(S[done], 1)
            yield


def project_in(K, l):
    nc, S, io, G = K.nc, K.S, K.io, K.G
    cqkv, krdt, z = K.at(A_CQKV, T, 512), K.at(A_KRDT, T, 64), K.at(A_Z, T, D)
    xbc, uin = K.at(A_XBC, XC, XOUT), K.at(A_UIN, KD, UIN)
    xin = K.at(A_FREE, 6, XIN)
    sig = K.at(A_FREE + 6 * XIN, 2, TOK)
    steps = K.dve_steps
    with nc.Block() as block:
        @block.sync
        def _(sp):
            K.load_weights(sp, l, 23 + 3)

        @block.gpsimd
        def _(pool):
            for a, b in ((0, 2), (2 + P, 4 + P), (XIN - 2, XIN)):
                nc.gpsimd.memset(xin[:, :, a:b], 0.0)
            for a, b in ((0, 15), (15 + P, 30 + P), (UIN - 15, UIN)):
                last = nc.gpsimd.memset(uin[:, :, a:b], 0.0)
            last.then_inc(S["pads"], 1)

        @block.tensor
        def _(pe):
            def by_tokens(name, chunk, width, t):
                w = K.weights(chunk, KD, width)
                K.wait_bank(pe, name)
                for k in range(KD):
                    mm = nc.tensor.matmul(K.bank(name)[:, 0:width], K.hT[:, k, t * P:(t + 1) * P], w[:, k, :],
                                          start=k == 0, stop=k == KD - 1)
                K.full(mm)

            def by_features(name, chunk, m):
                w = K.weights(chunk, KD, 512)
                K.wait_weights(pe, chunk)
                K.wait_bank(pe, name)
                for k in range(KD):
                    mm = nc.tensor.matmul(K.bank(name)[:, 0:TOK], w[:, k, m * P:(m + 1) * P], K.hT[:, k, :],
                                          start=k == 0, stop=k == KD - 1)
                K.full(mm)

            K.wait_weights(pe, ("big", W_CQKV))
            for t in range(T):
                by_tokens(("cqkv", t), ("big", W_CQKV), 512, t)
            K.wait_weights(pe, ("small", 0))
            for t in range(T):
                by_tokens(("krdt", t), ("small", 0), 64, t)
            for h in range(2):
                K.wait_weights(pe, ("big", W_Z + h))
                for t in range(T):
                    by_tokens(("z", h, t), ("big", W_Z + h), 512, t)
            for m in range(XC):
                by_features(("xbc", m), ("big", W_XBC + m // 4), m % 4)
            for m in range(KD):
                by_features(("gt", m), ("big", W_GLU + 2 * (m // 4)), m % 4)
                by_features(("a", m), ("big", W_GLU + 2 * (m // 4) + 1), m % 4)

        @block.scalar
        def _(act):
            for t in range(T):
                K.wait_full(act, ("cqkv", t))
                K.took(nc.scalar.copy(cqkv[:, t, :], K.bank(("cqkv", t))[:, :]), ("cqkv", t))
            for t in range(T):
                K.wait_full(act, ("krdt", t))
                K.took(nc.scalar.copy(krdt[:, t, :], K.bank(("krdt", t))[:, 0:64]), ("krdt", t))
            for h in range(2):
                for t in range(T):
                    K.wait_full(act, ("z", h, t))
                    K.took(nc.scalar.activation(z[:, t, h * 512:(h + 1) * 512], K.bank(("z", h, t))[:, :],
                                                ACT.Silu), ("z", h, t))
            act.wait_ge(S["pads"], 1)

            def silu(m):
                act.wait_ge(S["x_conv_done"], m + 1)
                nc.scalar.activation(xbc[:, m, :], xbc[:, m, :], ACT.Silu,
                                     bias=K.vec[:, V_CB + m:V_CB + m + 1]).then_inc(S["x_silu"], 1)

            for m in range(XC):
                if m >= 6:
                    act.wait_ge(S["x_conv_done"], m - 5)
                K.wait_full(act, ("xbc", m))
                b = K.bank(("xbc", m))
                nc.scalar.copy(xin[:, m % 6, 2:2 + P], b[:, 0:P])
                K.took(nc.scalar.copy(xin[:, m % 6, 4 + P:4 + 3 * P], b[:, P:3 * P]), ("xbc", m))
                if m >= 3:
                    silu(m - 3)
            for m in range(XC - 3, XC):
                silu(m)
            for m in range(KD):
                if m >= 2:
                    K.wait_taken(act, ("a", m - 2))
                K.wait_full(act, ("gt", m))
                K.took(nc.scalar.activation(sig[:, m % 2, :], K.bank(("gt", m))[:, 0:TOK], ACT.Sigmoid), ("gt", m))

        @block.vector
        def _(dve):
            dve.wait_ge(S["pads"], 1)
            dve.wait_ge(S["loads2"], 32)
            for m in range(0, XC, 2):
                K.wait_taken(dve, ("xbc", m + 1))
                for _ in taps(K, dve, xbc, xin, V_CW, None, XW, XOUT, 6, "x_conv_done", (m, m + 1)):
                    pass
            for m in range(0, KD, 2):
                for j in (m, m + 1):
                    K.wait_full(dve, ("a", j))
                    K.wait_taken(dve, ("gt", j))
                    b = K.bank(("a", j))
                    n = steps(nc.vector.tensor_tensor(uin[:, j, 15:15 + P], b[:, 0:P], sig[:, j % 2, 0:P], ALU.mult))
                    K.took(nc.vector.tensor_tensor(uin[:, j, 30 + P:30 + 3 * P], b[:, P:3 * P], sig[:, j % 2, P:3 * P],
                                                   ALU.mult), ("a", j))


KCOL = [0, 2, 3]


def attention(K, l):
    nc, S, io, G = K.nc, K.S, K.io, K.G
    cqkv, krdt = K.at(A_CQKV, T, 512), K.at(A_KRDT, T, 64)
    o = K.hn
    off = A_FREE
    cqT = K.at(off, KQ, TOK)
    ckvT = K.at(off + 1152, 512)
    krT = K.at(off + 1664, 512)
    q = K.at(off + 2176, T, HEADS * QK)
    v = K.at(off + 6784, 4, HEADS * VD)
    kT = K.at(off + 10880, 4, 512)
    qT = K.at(off + 12928, 2, TOK)
    pr = K.at(off + 13696, 2, 896)
    pT = K.at(off + 15504, 2, 896)
    krp = K.at(off + 10880, T, QK)
    tmp = K.at(off + 10880 + T * QK, HEADS * ROPE)
    mx = K.at(off + 15488, 2, 4)
    sm = K.at(off + 15496, 2, 4)
    steps = K.dve_steps
    st = K.st
    SC = QK ** -0.5
    with nc.Block() as block:
        @block.sync
        def _(sp):
            sp.dma_start(ckvT[:, P:2 * P], io["cache_kvT"][bass.ds(l, 1)].rearrange("a p n -> p (a n)")).then_inc(S["ctx_loads"], 16)
            sp.dma_start(krT[NOPE:QK, P:2 * P], io["cache_krT"][bass.ds(l, 1)].rearrange("a p n -> p (a n)")).then_inc(S["ctx_loads"], 16)
            sp.dma_start(io["new_krope"][bass.ds(l, 1)].rearrange("a p n -> p (a n)"), krdt[:, 0, 0:ROPE]).then_inc(S["stores"], 16)
            sp.wait_ge(S["kv_ready"], 3)
            sp.dma_start(io["new_ckv"][bass.ds(l, 1)].rearrange("a p n -> p (a n)"), cqkv[:, 0, Q_RANK:512]).then_inc(S["stores"], 16)
            K.load_weights(sp, l, 30)
            sp.wait_ge(S["stores"], 32)

        @block.scalar
        def _(act):
            for t in range(T):
                nc.scalar.activation(q[:, t, 0:Q_RANK], cqkv[:, t, 0:Q_RANK], ACT.Square,
                                     accum_out=st[:, 16 + t:17 + t])
                nc.scalar.activation(q[:, t, Q_RANK:512], cqkv[:, t, Q_RANK:512], ACT.Square,
                                     accum_out=st[:, 19 + t:20 + t]).then_inc(S["sq_ready"], 1)
            act.wait_ge(S["lat_var"], 1)
            nc.scalar.activation(st[:, 16:22], st[:, 16:22], ACT.Sqrt).then_inc(S["ln_std"], 1)
            act.wait_ge(S["loads2"], 32)
            for t in range(T):
                K.wait_full(act, ("cqT", t))
                for k in range(KQ):
                    ins = nc.scalar.activation(cqT[:, k, t * P:(t + 1) * P], K.bank(("cqT", t))[:, k * P:(k + 1) * P],
                                               ACT.Copy, scale=K.vec[:, V_GQ + k:V_GQ + k + 1])
                K.took(ins, ("cqT", t))
            K.wait_full(act, ("kvT", 0))
            b = K.bank(("kvT", 0))
            nc.scalar.copy(ckvT[:, 0:P], b[:, 0:P])
            K.took(nc.scalar.copy(ckvT[:, 2 * P:4 * P], b[:, P:3 * P]), ("kvT", 0))
            for c in range(3):
                for t in range(T):
                    K.wait_full(act, ("q", c, t))
                    K.took(nc.scalar.copy(q[:, t, c * 512:(c + 1) * 512], K.bank(("q", c, t))[:, :]), ("q", c, t))
            for step, h in attention_order():
                if step == "QT":
                    if h >= 2:
                        K.wait_full(act, ("SB", h - 2))
                    K.wait_full(act, (step, h))
                    K.took(nc.scalar.copy(qT[0:QK, h % 2, :], K.bank((step, h))[0:QK, 0:TOK]), (step, h))
                if step == "SB":
                    act.wait_ge(S["max_ready"], h + 1)
                    if h >= 2:
                        K.wait_full(act, ("PB", h - 2))
                        K.wait_taken(act, ("PV", h - 2))
                    pieces = [("SA", 0, P, 0), ("SA", P, 512, 1), ("SB", 0, TOK, 2)]
                    for name, a, z, j in pieces:
                        d = 0 if name == "SA" else 512
                        ins = nc.scalar.activation(pr[:, h % 2, d + a:d + z], K.bank((name, h))[:, a:z], ACT.Exp,
                                                   bias=mx[:, h % 2, j:j + 1], scale=SC,
                                                   accum_out=sm[:, h % 2, j:j + 1])
                        if j:
                            K.took(ins, (name, h))
                if step == "PB":
                    if h >= 2:
                        K.wait_full(act, ("PV", h - 2))
                    K.wait_full(act, (step, h))
                    K.took(nc.scalar.copy(pT[:, h % 2, 512:896], K.bank((step, h))[:, 0:TOK]), (step, h))

        @block.tensor
        def _(pe):
            for t in range(T):
                pe.wait_ge(S["cq_ready"], t + 1)
                K.wait_bank(pe, ("cqT", t))
                for k in range(KQ):
                    mm = nc.tensor.transpose(K.bank(("cqT", t))[:, k * P:(k + 1) * P], cqkv[:, t, k * P:(k + 1) * P], K.ident)
                K.full(mm)
            pe.wait_ge(S["kv_ready"], 3)
            K.wait_bank(pe, ("kvT", 0))
            for t in range(T):
                mm = nc.tensor.transpose(K.bank(("kvT", 0))[:, t * P:(t + 1) * P], cqkv[:, t, Q_RANK:512], K.ident)
            K.full(mm)
            pe.wait_ge(S["kr_ready"], 1)
            K.wait_bank(pe, ("krT", 0))
            for t in range(T):
                mm = nc.tensor.transpose(K.bank(("krT", 0))[0:QK, t * P:(t + 1) * P], krp[:, t, :], K.ident)
            K.full(mm)
            K.wait_taken(pe, ("cqT", 2))
            for c in range(3):
                w = K.weights(("uq", c), KQ, 512)
                K.wait_weights(pe, ("uq", c))
                for t in range(T):
                    K.wait_bank(pe, ("q", c, t))
                    for k in range(KQ):
                        mm = nc.tensor.matmul(K.bank(("q", c, t))[:, :], cqT[:, k, t * P:(t + 1) * P], w[:, k, :],
                                              start=k == 0, stop=k == KQ - 1)
                    K.full(mm)
            wv = K.weights(("ukv", 0), HEADS, P)
            K.wait_weights(pe, ("ukv", 0))
            pe.wait_ge(S["ctx_loads"], 48)
            K.wait_taken(pe, ("kvT", 0))
            for kt in range(4):
                for c in range(2):
                    K.wait_bank(pe, ("v", kt, c))
                    K.full(nc.tensor.matmul(K.bank(("v", kt, c))[:, :], ckvT[:, kt * P:(kt + 1) * P],
                                            wv[:, 8 * c:8 * c + 8, NOPE:P], start=True, stop=True))
            for step, h in attention_order():
                b = K.bank((step, h))
                if step == "K":
                    K.wait_bank(pe, (step, h))
                    K.full(nc.tensor.matmul(b[0:NOPE, :], wv[:, h, 0:NOPE], ckvT[:, :], start=True, stop=True))
                if step == "QT":
                    if h == 0:
                        pe.wait_ge(S["q_roped"], 2)
                        K.wait_taken(pe, ("q", 2, 2))
                    K.wait_bank(pe, (step, h))
                    for t in range(T):
                        mm = nc.tensor.transpose(b[0:QK, t * P:(t + 1) * P], q[:, t, h * QK:(h + 1) * QK], K.ident)
                    K.full(mm)
                if step == "SA":
                    K.wait_taken(pe, ("K", h))
                    K.wait_taken(pe, ("QT", h))
                    if h == 0:
                        pe.wait_ge(S["rope_rows"], 1)
                    K.wait_bank(pe, (step, h))
                    nc.tensor.matmul(b[:, 0:P], qT[0:QK, h % 2, 0:P], kT[0:QK, h % 4, 0:P], start=True, stop=True)
                    K.full(nc.tensor.matmul(b[:, P:512], qT[0:QK, h % 2, P:2 * P], kT[0:QK, h % 4, P:512],
                                            start=True, stop=True))
                if step == "SB":
                    K.wait_bank(pe, (step, h))
                    K.full(nc.tensor.matmul(b[:, 0:TOK], qT[0:QK, h % 2, 2 * P:3 * P], kT[0:QK, h % 4, P:512],
                                            start=True, stop=True))
                if step in ("PA", "PB"):
                    K.wait_taken(pe, ("SB", h))
                    K.wait_bank(pe, (step, h))
                    d = 0 if step == "PA" else 512
                    for j in range(4 if step == "PA" else 3):
                        mm = nc.tensor.transpose(b[:, j * P:(j + 1) * P], pr[:, h % 2, d + j * P:d + (j + 1) * P], K.ident)
                    K.full(mm)
                if step == "PV":
                    K.wait_taken(pe, ("PA", h))
                    K.wait_taken(pe, ("PB", h))
                    K.wait_bank(pe, (step, h))
                    vh = v[:, :, h * VD:(h + 1) * VD]
                    nc.tensor.matmul(b[:, 0:VD], pT[:, h % 2, 0:P], vh[:, 0, :], start=True, stop=True)
                    for t in (1, 2):
                        for j in range(3):
                            a = ((1 if t == 1 else 4) + j) * P
                            mm = nc.tensor.matmul(b[:, t * VD:(t + 1) * VD], pT[:, h % 2, a:a + P], vh[:, 1 + j, :],
                                                  start=j == 0, stop=j == 2)
                    K.full(mm)

        @block.vector
        def _(dve):
            dve.wait_ge(S["sq_ready"], 3)
            n = steps(nc.vector.tensor_scalar(st[:, 16:19], st[:, 16:19], 1.0 / Q_RANK, EPS, ALU.mult, ALU.add))
            nc.vector.tensor_scalar(st[:, 19:22], st[:, 19:22], 1.0 / KV_RANK, EPS, ALU.mult, ALU.add).then_inc(S["lat_var"], 1)
            dve.wait_ge(S["ln_std"], 1)
            dve.wait_ge(S["dve_step"], steps(nc.vector.reciprocal(st[:, 16:22], st[:, 16:22])))
            dve.wait_ge(S["loads2"], 32)
            for t in range(T):
                nc.vector.tensor_scalar(cqkv[:, t, 0:Q_RANK], cqkv[:, t, 0:Q_RANK], st[:, 16 + t:17 + t], None,
                                        ALU.mult).then_inc(S["cq_ready"], 1)
                nc.vector.scalar_tensor_tensor(out=cqkv[:, t, Q_RANK:512], in0=cqkv[:, t, Q_RANK:512],
                                               scalar=st[:, 19 + t:20 + t], in1=K.row[:, R_GKV:R_GKV + P],
                                               op0=ALU.mult, op1=ALU.mult).then_inc(S["kv_ready"], 1)

            def rope(src, dst, scratch, heads, t, last=None):
                C = K.C[:, C_RC + 32 * (t - 1):C_RC + 32 * t].rearrange("p (a b n) -> p a b n", a=2, b=2)
                Z = K.C[:, C_RS + 32 * (t - 1):C_RS + 32 * t].rearrange("p (a b n) -> p a b n", a=2, b=2)
                for b in range(2):
                    for a in range(2):
                        s0 = src[:, :, 16 * a + 8 * (1 - b):16 * a + 8 * (1 - b) + 8]
                        o0 = scratch[:, :, 16 * a + 8 * b:16 * a + 8 * b + 8]
                        z0 = Z[:, a, b, :].unsqueeze(1).to_broadcast([P, heads, 8])
                        n = steps(nc.vector.tensor_tensor(o0, s0, z0, ALU.mult))
                cc = K.C[:, C_RC + 32 * (t - 1):C_RC + 32 * t].unsqueeze(1).to_broadcast([P, heads, ROPE])
                dve.wait_ge(S["dve_step"], n)
                n = steps(nc.vector.tensor_tensor(dst, src, cc, ALU.mult))
                dve.wait_ge(S["dve_step"], n)
                ins = nc.vector.tensor_tensor(dst, dst, scratch, ALU.add)
                if last:
                    ins.then_inc(S[last], 1)
                else:
                    steps(ins)

            steps(nc.vector.memset(krp[:, :, 0:NOPE], 0.0))
            steps(nc.vector.tensor_copy(krp[:, 0, NOPE:QK], krdt[:, 0, 0:ROPE]))
            for t in (1, 2):
                rope(krdt[:, t:t + 1, 0:ROPE], krp[:, t:t + 1, NOPE:QK],
                     tmp[:, 32 * t:32 * t + 32].unsqueeze(1), 1, t, "kr_ready" if t == 2 else None)
            K.wait_full(dve, ("krT", 0))
            b = K.bank(("krT", 0))
            steps(nc.vector.tensor_copy(krT[NOPE:QK, 0:P], b[NOPE:QK, 0:P]))
            K.took(nc.vector.tensor_copy(krT[NOPE:QK, 2 * P:4 * P], b[NOPE:QK, P:3 * P]), ("krT", 0))
            for t in (1, 2):
                K.wait_taken(dve, ("q", 2, t))
                if t == 2:
                    dve.wait_ge(S["q_roped"], 1)
                qr = q[:, t, :].rearrange("p (h n) -> p h n", h=HEADS)[:, :, NOPE:QK]
                rope(qr, qr, tmp.rearrange("p (h n) -> p h n", h=HEADS), HEADS, t, "q_roped")
            dve.wait_ge(S["q_roped"], 2)
            dve.wait_ge(S["ctx_loads"], 48)
            K.wait_taken(dve, ("krT", 0))
            nc.vector.tensor_copy(kT[NOPE:QK, :, :], krT[NOPE:QK, :].unsqueeze(1).to_broadcast([ROPE, 4, 512]))\
                .then_inc(S["rope_rows"], 1)
            for kt in range(4):
                for c in range(2):
                    K.wait_full(dve, ("v", kt, c))
                    K.took(nc.vector.tensor_copy(v[:, kt, c * 512:(c + 1) * 512], K.bank(("v", kt, c))[:, :]), ("v", kt, c))
            for step, h in attention_order():
                b = K.bank((step, h))
                if step == "K":
                    if h >= 4:
                        K.wait_full(dve, ("SB", h - 4))
                    K.wait_full(dve, (step, h))
                    K.took(nc.vector.tensor_copy(kT[0:NOPE, h % 4, :], b[0:NOPE, :]), (step, h))
                if step == "SB":
                    K.wait_full(dve, ("SB", h))
                    if h >= 2:
                        K.wait_taken(dve, ("SB", h - 2))
                    sa = K.bank(("SA", h))
                    steps(nc.vector.reduce_max(mx[:, h % 2, 0:1], sa[:, 0:P], AX.X))
                    steps(nc.vector.reduce_max(mx[:, h % 2, 1:2], sa[:, P:512], AX.X))
                    n = steps(nc.vector.reduce_max(mx[:, h % 2, 2:3], b[:, 0:TOK], AX.X))
                    dve.wait_ge(S["dve_step"], n)
                    nc.vector.tensor_scalar(mx[:, h % 2, 0:3], mx[:, h % 2, 0:3], -SC, None, ALU.mult)\
                        .then_inc(S["max_ready"], 1)
                if step == "PA":
                    if h >= 2:
                        K.wait_full(dve, ("PV", h - 2))
                    K.wait_full(dve, (step, h))
                    K.took(nc.vector.tensor_copy(pT[:, h % 2, 0:512], b[:, :]), (step, h))
                if step == "PV":
                    K.wait_taken(dve, ("SB", h))
                    n = steps(nc.vector.reciprocal(sm[:, h % 2, 0:3], sm[:, h % 2, 0:3]))
                    dve.wait_ge(S["dve_step"], n)
                    K.wait_full(dve, (step, h))
                    K.took(nc.vector.tensor_tensor(
                        o[:, :, h * VD:(h + 1) * VD], b[:, 0:T * VD].rearrange("p (t n) -> p t n", t=T),
                        sm[:, h % 2, 0:3].unsqueeze(2).to_broadcast([P, T, VD]), ALU.mult), (step, h))


def ssd(K, l):
    nc, S, io, G = K.nc, K.S, K.io, K.G
    krdt, z = K.at(A_KRDT, T, 64), K.at(A_Z, T, D)
    xbc = K.at(A_XBC, XC, XOUT)
    off = A_FREE
    xs = K.at(off, T, D)
    bt = K.at(off + 3072, T, 2 * SN)
    cbm = K.at(off + 3840, 2, 6 * P)
    y = K.at(off + 5376, T, D)
    H = K.at(off + 8448, 2, D)
    xdt = K.at(off + 10496, 2, 512)
    xw = K.at(off + 11520, 512)
    seg = K.at(off + 12032, 2, 512)
    M = K.at(off + 13056, 2, 512)
    tmp = K.at(off + 14080, 512)
    sm = off + 14592
    raw, dt, aA, ab, acum, tot = [K.at(sm + 96 * i, 96) for i in range(6)]
    ea, dend, etot = [K.at(sm + 96 * i, 96) for i in range(6, 9)]
    A = K.at(A_CQKV, 32)
    outs = K.at(A_CQKV + 64, 2, 512)
    steps = K.dve_steps
    units = [(t, d, g) for t, d in SSD_UNITS for g in range(SG)]

    def heads(a, u):
        t, d, g = u
        c = 32 * t + 16 * d + 8 * g
        return a[:, c:c + 8]

    def spread8(a, u):
        return heads(a, u).unsqueeze(2).to_broadcast([P, HG, SP_])

    def h8(v):
        return v.rearrange("p (h n) -> p h n", h=HG)

    with nc.Block() as block:
        @block.sync
        def _(sp):
            sp.dma_start(H, io["h0T"][bass.ds(l, 1)].rearrange("a p n -> p (a n)").rearrange("p (d n) -> p d n", d=2)).then_inc(S["ctx_loads"], 16)
            for u in units:
                if u[0] == 0:
                    K.wait_taken(sp, ("CS", u))
                    dst = io["new_state"][bass.ds(l, 1), u[1]].rearrange("a p n -> p (a n)")[:, u[2] * 512:(u[2] + 1) * 512]
                    sp.dma_start(dst, outs[:, u[2], :]).then_inc(S["stores"], 16)
            sp.wait_ge(S["stores"], 32 + 64)

        @block.scalar
        def _(act):
            act.wait_ge(S["dt_abs"], 1)
            nc.scalar.activation(ab, ab, ACT.Exp, scale=-1.0).then_inc(S["act_step"], 1)
            nc.scalar.activation(A, K.row[:, R_ALOG:R_ALOG + 32], ACT.Exp).then_inc(S["act_step"], 1)
            act.wait_ge(S["act_step"], 1)
            nc.scalar.activation(ab, ab, ACT.Ln, bias=K.one).then_inc(S["dt_ln"], 1)
            for t in range(T):
                for c in range(2):
                    K.wait_full(act, ("xs", t, c))
                    K.took(nc.scalar.copy(xs[:, t, c * 512:(c + 1) * 512], K.bank(("xs", t, c))[:, :]), ("xs", t, c))
            for g in range(SG):
                K.wait_full(act, ("bt", g))
                K.took(nc.scalar.copy(bt[:, :, g * SN:(g + 1) * SN],
                                      K.bank(("bt", g))[:, 0:TOK].rearrange("p (t n) -> p t n", t=T)), ("bt", g))
            act.wait_ge(S["cum_ready"], 1)
            nc.scalar.activation(ea, acum, ACT.Exp)
            nc.scalar.activation(dend, dend, ACT.Exp)
            nc.scalar.activation(etot, tot, ACT.Exp).then_inc(S["exps_ready"], 1)
            for i in range(2 * len(units)):
                K.wait_taken(act, (f"AB{i % 2}", units[i // 2]))
                if i >= 2:
                    act.wait_ge(S["m_ready"], i - 1)
                nc.scalar.activation(seg[:, i % 2, :], seg[:, i % 2, :], ACT.Exp).then_inc(S["exp_seg"], 1)

        @block.tensor
        def _(pe):
            pe.wait_ge(S["dta_ready"], 1)
            K.wait_bank(pe, ("cum", 0))
            b = K.bank(("cum", 0))
            for t in range(T):
                for d in range(2):
                    c = 32 * t + 16 * d
                    nc.tensor.matmul(b[:, c:c + 16], K.tri[d], aA[:, c:c + 16], start=True, stop=True)
            K.full(nc.tensor.matmul(b[:, 96:192], K.ones, aA, start=True, stop=True))
            for t in range(T):
                for c in range(2):
                    K.wait_bank(pe, ("xs", t, c))
                    for k in range(4):
                        mm = nc.tensor.transpose(K.bank(("xs", t, c))[:, k * P:(k + 1) * P],
                                                 xbc[:, 4 * c + k, tokens(t, 2)], K.ident)
                    K.full(mm)
            for g in range(SG):
                K.wait_bank(pe, ("bt", g))
                for t in range(T):
                    mm = nc.tensor.transpose(K.bank(("bt", g))[:, t * P:(t + 1) * P], xbc[:, 8 + g, tokens(t, 2)], K.ident)
                K.full(mm)
            for j in range(2):
                K.wait_bank(pe, ("cb", j))
                for i in range(4 * j, min(4 * j + 4, 6)):
                    t, g = i // 2, i % 2
                    mm = nc.tensor.matmul(K.bank(("cb", j))[:, (i % 4) * P:(i % 4 + 1) * P], xbc[:, 8 + g, tokens(t, 2)],
                                          xbc[:, 10 + g, tokens(t, 2)], start=True, stop=True)
                K.full(mm)
            n_xw = 0
            pe.wait_ge(S["ctx_loads"], 64)
            for step, u in ssd_order():
                t, d, g = u
                i = units.index(u)
                name = (step, u)
                b = K.bank(name)
                if step in ("AB0", "AB1"):
                    K.wait_bank(pe, name)
                    for j in range(4):
                        c = 32 * t + 16 * d + 8 * g + 4 * (step == "AB1") + j
                        mm = nc.tensor.matmul(b[:, j * P:(j + 1) * P], aA[:, c:c + 1].to_broadcast([P, P]), K.tri[d],
                                              start=True, stop=True)
                    K.full(mm)
                if step == "YD":
                    pe.wait_ge(S["xdt_ready"], i + 1)
                    K.wait_bank(pe, name)
                    for j in range(HG):
                        if j % 4 == 0:
                            pe.wait_ge(S["m_ready"], 2 * i + j // 4 + 1)
                        mm = nc.tensor.matmul(b[:, j * SP_:(j + 1) * SP_], M[:, j // 4, (j % 4) * P:(j % 4 + 1) * P],
                                              xdt[:, i % 2, j * SP_:(j + 1) * SP_], start=True, stop=True)
                    K.full(mm)
                if step == "YO":
                    if (t, d) in ((2, 0), (1, 1)):
                        K.wait_taken(pe, ("CS", (3 - t, d, g)))
                    K.wait_bank(pe, name)
                    K.full(nc.tensor.matmul(b[:, :], xbc[:, 10 + g, tokens(t, 2)], H[:, d, g * 512:(g + 1) * 512],
                                            start=True, stop=True))
                if step == "CS":
                    n_xw += 1
                    pe.wait_ge(S["xw_ready"], n_xw)
                    K.wait_bank(pe, name)
                    K.full(nc.tensor.matmul(b[:, :], bt[:, t, g * SN:(g + 1) * SN], xw, start=True, stop=True))

        @block.vector
        def _(dve):
            r3 = raw.rearrange("p (t n) -> p t n", t=T)
            n = steps(nc.vector.tensor_tensor(r3, krdt[:, :, 32:64],
                                              K.row[:, R_DTB:R_DTB + 32].unsqueeze(1).to_broadcast([P, T, 32]), ALU.add))
            dve.wait_ge(S["dve_step"], n)
            nc.vector.scalar_tensor_tensor(out=ab, in0=raw, scalar=-1.0, in1=raw, op0=ALU.mult, op1=ALU.max).then_inc(S["dt_abs"], 1)
            n = steps(nc.vector.tensor_scalar(dt, raw, 0.0, None, ALU.max))
            dve.wait_ge(S["dve_step"], n)
            dve.wait_ge(S["dt_ln"], 1)
            n = steps(nc.vector.tensor_tensor(dt, dt, ab, ALU.add))
            dve.wait_ge(S["dve_step"], n)
            dve.wait_ge(S["act_step"], 2)
            nc.vector.scalar_tensor_tensor(out=aA.rearrange("p (t n) -> p t n", t=T), in0=dt.rearrange("p (t n) -> p t n", t=T),
                                           scalar=-1.0, in1=A.unsqueeze(1).to_broadcast([P, T, 32]),
                                           op0=ALU.mult, op1=ALU.mult).then_inc(S["dta_ready"], 1)
            K.wait_full(dve, ("cum", 0))
            b = K.bank(("cum", 0))
            steps(nc.vector.tensor_copy(acum, b[:, 0:96]))
            K.took(nc.vector.tensor_copy(tot, b[:, 96:192]), ("cum", 0))
            K.wait_taken(dve, ("cum", 0))
            nc.vector.tensor_tensor(dend, tot, acum, ALU.subtract).then_inc(S["cum_ready"], 1)
            for t in range(T):
                K.wait_taken(dve, ("xs", t, 1))
                n = steps(nc.vector.tensor_tensor(
                    y[:, t, :].rearrange("p (h n) -> p h n", h=SH), xs[:, t, :].rearrange("p (h n) -> p h n", h=SH),
                    K.row[:, R_D:R_D + SH].unsqueeze(2).to_broadcast([P, SH, SP_]), ALU.mult))
            dve.wait_ge(S["dve_step"], n)
            for j in range(2):
                K.wait_full(dve, ("cb", j))
                cnt = 4 if j == 0 else 2
                src = K.bank(("cb", j))[:, 0:cnt * P].rearrange("p (a n) -> p a n", a=cnt)
                for d in range(2):
                    dst = cbm[:, d, 4 * j * P:(4 * j + cnt) * P].rearrange("p (a n) -> p a n", a=cnt)
                    ins = nc.vector.tensor_tensor(dst, src, K.tri[d].unsqueeze(1).to_broadcast([P, cnt, P]), ALU.mult)
                    if d:
                        K.took(ins, ("cb", j))
            K.wait_taken(dve, ("cb", 1))
            dve.wait_ge(S["exps_ready"], 1)
            n_h = n_out = 0
            y_last = {}
            for step, u in ssd_order():
                t, d, g = u
                i = units.index(u)
                name = (step, u)
                b = K.bank(name)
                yv = y[:, t, g * 512:(g + 1) * 512]
                if step == "AB0":
                    if i >= 2:
                        K.wait_full(dve, ("YD", units[i - 2]))
                    nc.vector.tensor_tensor(h8(xdt[:, i % 2, :]), h8(xs[:, t, g * 512:(g + 1) * 512]), spread8(dt, u),
                                            ALU.mult).then_inc(S["xdt_ready"], 1)
                if step in ("AB0", "AB1"):
                    k = 2 * i + (step == "AB1")
                    K.wait_full(dve, name)
                    if k >= 2:
                        dve.wait_ge(S["m_ready"], k - 1)
                    for j in range(4):
                        c = 32 * t + 16 * d + 8 * g + 4 * (step == "AB1") + j
                        ins = nc.vector.tensor_scalar(seg[:, k % 2, j * P:(j + 1) * P], b[:, j * P:(j + 1) * P],
                                                      acum[:, c:c + 1], 0.0, ALU.subtract, ALU.min)
                        if j < 3:
                            steps(ins)
                    K.took(ins, name)
                if step == "AB1":
                    for k in (2 * i, 2 * i + 1):
                        dve.wait_ge(S["exp_seg"], k + 1)
                        if i >= 1:
                            K.wait_full(dve, ("YD", units[i - 1]))
                        cb = cbm[:, d, (2 * t + g) * P:(2 * t + g + 1) * P].unsqueeze(1).to_broadcast([P, 4, P])
                        nc.vector.tensor_tensor(M[:, k % 2, :].rearrange("p (a n) -> p a n", a=4),
                                                seg[:, k % 2, :].rearrange("p (a n) -> p a n", a=4), cb,
                                                ALU.mult).then_inc(S["m_ready"], 1)
                    if state_of(u):
                        prev = [w for w in units[:i] if state_of(w)]
                        if prev:
                            K.wait_full(dve, ("CS", prev[-1]))
                        dve.wait_ge(S["xdt_ready"], i + 1)
                        nc.vector.tensor_tensor(h8(xw), h8(xdt[:, i % 2, :]), spread8(dend, u), ALU.mult).then_inc(S["xw_ready"], 1)
                if step == "YD":
                    if (t, g) in y_last:
                        dve.wait_ge(S["dve_step"], y_last[(t, g)])
                    K.wait_full(dve, name)
                    K.took(nc.vector.tensor_tensor(yv, yv, b[:, :], ALU.add), name)
                    K.wait_taken(dve, name)
                if step == "YO":
                    K.wait_full(dve, name)
                    K.took(nc.vector.tensor_tensor(h8(tmp), h8(b[:, :]), spread8(ea, u), ALU.mult), name)
                    K.wait_taken(dve, name)
                    y_last[(t, g)] = steps(nc.vector.tensor_tensor(yv, yv, tmp, ALU.add))
                if step == "CS":
                    K.wait_full(dve, name)
                    if t == 0:
                        if n_out >= 2:
                            dve.wait_ge(S["stores"], 32 + 32)
                        K.took(nc.vector.tensor_copy(outs[:, g, :], b[:, :]), name)
                        n_out += 1
                    else:
                        if ("YO", u) in G.names:
                            K.wait_full(dve, ("YO", u))
                        dve.wait_ge(S["ctx_loads"], 64)
                        Hs = H[:, d, g * 512:(g + 1) * 512]
                        n = steps(nc.vector.tensor_tensor(h8(Hs), h8(Hs), spread8(etot, u), ALU.mult))
                        dve.wait_ge(S["dve_step"], n)
                        K.took(nc.vector.tensor_tensor(Hs, Hs, b[:, :], ALU.add), name)


def branches(K, l):
    nc, S, io, G = K.nc, K.S, K.io, K.G
    z, uin = K.at(A_Z, T, D), K.at(A_UIN, KD, UIN)
    off = A_FREE
    y = K.at(off + 5376, T, D)
    oT = K.at(off, KD, TOK)
    yT = K.at(A_XBC, KD, TOK)
    uT = K.at(A_UIN, KD, TOK)
    merged = K.hn[:, :, :].rearrange("p t n -> p (t n)").rearrange("p (k n) -> p k n", k=KD)
    mean = K.at(A_CQKV, UOUT)
    std = K.at(A_CQKV + 400, UOUT)
    gs = K.at(A_CQKV + 800, 2, TOK)
    tmp = K.at(off + 3072, 2, 512)
    sqt = K.at(off + 4096, D)
    gt = K.at(A_Z, 2, D)
    uc = K.at(off + 8448, KD, UOUT)
    squ = K.at(off + 11640, KD, UOUT)
    steps = K.dve_steps
    st = K.st
    srcs = [oT, yT, uT]
    with nc.Block() as block:
        @block.sync
        def _(sp):
            sp.wait_ge(S["y_ready"], 3)
            sp.dma_start(gt, spread(io, 2)).then_inc(S["loads3"], 16)
            K.load_weights(sp, l, len(K.chunks) - 1)

        @block.scalar
        def _(act):
            for k in range(KD):
                K.wait_full(act, ("oT", k))
                K.took(nc.scalar.copy(oT[:, k, :], K.bank(("oT", k))[:, 0:TOK]), ("oT", k))
            for t in range(T):
                act.wait_ge(S["y_ready"], t + 1)
                act.wait_ge(S["stats_sq"], 3 + t)
                nc.scalar.activation(sqt, y[:, t, :], ACT.Square, accum_out=st[:, 24 + t:25 + t]).then_inc(S["stats_sq"], 1)
            act.wait_ge(S["stats_var"], 2)
            nc.scalar.activation(st[:, 27:30], st[:, 24:27], ACT.Sqrt).then_inc(S["stats_sqrt"], 1)
            for k in range(KD):
                K.wait_full(act, ("yT", k))
                K.took(nc.scalar.activation(yT[:, k, :], K.bank(("yT", k))[:, 0:TOK], ACT.Copy,
                                            scale=K.vec[:, V_GS + k:V_GS + k + 1]), ("yT", k))
            for i, (br, h, m) in enumerate(BRANCH_ORDER):
                name = ("gate", br, h, m)
                if i >= 2:
                    K.wait_taken(act, ("br", *BRANCH_ORDER[i - 2]))
                K.wait_full(act, name)
                c = V_BG + 8 * br + 4 * h + m
                K.took(nc.scalar.activation(gs[:, i % 2, :], K.bank(name)[:, 0:TOK], ACT.Sigmoid,
                                            bias=K.vec[:, c:c + 1]), name)
                if LN_AFTER.get((br, h, m)) == "mu":
                    K.wait_full(act, ("mu", 0))
                    K.took(nc.scalar.mul(mean, K.bank(("mu", 0))[:, 0:UOUT], 1.0 / D), ("mu", 0))
                    act.wait_ge(S["uc_ready"], 1)
                    for k in range(KD):
                        nc.scalar.activation(squ[:, k, :], uc[:, k, :], ACT.Square).then_inc(S["squares"], 1)
                if LN_AFTER.get((br, h, m)) == "var":
                    K.wait_full(act, ("var", 0))
                    K.took(nc.scalar.activation(std, K.bank(("var", 0))[:, 0:UOUT], ACT.Sqrt, scale=1.0 / D, bias=K.eps), ("var", 0))
                    act.wait_ge(S["ln_ready"], 1)
                    for k in range(KD):
                        for a, e, b0 in ((0, P, 0), (P + 15, UOUT, P)):
                            ins = nc.scalar.activation(uT[:, k, b0:b0 + e - a], uc[:, k, a:e], ACT.Silu,
                                                       scale=K.vec[:, V_LG + k:V_LG + k + 1], bias=K.vec[:, V_LB + k:V_LB + k + 1])
                    ins.then_inc(S["uT_ready"], 1)

        @block.tensor
        def _(pe):
            for k in range(KD):
                K.wait_bank(pe, ("oT", k))
                for t in range(T):
                    mm = nc.tensor.transpose(K.bank(("oT", k))[:, t * P:(t + 1) * P], K.hn[:, t, k * P:(k + 1) * P], K.ident)
                K.full(mm)
            pe.wait_ge(S["yn_ready"], 3)
            for k in range(KD):
                K.wait_bank(pe, ("yT", k))
                for t in range(T):
                    mm = nc.tensor.transpose(K.bank(("yT", k))[:, t * P:(t + 1) * P], y[:, t, k * P:(k + 1) * P], K.ident)
                K.full(mm)
            for br, h, m in BRANCH_ORDER:
                for what, name, src in (("g", ("gate", br, h, m), K.hT), ("o", ("br", br, h, m), srcs[br])):
                    chunk = ("big", W_BR + 4 * br + 2 * h + (what == "o"))
                    w = K.weights(chunk, KD, 512)
                    K.wait_weights(pe, chunk)
                    if what == "o" and h == 0 and m == 0:
                        if br == 0:
                            K.wait_taken(pe, ("oT", KD - 1))
                        if br == 1:
                            K.wait_taken(pe, ("yT", KD - 1))
                        if br == 2:
                            pe.wait_ge(S["uT_ready"], 1)
                    K.wait_bank(pe, name)
                    for k in range(KD):
                        mm = nc.tensor.matmul(K.bank(name)[:, 0:TOK], w[:, k, m * P:(m + 1) * P], src[:, k, :],
                                              start=k == 0, stop=k == KD - 1)
                    K.full(mm)
                if (br, h, m) in LN_AFTER:
                    name = (LN_AFTER[br, h, m], 0)
                    K.wait_bank(pe, name)
                    if name[0] == "mu":
                        pe.wait_ge(S["u_conv_done"], KD)
                    for k in range(KD):
                        if name[0] == "var":
                            pe.wait_ge(S["squares"], k + 1)
                        mm = nc.tensor.matmul(K.bank(name)[:, 0:UOUT], K.ones, (uc if name[0] == "mu" else squ)[:, k, :],
                                              start=k == 0, stop=k == KD - 1)
                    K.full(mm)
            for h in range(2):
                w = K.weights(("big", W_OUT + h), KD, 512)
                K.wait_weights(pe, ("big", W_OUT + h))
                for t in range(T):
                    pe.wait_ge(S["merged"], 16)
                    K.wait_bank(pe, ("out", h, t))
                    for k in range(KD):
                        mm = nc.tensor.matmul(K.bank(("out", h, t))[:, :], merged[:, k, t * P:(t + 1) * P], w[:, k, :],
                                              start=k == 0, stop=k == KD - 1)
                    K.full(mm)

        @block.vector
        def _(dve):
            for t in range(T):
                nc.vector.tensor_tensor(y[:, t, :], y[:, t, :], z[:, t, :], ALU.mult).then_inc(S["y_ready"], 1)
            dve.wait_ge(S["stats_sq"], 6)
            nc.vector.tensor_scalar(st[:, 24:27], st[:, 24:27], 1.0 / D, EPS, ALU.mult, ALU.add).then_inc(S["stats_var"], 1)
            dve.wait_ge(S["stats_sqrt"], 2)
            dve.wait_ge(S["dve_step"], steps(nc.vector.reciprocal(st[:, 27:30], st[:, 27:30])))
            dve.wait_ge(S["y_ready"], 3)
            for t in range(T):
                nc.vector.tensor_scalar(y[:, t, :], y[:, t, :], st[:, 27 + t:28 + t], None, ALU.mult).then_inc(S["yn_ready"], 1)

            def convolution():
                for m in range(0, KD, 2):
                    yield from taps(K, dve, uc, uin, V_UW, V_UB, CW, UOUT, KD, "u_conv_done", (m, m + 1))

            conv = convolution()
            per_block = -(-CW * KD // BRANCH_ORDER.index((1, 1, 0)))
            for i, (br, h, m) in enumerate(BRANCH_ORDER):
                for _ in range(per_block):
                    next(conv, None)
                mo = merged[:, 4 * h + m, :]
                name = ("br", br, h, m)
                K.wait_full(dve, name)
                K.wait_taken(dve, ("gate", br, h, m))
                b = K.bank(name)[:, 0:TOK]
                if br == 0:
                    K.took(nc.vector.tensor_tensor(mo, b, gs[:, i % 2, :], ALU.mult), name)
                else:
                    n = i - 8
                    if n >= 2:
                        dve.wait_ge(S["merged"], n - 1)
                    K.took(nc.vector.tensor_tensor(tmp[:, i % 2, 0:TOK], b, gs[:, i % 2, :], ALU.mult), name)
                    K.wait_taken(dve, name)
                    if br == 2:
                        dve.wait_ge(S["merged"], n - 7)
                    nc.vector.tensor_tensor(mo, mo, tmp[:, i % 2, 0:TOK], ALU.add).then_inc(S["merged"], 1)
                if (br, h, m) in LN_AFTER:
                    K.wait_taken(dve, (LN_AFTER[br, h, m], 0))
                    if LN_AFTER[br, h, m] == "mu":
                        nc.vector.tensor_tensor(uc, uc, mean.unsqueeze(1).to_broadcast([P, KD, UOUT]), ALU.subtract)\
                            .then_inc(S["uc_ready"], 1)
                    else:
                        dve.wait_ge(S["dve_step"], steps(nc.vector.reciprocal(std, std)))
                        dve.wait_ge(S["squares"], KD)
                        nc.vector.tensor_tensor(uc, uc, std.unsqueeze(1).to_broadcast([P, KD, UOUT]), ALU.mult)\
                            .then_inc(S["ln_ready"], 1)
            dve.wait_ge(S["loads3"], 48)
            for h in range(2):
                for t in range(T):
                    i = T * h + t
                    if i >= 2:
                        dve.wait_ge(S["x_added"], i - 1)
                    else:
                        dve.wait_ge(S["merged"], 16)
                    K.wait_full(dve, ("out", h, t))
                    K.took(nc.vector.tensor_tensor(tmp[:, i % 2, :], K.bank(("out", h, t))[:, :], gt[:, min(t, 1), h * 512:(h + 1) * 512],
                                                   ALU.mult), ("out", h, t))
                    K.wait_taken(dve, ("out", h, t))
                    xv = K.x[:, t, h * 512:(h + 1) * 512]
                    nc.vector.tensor_tensor(xv, xv, tmp[:, i % 2, :], ALU.add).then_inc(S["x_added"], 1)


U = 8
TRIPS = SLOTS // (2 * U)
B_ROUTE = CHUNK


def experts(K, l):
    nc, S, io, G = K.nc, K.S, K.io, K.G
    o = B_ROUTE
    gw, ei = K.at(o, T * SLOTS), K.at(o + 384, T * SLOTS).bitcast(U32)
    g2 = K.at(o + 768, 2, D)
    qT = K.at(o + 2816, 16, TOK)
    keys = K.at(o + 8960, 2, P)
    s = K.at(o + 9216, 2, 16 * NKEYS)
    cand = K.at(o + 13312, PH, 256)
    mrow, srow, sq = K.at(o + 15360, 2, D), K.at(o + 17408, 2, D), K.at(o + 19456, D)
    acc, junk = K.at(o + 15360, D), K.at(o + 16384, D)
    hot = K.at(o + 17408, SLOTS, TOPK)
    o2 = o + 20480
    v1 = K.at(o2, 16, TOPK)
    x1 = K.at(o2 + 256, 16, TOPK).bitcast(U32)
    f1 = K.at(o2 + 512, 16, TOPK)
    v2 = K.at(o2 + 768, PH, TOPK)
    x2 = K.at(o2 + 896, PH, TOPK).bitcast(U32)
    hi, lo = K.at(o2 + 1024, SLOTS).bitcast(U32), K.at(o2 + 1152, SLOTS).bitcast(U32)
    hf, lf = K.at(o2 + 1280, SLOTS), K.at(o2 + 1408, SLOTS)
    e1, e2 = K.at(o2 + 1536, SLOTS), K.at(o2 + 1664, SLOTS)
    ex, sm = K.at(o2 + 1792, PH, TOPK), K.at(o2 + 1920, PH)
    o3 = o2 + 1936
    stage = K.at(o3, 2, U).bitcast(U32)
    dots, gel, wgt, gws = [K.at(o3 + 16 + 16 * i, 2, U) for i in range(4)]
    tick = K.at(o3 + 80, 1 + 2 * U)
    rows = K.arena[:, 0:U * 2 * D].rearrange("p (u n) -> p u n", u=U)
    steps = K.dve_steps
    with nc.Block() as block:
        @block.sync
        def _(sp):
            for v, dst in ((4, mrow), (3, srow)):
                sp.dma_start(dst, spread(io, v)).then_inc(S["loads3"], 16)
            K.load_weights(sp, l, len(K.chunks))
            sp.dma_start(keys, io["keysT"][bass.ds(l, 1)].rearrange("a p n -> p (a n)").rearrange("p (d n) -> p d n", d=2)).then_inc(S["key_loads"], 16)
            sp.dma_start(g2, spread(io, 5)).then_inc(S["key_loads"], 16)

        @block.gpsimd
        def _(pool):
            def pass_wait(n):
                nc.gpsimd.tensor_tensor(tick[:, 1 + n:2 + n], tick[:, 0:1], tick[:, 0:1], ALU.add)

            nc.gpsimd.memset(tick[:, 0:1], 0.0).then_inc(S["pool_step"], 1)
            pool.wait_ge(S["pool_step"], 1)
            K.wait_full(pool, ("pq", 15))
            for t in range(T):
                pool.wait_ge(S["routed"], t + 1)
                with pool.Fori(0, TRIPS) as i:
                    for r in range(2):
                        nc.gpsimd.tensor_copy(stage[:, r, :], ei[:, bass.ds(i * (2 * U) + (t * SLOTS + r * U), U)])\
                            .then_inc(S["staged"], 1)
                        for k in range(U):
                            if k == 0:
                                pool.wait_ge(S["staged"], i * 2 + (2 * t * TRIPS + r + 1))
                            pool.wait_ge(S["slot_done"], i * (2 * U) + (t * SLOTS + r * U + k + 1))
                            pass_wait(r * U + k)
                            nc.gpsimd.indirect_dma_start(rows[:, k, :], None, io["experts"],
                                                         bass.IndirectOffsetOnAxis(ap=stage[:, r, k:k + 1], axis=0))\
                                .then_inc(K.gathered[k], 16)

        @block.scalar
        def _(act):
            norm_act_stats(K, act, sq, 4, 2)
            norm_act_take(K, act, "n2")
            for c in range(4):
                K.wait_full(act, ("pq0", c))
                K.took(nc.scalar.copy(qT[:, 4 * c:4 * c + 4, 0:P],
                                      K.bank(("pq0", c))[:, :].rearrange("p (k n) -> p k n", k=4)), ("pq0", c))

            def scores(t):
                for c in range(4):
                    K.wait_full(act, ("ps", t, c))
                    K.took(nc.scalar.copy(s[:, t % 2, c * 512:(c + 1) * 512], K.bank(("ps", t, c))[:, :]), ("ps", t, c))

            def soft(t):
                act.wait_ge(S["soft_in"], t + 1)
                nc.scalar.activation(ex, ex, ACT.Exp).then_inc(S["soft_exp"], 1)

            scores(0)
            for m in range(16):
                K.wait_full(act, ("pq", m))
                K.took(nc.scalar.copy(qT[:, m, P:TOK], K.bank(("pq", m))[:, 0:2 * P]), ("pq", m))
            scores(1)
            act.wait_ge(S["s_read"], 1)
            scores(2)
            for t in range(T):
                soft(t)
                act.wait_ge(S["gates_ready"], t + 1)
                with act.Fori(0, TRIPS) as i:
                    nc.scalar.copy(gws.rearrange("p a b -> p (a b)"), gw[:, bass.ds(i * (2 * U) + t * SLOTS, 2 * U)])\
                        .then_inc(S["gw_staged"], 1)
                    act.wait_ge(S["gw_staged"], i + (t * TRIPS + 1))
                    for n in range(2 * U):
                        r, k = n // U, n % U
                        act.wait_ge(S["dot_done"], i * (2 * U) + (t * SLOTS + n + 1))
                        nc.scalar.activation(gel[:, r, k:k + 1], dots[:, r, k:k + 1], ACT.Gelu).then_inc(S["gelu_done"], 1)
                        act.wait_ge(S["gelu_done"], i * (2 * U) + (t * SLOTS + n + 1))
                        nc.scalar.activation(wgt[:, r, k:k + 1], gel[:, r, k:k + 1], ACT.Copy,
                                             scale=gws[:, r, k:k + 1]).then_inc(S["weight_done"], 1)
                    act.wait_ge(S["weight_done"], i * (2 * U) + (t * SLOTS + 2 * U))

        @block.tensor
        def _(pe):
            norm_pe(K, pe, "n2", 1)

            def scores(t):
                for c in range(4):
                    K.wait_bank(pe, ("ps", t, c))
                    for j in range(4):
                        m = 4 * c + j
                        mm = nc.tensor.matmul(K.bank(("ps", t, c))[:, j * P:(j + 1) * P], qT[:, m, t * P:(t + 1) * P],
                                              keys[:, m % 2, :], start=True, stop=True)
                    K.full(mm)

            K.wait_taken(pe, ("n2", 0, 1))
            for c in range(4):
                chunk = ("big", W_PQ + c)
                wt = K.weights(chunk, KD, 512)
                K.wait_weights(pe, chunk)
                K.wait_bank(pe, ("pq0", c))
                for j in range(4):
                    for k in range(KD):
                        mm = nc.tensor.matmul(K.bank(("pq0", c))[:, j * P:(j + 1) * P], wt[:, k, j * P:(j + 1) * P],
                                              K.hT[:, k, 0:P], start=k == 0, stop=k == KD - 1)
                K.full(mm)
            pe.wait_ge(S["key_loads"], 32)
            K.wait_taken(pe, ("pq0", 3))
            scores(0)
            K.wait_taken(pe, ("n2", 2, 1))
            for m in range(16):
                wt = K.weights(("big", W_PQ + m // 4), KD, 512)
                K.wait_bank(pe, ("pq", m))
                for k in range(KD):
                    mm = nc.tensor.matmul(K.bank(("pq", m))[:, 0:2 * P], wt[:, k, (m % 4) * P:(m % 4 + 1) * P],
                                          K.hT[:, k, P:TOK], start=k == 0, stop=k == KD - 1)
                K.full(mm)
            K.wait_taken(pe, ("pq", 15))
            scores(1)
            scores(2)

        @block.vector
        def _(dve):
            norm_stats_dve(K, dve, 4, 2)
            dve.wait_ge(S["loads3"], 80)
            norm_apply_dve(K, dve, mrow, srow, 4)
            dve.wait_ge(S["h_ready"], 6)

            def top16(src, vals, idx, ms):
                for m in ms:
                    k = steps(nc.vector.max(out=vals[:, m, 0:8], in_=src[:, m, :]))
                dve.wait_ge(S["dve_step"], k)
                for m in ms:
                    k = steps(nc.vector.max_index(idx[:, m, 0:8], vals[:, m, 0:8], src[:, m, :]))
                dve.wait_ge(S["dve_step"], k)
                for m in ms:
                    k = steps(nc.vector.match_replace(out=src[:, m, :], in_to_replace=vals[:, m, 0:8],
                                                      in_values=src[:, m, :], imm_value=NEG))
                dve.wait_ge(S["dve_step"], k)
                for m in ms:
                    k = steps(nc.vector.max(out=vals[:, m, 8:16], in_=src[:, m, :]))
                dve.wait_ge(S["dve_step"], k)
                for m in ms:
                    k = steps(nc.vector.max_index(idx[:, m, 8:16], vals[:, m, 8:16], src[:, m, :]))
                dve.wait_ge(S["dve_step"], k)

            def chosen(places, ids, out):
                iota = K.C[:, C_IOTA:C_IOTA + TOPK].unsqueeze(1).to_broadcast([P, SLOTS, TOPK])
                k = steps(nc.vector.tensor_tensor(hot, places.unsqueeze(2).to_broadcast([P, SLOTS, TOPK]), iota, ALU.is_equal))
                dve.wait_ge(S["dve_step"], k)
                for h in range(PH):
                    hv = hot[:, h * TOPK:(h + 1) * TOPK, :]
                    k = steps(nc.vector.tensor_tensor(hv, hv, ids[:, 2 * h, :].unsqueeze(1).to_broadcast([P, TOPK, TOPK]), ALU.mult))
                dve.wait_ge(S["dve_step"], k)
                return steps(nc.vector.tensor_reduce(out, hot, AX.X, ALU.add))

            def route_keys(t, half):
                K.wait_taken(dve, ("ps", t, 2 * half + 1))
                sv = s[:, t % 2, :].rearrange("p (m n) -> p m n", m=16)
                top16(sv, v1, x1, range(8 * half, 8 * half + 8))
                if half:
                    nc.vector.tensor_copy(f1, x1).then_inc(S["s_read"], 1)

            def route_experts(t):
                for h in range(PH):
                    k = steps(nc.vector.tensor_tensor(
                        cand[:, h, :].rearrange("p (a b) -> p a b", a=TOPK),
                        v1[:, 2 * h, :].unsqueeze(2).to_broadcast([P, TOPK, TOPK]),
                        v1[:, 2 * h + 1, :].unsqueeze(1).to_broadcast([P, TOPK, TOPK]), ALU.add))
                dve.wait_ge(S["dve_step"], k)
                top16(cand, v2, x2, range(PH))
                nc.vector.tensor_tensor(ex, v2, v2[:, :, 0:1].to_broadcast([P, PH, TOPK]), ALU.subtract).then_inc(S["soft_in"], 1)
                xf = x2.rearrange("p a b -> p (a b)")
                steps(nc.vector.tensor_scalar(hi, xf, 4, None, ALU.logical_shift_right))
                k = steps(nc.vector.tensor_scalar(lo, xf, 15, None, ALU.bitwise_and))
                dve.wait_ge(S["dve_step"], k)
                steps(nc.vector.tensor_copy(hf, hi))
                k = steps(nc.vector.tensor_copy(lf, lo))
                dve.wait_ge(S["dve_step"], k)
                dve.wait_ge(S["s_read"], t + 1)
                k = chosen(hf, f1, e1)
                dve.wait_ge(S["dve_step"], k)
                k = chosen(lf, f1[:, 1:16, :], e2)
                dve.wait_ge(S["dve_step"], k)
                k = steps(nc.vector.scalar_tensor_tensor(out=e1, in0=e1, scalar=float(NKEYS), in1=e2, op0=ALU.mult, op1=ALU.add))
                dve.wait_ge(S["dve_step"], k)
                k = steps(nc.vector.tensor_scalar(e1, e1, K.row[:, R_BASE:R_BASE + 1], None, ALU.add))
                dve.wait_ge(S["dve_step"], k)
                nc.vector.tensor_copy(ei[:, t * SLOTS:(t + 1) * SLOTS], e1).then_inc(S["routed"], 1)
                dve.wait_ge(S["routed"], t + 1)

            def route_gates(t):
                dve.wait_ge(S["soft_exp"], t + 1)
                k = steps(nc.vector.tensor_reduce(sm, ex, AX.X, ALU.add))
                dve.wait_ge(S["dve_step"], k)
                k = steps(nc.vector.reciprocal(sm, sm))
                dve.wait_ge(S["dve_step"], k)
                nc.vector.tensor_tensor(gw[:, t * SLOTS:(t + 1) * SLOTS].rearrange("p (a b) -> p a b", a=PH), ex,
                                        sm.unsqueeze(2).to_broadcast([P, PH, TOPK]), ALU.mult).then_inc(S["gates_ready"], 1)
                dve.wait_ge(S["gates_ready"], t + 1)

            def dot(t, i, n):
                r, k = n // U, n % U
                dve.wait_ge(K.gathered[k], (l * (2 * T * TRIPS) + i * 2) * 16 + 16 * (2 * t * TRIPS + r + 1))
                if n:
                    dve.wait_ge(S["dot_done"], i * (2 * U) + (t * SLOTS + n))
                nc.vector.tensor_tensor_reduce(out=junk, in0=rows[:, k, 0:D], in1=K.hn[:, t, :], scale=1.0, scalar=0.0,
                                               op0=ALU.mult, op1=ALU.add, accum_out=dots[:, r, k:k + 1]).then_inc(S["dot_done"], 1)

            def add(t, i, n):
                r, k = n // U, n % U
                dve.wait_ge(S["weight_done"], i * (2 * U) + (t * SLOTS + n + 1))
                dve.wait_ge(S["slot_done"], i * (2 * U) + (t * SLOTS + n + U))
                nc.vector.scalar_tensor_tensor(out=acc, in0=rows[:, k, D:2 * D], scalar=wgt[:, r, k:k + 1], in1=acc,
                                               op0=ALU.mult, op1=ALU.add).then_inc(S["slot_done"], 1)

            def slots(t, first, last):
                with dve.Fori(first, last) as i:
                    for n in range(2 * U):
                        dot(t, i, n)
                        if n >= 2:
                            add(t, i, n - 2)
                    dve.wait_ge(S["dot_done"], i * (2 * U) + (t * SLOTS + 2 * U))
                    add(t, i, 2 * U - 2)
                    add(t, i, 2 * U - 1)

            dve.wait_ge(S["stats_sq"], 9)
            nc.vector.memset(acc, 0.0).then_inc(S["slot_done"], U)
            route_keys(0, 0)
            route_keys(0, 1)
            route_experts(0)
            route_gates(0)
            dve.wait_ge(S["key_loads"], 32)
            for t in range(T):
                if t < T - 1:
                    slots(t, 0, 2)
                    route_keys(t + 1, 0)
                    slots(t, 2, 4)
                    route_keys(t + 1, 1)
                    slots(t, 4, 6)
                    route_experts(t + 1)
                    slots(t, 6, TRIPS)
                else:
                    slots(t, 0, TRIPS)
                dve.wait_ge(S["slot_done"], (t + 1) * SLOTS + U)
                k = steps(nc.vector.tensor_tensor(junk, acc, g2[:, min(t, 1), :], ALU.mult))
                dve.wait_ge(S["dve_step"], k)
                k = steps(nc.vector.tensor_tensor(K.x[:, t, :], K.x[:, t, :], junk, ALU.add))
                if t < T - 1:
                    k = steps(nc.vector.memset(acc, 0.0))
                    dve.wait_ge(S["dve_step"], k)
                    route_gates(t + 1)


def trunk_kernel(nc, io):
    K = Kernel(nc, io)
    S = K.S
    with nc.Block() as block:
        @block.sync
        def _(sp):
            sp.dma_start(K.x[:, :, :], io["x"].rearrange("(t p) n -> p t n", p=P)).then_inc(S["loads"], 16)
            sp.dma_start(K.C[:, :], io["consts"]).then_inc(S["loads"], 16)
            sp.wait_ge(S["loads"], 32)
    nc.all_engine_barrier(sems_to_clear=S.span())
    with nc.Fori(0, DEPTH) as l:
        K.loaded, K.pe_at, K.takes = 0, 0, {"act": 0, "dve": 0}
        modulate_and_norm(K, l)
        project_in(K, l)
        attention(K, l)
        ssd(K, l)
        branches(K, l)
        experts(K, l)
        assert K.loaded == len(K.chunks) and K.pe_at == len(K.G.names)
        nc.all_engine_barrier(sems_to_clear=S.span())
    final_norm(K)


def final_norm(K):
    nc, S, io = K.nc, K.S, K.io
    gf = K.at(0, D)
    sq = K.at(D, D)
    y = K.at(2 * D, T, D)
    K.dve_steps = Steps(S["dve_step"])
    with nc.Block() as block:
        @block.sync
        def _(sp):
            sp.dma_start(gf, io["g_final"].to_broadcast([P, D])).then_inc(S["loads"], 16)
            for t in range(T):
                sp.wait_ge(S["h_ready"], t + 1)
                sp.dma_start(io["y"][t * P:(t + 1) * P, :], y[:, t, :]).then_inc(S["stores"], 16)
            sp.wait_ge(S["stores"], 16 * T)

        @block.scalar
        def _(act):
            norm_act_stats(K, act, sq, 0)

        @block.vector
        def _(dve):
            norm_stats_dve(K, dve, 0)
            dve.wait_ge(S["loads"], 16)
            for t in range(T):
                nc.vector.scalar_tensor_tensor(out=y[:, t, :], in0=K.x[:, t, :], scalar=K.st[:, 3 + t:4 + t], in1=gf,
                                               op0=ALU.mult, op1=ALU.mult).then_inc(S["h_ready"], 1)


def kernel(**a):
    import concourse.bacc as _bacc
    from concourse.bass_utils import run_bass_kernel_spmd as _run

    a = {k: np.ascontiguousarray(v) for k, v in a.items()}
    L = DEPTH

    def big(w, cols):
        w = w[:, :, cols]
        n = w.shape[2] // 512
        return w.reshape(L, KD, P, n, 512).transpose(0, 3, 2, 1, 4).reshape(L, n, P, CHUNK)

    OCQ, OKR, OZ, OX, ODT, OG = 0, 512, 544, 1568, 3104, 3136
    w_in = a["w_in"]
    glu = big(w_in, slice(OG, OG + 2 * D))
    parts = [big(a["w_mod"], slice(None)), big(w_in, slice(0, 512)), big(w_in, slice(OZ, OZ + D)),
             big(w_in, slice(OX, OX + XC * P)), glu[:, 2:3], glu[:, 0:1], glu[:, 3:4], glu[:, 1:2]]
    gate = big(a["w_gate"], slice(None))
    for b, name in enumerate(("w_attn_out", "w_ssd_out", "w_cv_pw2")):
        w = big(a[name], slice(None))
        for h in range(2):
            parts += [gate[:, 2 * b + h:2 * b + h + 1], w[:, h:h + 1]]
    parts += [big(a["w_out"], slice(None)), big(a["w_peer_q"], slice(None))]
    w_big = np.concatenate(parts, axis=1)
    small = np.concatenate([w_in[:, :, OKR:OZ], w_in[:, :, ODT:OG]], axis=2)
    w_small = small.reshape(L, 1, KD, P, 64).transpose(0, 1, 3, 2, 4).reshape(L, 1, P, KD * 64)
    w_uq = a["w_uq"].reshape(L, KQ, P, 3, 512).transpose(0, 3, 2, 1, 4).reshape(L, 3, P, KQ * 512)
    w_ukv = a["w_ukv"].reshape(L, 1, P, 2048)

    def cols(v):
        return v.reshape(L, -1, P).transpose(0, 2, 1)

    def taps(w, n):
        return w.reshape(L, w.shape[1], n, P).transpose(0, 3, 2, 1).reshape(L, P, -1)

    vecs = np.concatenate([cols(a["g_q_norm"]), taps(a["ssd_conv_w"], XC), cols(a["ssd_conv_b"]), taps(a["cv_dw_w"], KD),
                           cols(a["cv_dw_b"]), cols(a["cv_ln_g"]), cols(a["cv_ln_b"]), cols(a["g_ssd_norm"]),
                           cols(a["b_gate"])], axis=2)
    base = (np.arange(L) * NKEYS * NKEYS).astype(np.float32)[:, None]
    rows = np.concatenate([a["g_kv_norm"], a["ssd_dt_bias"].reshape(L, 32), a["ssd_a_log"].reshape(L, 32), a["ssd_d"], base], axis=1)

    consts = np.zeros((P, N_CONST), np.float32)
    i = np.arange(P)
    consts[:, C_ID:C_ID + P] = np.eye(P)
    consts[:, C_TF:C_TF + P] = i[:, None] <= i[None, :]
    consts[:, C_TB:C_TB + P] = i[:, None] >= i[None, :]
    consts[:, C_ONE:C_ONE + P] = 1.0
    inv = (np.float32(10000.0) ** (-np.arange(8, dtype=np.float32) / np.float32(8))).astype(np.float32)
    for t in range(2):
        tok = t * P + i
        for ax, pos in enumerate((tok // 64, tok % 64)):
            ang = pos.astype(np.float32)[:, None] * inv
            for half in range(2):
                c = 32 * t + 16 * ax + 8 * half
                consts[:, C_RC + c:C_RC + c + 8] = np.cos(ang)
                consts[:, C_RS + c:C_RS + c + 8] = np.sin(ang) if half else -np.sin(ang)
    consts[:, C_IOTA:C_IOTA + TOPK] = np.arange(TOPK)
    consts[:, C_EPS] = EPS
    consts[:, C_EPS + 1] = 1.0

    h0 = np.stack([a["state_ssd_fwd"][0], a["state_ssd_bwd"][0]], axis=1)
    arrays = {
        "x": np.concatenate([a["x_prompt"][0], a["x_sample"][0]], axis=0),
        "c_rows": np.stack([a["c_ctx"].reshape(KD, P), a["c"][0].reshape(KD, P)], axis=2).transpose(1, 0, 2).reshape(P, KD * 2),
        "w_big": w_big, "w_small": w_small, "w_uq": w_uq, "w_ukv": w_ukv,
        "mod_rows": np.concatenate([a["b_mod"], a["g_norm1"], a["g_norm2"]], axis=1),
        "vecs": vecs, "rows": rows, "consts": consts,
        "cache_kvT": a["cache_ckv"][0].transpose(0, 2, 1), "cache_krT": a["cache_krope"][0].transpose(0, 2, 1),
        "h0T": h0.transpose(0, 4, 1, 2, 3).reshape(L, P, 2 * D),
        "keysT": a["peer_keys"].transpose(0, 3, 1, 2).reshape(L, P, 2 * P),
        "experts": np.concatenate([a["peer_u"], a["peer_v"]], axis=2).reshape(L * NKEYS * NKEYS, 2 * D),
        "g_final": a["g_final"].reshape(1, D),
    }
    outs = {"y": (TOK, D), "new_ckv": (L, P, KV_RANK), "new_krope": (L, P, ROPE), "new_state": (L, 2, P, D)}
    nc = _bacc.Bacc("TRN2", target_bir_lowering=False, num_devices=1)
    io = {}
    for name in arrays:
        arrays[name] = np.ascontiguousarray(arrays[name])
        io[name] = nc.dram_tensor(f"in_{name}_dram", arrays[name].shape, F32, kind="ExternalInput").ap()
    for name, shape in outs.items():
        io[name] = nc.dram_tensor(f"out_{name}_dram", shape, F32, kind="ExternalOutput").ap()
    io["mod_scratch"] = nc.dram_tensor("mod_scratch", (2, 6 * D), F32, kind="Internal").ap()
    trunk_kernel(nc, io)
    r = _run(nc, [{f"in_{k}_dram": v for k, v in arrays.items()}], core_ids=[0]).results[0]
    y = r["out_y_dram"]
    s = r["out_new_state_dram"].reshape(L, 2, P, SH, SP_).transpose(1, 0, 3, 4, 2)[:, None]
    s = np.ascontiguousarray(s)
    return (y[None, :P], y[None, P:], r["out_new_ckv_dram"][None], r["out_new_krope_dram"][None], s[0], s[1])
```

```python
import math
from contextlib import ExitStack

import numpy as np

import concourse.bass as bass
from concourse import mybir

ALU = mybir.AluOpType
ACT = mybir.ActivationFunctionType
AX = mybir.AxisListType
F32 = mybir.dt.float32
U32 = mybir.dt.uint32

P = 128
D = 1024
KD = D // P
DEPTH = 2
T = 3
TOK = T * P
EPS = 1e-6
HEADS, NOPE, ROPE, VD = 16, 64, 32, 64
QK = NOPE + ROPE
Q_RANK, KV_RANK = 384, 128
KQ = Q_RANK // P
SH, SP_, SN, SG = 16, 64, 128, 2
HG = SH // SG
XC = 12
CW, XW = 31, 5
PH, TOPK, NKEYS = 8, 16, 128
SLOTS = PH * TOPK
NEG = -3.0e38

XIN, XOUT = 2 + P + 2 + 2 * P + 2, P + 2 + 2 * P
UIN, UOUT = 15 + P + 15 + 2 * P + 15, P + 15 + 2 * P

RING = 3
CHUNK = KD * 512
W_MOD, W_CQKV, W_Z, W_XBC, W_GLU = 0, 12, 13, 15, 18
W_BR, W_OUT, W_PQ = 22, 34, 36
N_BIG = 40

V_GQ, V_CW, V_CB, V_UW, V_UB, V_LG, V_LB, V_GS, V_BG = 0, 3, 63, 75, 323, 331, 339, 347, 355
N_VEC = 379
R_GKV, R_DTB, R_ALOG, R_D = 0, 128, 160, 192
R_BASE = 208
N_ROW = 209
C_ID, C_TF, C_TB, C_ONE, C_RC, C_RS, C_IOTA, C_EPS = 0, 128, 256, 384, 512, 576, 640, 656
N_CONST = 658

BANKS = 8


class Groups:

    def __init__(self):
        self.names, self.by = [], []

    def add(self, name, by):
        self.names.append(name)
        self.by.append(by)

    def number(self, name):
        return self.names.index(name)

    def bank(self, name):
        return self.number(name) % BANKS

    def taken(self, name):
        n = self.number(name)
        return self.by[n], sum(b == self.by[n] for b in self.by[:n + 1])

    def reused(self, name):
        n = self.number(name) - BANKS
        return self.names[n] if n >= 0 else None


FIRST = 4
LATE_ATTENTION, LATE_SSD, LATE_BRANCHES = [4, 5], [6, 7, 8, 9, 10], [11]
LATE_UNITS = [1, 4, 7, 10]


def first_norm_order():
    tiles = [(t, c) for t in range(T) for c in range(2)]
    for n in range(FIRST - 1):
        yield "mod", n
    for i in tiles[:5]:
        yield "n1", i
    yield "mod", FIRST - 1
    yield "n1", tiles[5]


SSD_UNITS = [(0, 0), (0, 1), (1, 0), (2, 1), (2, 0), (1, 1)]


def attention_order():
    for i in range(HEADS + 3):
        if i < HEADS:
            yield "K", i
            yield "QT", i
        if 0 <= i - 1 < HEADS:
            yield "SA", i - 1
            yield "SB", i - 1
        if 0 <= i - 2 < HEADS:
            yield "PA", i - 2
            yield "PB", i - 2
        if 0 <= i - 3 < HEADS:
            yield "PV", i - 3


def ssd_order():
    units = [(t, d, g) for t, d in SSD_UNITS for g in range(SG)]
    for i in range(len(units) + 1):
        if i < len(units):
            yield "AB0", units[i]
            yield "AB1", units[i]
        if i in LATE_UNITS:
            yield "MOD", LATE_SSD[1 + LATE_UNITS.index(i)]
        if i >= 1:
            u = units[i - 1]
            yield "YD", u
            if u[0] > 0:
                yield "YO", u
            if state_of(u):
                yield "CS", u


def state_of(u):
    t, d, _ = u
    return t == 0 or (t, d) in ((1, 0), (2, 1))


BRANCH_ORDER = [(b, h, m) for b in range(3) for h in range(2) for m in range(4)]
LN_AFTER = {(1, 1, 0): "mu", (1, 1, 2): "var"}


def plan():
    G = Groups()
    chunks, last = [], {}

    def use(chunk, group):
        if chunk not in last:
            chunks.append(chunk)
        last[chunk] = group

    def modulation(n, by):
        G.add(("mod", n), by)
        use(("big", W_MOD + n), ("mod", n))

    for what, i in first_norm_order():
        if what == "mod":
            modulation(i, "dve")
        else:
            G.add(("n1", *i), "act" if i[1] == 0 else "norm")
    G.add(("modT", 0), "dve")
    for t in range(T):
        G.add(("cqkv", t), "act")
        use(("big", W_CQKV), ("cqkv", t))
    for t in range(T):
        G.add(("krdt", t), "act")
        use(("small", 0), ("krdt", t))
    for h in range(2):
        for t in range(T):
            G.add(("z", h, t), "act")
            use(("big", W_Z + h), ("z", h, t))
    for m in range(XC):
        G.add(("xbc", m), "act")
        use(("big", W_XBC + m // 4), ("xbc", m))
    for m in range(KD):
        G.add(("gt", m), "act")
        use(("big", W_GLU + 2 * (m // 4)), ("gt", m))
        G.add(("a", m), "dve")
        use(("big", W_GLU + 2 * (m // 4) + 1), ("a", m))
    for n in LATE_ATTENTION[:1]:
        modulation(n, "act")
    for t in range(T):
        G.add(("cqT", t), "act")
    G.add(("kvT", 0), "act")
    G.add(("krT", 0), "dve")
    for n in LATE_ATTENTION[1:]:
        modulation(n, "act")
    for c in range(3):
        for t in range(T):
            G.add(("q", c, t), "act")
            use(("uq", c), ("q", c, t))
    for kt in range(4):
        for c in range(2):
            G.add(("v", kt, c), "dve")
            use(("ukv", 0), ("v", kt, c))
    for step, h in attention_order():
        G.add((step, h), {"K": "dve", "QT": "act", "SA": "act", "SB": "act", "PA": "dve", "PB": "act",
                          "PV": "dve"}[step])
        if step == "K":
            use(("ukv", 0), (step, h))
    for n in LATE_SSD[:1]:
        modulation(n, "act")
    G.add(("cum", 0), "dve")
    for t in range(T):
        for c in range(2):
            G.add(("xs", t, c), "act")
    G.add(("bt", 0), "act")
    G.add(("bt", 1), "act")
    G.add(("cb", 0), "dve")
    G.add(("cb", 1), "dve")
    for step, u in ssd_order():
        if step == "MOD":
            modulation(u, "act")
        else:
            G.add((step, u), "dve")
    for k in range(KD):
        G.add(("oT", k), "act")
    for n in LATE_BRANCHES:
        modulation(n, "act")
    for b, h, m in BRANCH_ORDER:
        if (b, h, m) == (1, 0, 0):
            for k in range(KD):
                G.add(("yT", k), "act")
        G.add(("gate", b, h, m), "act")
        use(("big", W_BR + 4 * b + 2 * h), ("gate", b, h, m))
        G.add(("br", b, h, m), "dve")
        use(("big", W_BR + 4 * b + 2 * h + 1), ("br", b, h, m))
        if (b, h, m) in LN_AFTER:
            G.add((LN_AFTER[b, h, m], 0), "act")
    for t in range(T):
        for h in range(2):
            G.add(("out", h, t), "dve")
            use(("big", W_OUT + h), ("out", h, t))
    for c in range(2):
        G.add(("n2", 0, c), "act")
    for half in range(2):
        for c in (2 * half, 2 * half + 1):
            G.add(("pq0", c), "act")
            use(("big", W_PQ + c), ("pq0", c))
        for c in (2 * half, 2 * half + 1):
            G.add(("ps", 0, c), "act")
    for t in (1, 2):
        for c in range(2):
            G.add(("n2", t, c), "act")
    for m in range(16):
        G.add(("pq", m), "act" if m < 8 else "dve")
        use(("big", W_PQ + m // 4), ("pq", m))
    for t in (1, 2):
        for c in range(4):
            G.add(("ps", t, c), "dve")
    return G, chunks, last


class Sems:

    def __init__(self, nc, names):
        self.all = {n: nc.alloc_semaphore(n) for n in names}

    def __getitem__(self, name):
        return self.all[name]

    def span(self):
        ids = [s.num for s in self.all.values()]
        assert max(ids) - min(ids) + 1 == len(ids)
        return range(min(ids), max(ids) + 1)


class Steps:

    def __init__(self, sem):
        self.sem, self.n = sem, 0

    def __call__(self, ins):
        ins.then_inc(self.sem, 1)
        self.n += 1
        return self.n


class Kernel:

    def __init__(self, nc, io):
        self.nc, self.io = nc, io
        self.G, self.chunks, self.last = plan()
        self.C = nc.alloc_sbuf_tensor("consts", [P, N_CONST], F32)
        self.x = nc.alloc_sbuf_tensor("x", [P, T, D], F32)
        self.hT = nc.alloc_sbuf_tensor("hT", [P, KD, TOK], F32)
        self.hn = nc.alloc_sbuf_tensor("hn", [P, T, D], F32)
        self.vec = nc.alloc_sbuf_tensor("vec", [P, N_VEC], F32)
        self.row = nc.alloc_sbuf_tensor("row", [P, N_ROW], F32)
        self.st = nc.alloc_sbuf_tensor("st", [P, 64], F32)
        self.pool_n = 30300
        self.ring0 = RING * CHUNK
        self.arena = nc.alloc_sbuf_tensor("arena", [P, self.ring0 + self.pool_n], F32)
        self.ps = [nc.alloc_psum_tensor(f"bank{b}", [P, 512], F32) for b in range(BANKS)]
        self.cT = self.st[:, 40:40 + 2 * KD].rearrange("p (k c) -> p k c", k=KD)
        self.ident = self.C[:, C_ID:C_ID + P]
        self.ones = self.C[:, C_ONE:C_ONE + P]
        self.tri = [self.C[:, C_TF:C_TF + P], self.C[:, C_TB:C_TB + P]]
        self.eps = self.C[:, C_EPS:C_EPS + 1]
        self.one = self.C[:, C_EPS + 1:C_EPS + 2]
        gather = [f"rows_landed{s}" for s in range(8)]
        self.gathered = [nc.alloc_semaphore(n) for n in gather]
        self.S = Sems(nc, NAMES + [f"weights_landed{i}" for i in range(RING)])

    def at(self, off, *shape):
        n = int(np.prod(shape))
        assert off + n <= self.pool_n, (off, shape)
        v = self.arena[:, self.ring0 + off:self.ring0 + off + n]
        if len(shape) == 2:
            v = v.rearrange("p (a b) -> p a b", a=shape[0])
        if len(shape) == 3:
            v = v.rearrange("p (a b c) -> p a b c", a=shape[0], b=shape[1])
        return v

    def late_rows(self):
        return [self.at(self.pool_n - 1536 + 512 * i, 512)[0:2, :] for i in range(3)]

    def h2(self, t):
        return self.at(25600, D) if t == 0 else self.hn[:, t, :]

    def place(self, chunk):
        n = self.chunks.index(chunk)
        return (n % RING if n < len(self.chunks) - 1 else RING) * CHUNK

    def weights(self, chunk, k, n):
        s = self.place(chunk)
        return self.arena[:, s:s + k * n].rearrange("p (k n) -> p k n", k=k)

    def load_weights(self, sp, l, upto):
        io = self.io
        while self.loaded < min(upto, len(self.chunks)):
            n = self.loaded
            kind, i = self.chunks[n]
            if n >= RING and n < len(self.chunks) - 1:
                sp.wait_ge(self.S["psum_full"], self.G.number(self.last[self.chunks[n - RING]]) + 1)
            src, width = {
                "big": (io["w_big"], CHUNK), "small": (io["w_small"], KD * 64),
                "uq": (io["w_uq"], KQ * 512), "ukv": (io["w_ukv"], 2048)}[kind]
            s = self.place(self.chunks[n])
            src = src[bass.ds(l, 1), i].rearrange("a p n -> p (a n)")
            landed = self.S["last_weights_landed" if n == len(self.chunks) - 1 else f"weights_landed{n % RING}"]
            sp.dma_start(self.arena[:, s:s + width], src).then_inc(landed, 16)
            self.loaded += 1

    def wait_weights(self, pe, chunk):
        n = self.chunks.index(chunk)
        if n == len(self.chunks) - 1:
            pe.wait_ge(self.S["last_weights_landed"], 16)
        else:
            pe.wait_ge(self.S[f"weights_landed{n % RING}"], 16 * (n // RING + 1))

    def bank(self, name):
        return self.ps[self.G.bank(name)]

    def wait_bank(self, pe, name):
        assert self.G.names[self.pe_at] == name, (self.G.names[self.pe_at], name)
        self.pe_at += 1
        old = self.G.reused(name)
        if old is not None:
            self.wait_taken(pe, old)

    def wait_taken(self, eng, name):
        by, n = self.G.taken(name)
        eng.wait_ge(self.S[by + "_took"], n)

    def wait_full(self, eng, name):
        eng.wait_ge(self.S["psum_full"], self.G.number(name) + 1)

    def full(self, ins):
        ins.then_inc(self.S["psum_full"], 1)

    def took(self, ins, name):
        by, n = self.G.taken(name)
        self.takes[by] += 1
        assert self.takes[by] == n, (name, self.takes[by], n)
        ins.then_inc(self.S[by + "_took"], 1)


NAMES = ["psum_full", "act_took", "dve_took", "norm_took", "dve_step", "act_step", "pool_step", "loads", "loads2",
         "loads3", "stores", "mod_scaled", "mod_stored", "stats_sq", "stats_var", "stats_sqrt", "h_ready",
         "x_conv_done", "x_silu", "u_conv_done", "cq_ready", "kv_ready", "kr_ready", "q_roped", "rope_rows",
         "max_ready", "dt_abs", "dt_ln", "cum_ready", "exps_ready", "exp_seg", "m_ready", "xdt_ready", "xw_ready",
         "y_ready", "yn_ready", "uc_ready", "sq_ready", "ln_std", "ln_ready", "uT_ready", "merged", "x_added",
         "soft_in", "soft_exp", "routed", "staged", "dot_done", "gelu_done", "weight_done", "slot_done", "pads",
         "gw_staged", "ctx_loads", "silu_c", "skip_ready", "last_weights_landed", "norm_rows", "mod_done",
         "bias_landed", "mod_biased", "lat_var", "dta_ready", "key_loads", "gates_ready", "squares"]


def modulate_and_norm(K, l):
    nc, S, io = K.nc, K.S, K.io
    rows = K.at(0, FIRST * 512)
    brow = K.at(2048, FIRST * 512)
    grow = K.at(4096, D)
    sq = K.at(5120, D)
    mcol = K.at(6144, 2 * KD, 2)
    steps = Steps(S["dve_step"])
    K.dve_steps = steps
    with nc.Block() as block:
        @block.sync
        def _(sp):
            sp.dma_start(K.cT.rearrange("p a b -> p (a b)"), io["c_rows"]).then_inc(S["ctx_loads"], 16)
            K.load_weights(sp, l, 2)
            sp.dma_start(brow[0:2, :], io["mod_rows"][bass.ds(l, 1), 0:FIRST * 512].to_broadcast([2, FIRST * 512])).then_inc(S["loads"], 16)
            sp.dma_start(grow[0:2, :], io["mod_rows"][bass.ds(l, 1), 6 * D:7 * D].to_broadcast([2, D])).then_inc(S["loads"], 16)
            K.load_weights(sp, l, FIRST)
            sp.dma_start(K.vec[:, :], io["vecs"][bass.ds(l, 1)].rearrange("a p n -> p (a n)")).then_inc(S["loads2"], 16)
            sp.dma_start(K.row[:, :], io["rows"][bass.ds(l, 1), :].to_broadcast([P, N_ROW])).then_inc(S["loads2"], 16)
            K.load_weights(sp, l, FIRST + 3)

        @block.scalar
        def _(act):
            act.wait_ge(S["ctx_loads"], 16)
            nc.scalar.activation(K.cT, K.cT, ACT.Silu).then_inc(S["silu_c"], 1)
            norm_act_stats(K, act, sq, 0)
            K.wait_taken(act, ("modT", 0))
            for t in range(T):
                name = ("n1", t, 0)
                K.wait_full(act, name)
                for k in range(4):
                    ins = nc.scalar.activation(K.hT[:, k, t * P:(t + 1) * P], K.bank(name)[:, k * P:(k + 1) * P], ACT.Identity,
                                               scale=mcol[:, KD + k, min(t, 1):min(t, 1) + 1], bias=mcol[:, k, min(t, 1):min(t, 1) + 1])
                K.took(ins, name)

        @block.tensor
        def _(pe):
            pe.wait_ge(S["silu_c"], 1)
            for what, i in first_norm_order():
                if what == "mod":
                    modulation_pe(K, pe, i)
                else:
                    t, c = i
                    pe.wait_ge(S["h_ready"], t + 1)
                    K.wait_bank(pe, ("n1", t, c))
                    for k in range(4):
                        f = (4 * c + k) * P
                        mm = nc.tensor.transpose(K.bank(("n1", t, c))[:, k * P:(k + 1) * P], K.hn[:, t, f:f + P], K.ident)
                    K.full(mm)
            pe.wait_ge(S["mod_scaled"], 2)
            K.wait_bank(pe, ("modT", 0))
            for j in range(2 * KD):
                mm = nc.tensor.transpose(K.bank(("modT", 0))[:, 2 * j:2 * j + 2], rows[0:2, j * P:(j + 1) * P],
                                         K.C[0:2, C_ID:C_ID + 2])
            K.full(mm)

        @block.vector
        def _(dve):
            norm_stats_dve(K, dve, 0)
            for t in range(T):
                nc.vector.tensor_scalar(K.hn[:, t, :], K.x[:, t, :], K.st[:, 3 + t:4 + t], None, ALU.mult).then_inc(S["h_ready"], 1)
            dve.wait_ge(S["loads"], 32)
            for n in range(FIRST):
                r = rows[0:2, n * 512:(n + 1) * 512]
                K.wait_full(dve, ("mod", n))
                for j in range(4):
                    ins = nc.vector.tensor_copy(r[:, j * P:(j + 1) * P], K.bank(("mod", n))[32 * j:32 * j + 2, 0:P])
                K.took(ins, ("mod", n))
                K.wait_taken(dve, ("mod", n))
                k = steps(nc.vector.tensor_tensor(r, r, brow[0:2, n * 512:(n + 1) * 512], ALU.add))
                dve.wait_ge(S["dve_step"], k)
                if n >= 2:
                    nc.vector.scalar_tensor_tensor(out=r, in0=r, scalar=1.0, in1=grow[0:2, (n - 2) * 512:(n - 1) * 512],
                                                   op0=ALU.add, op1=ALU.mult).then_inc(S["mod_scaled"], 1)
            K.wait_full(dve, ("modT", 0))
            K.took(nc.vector.tensor_copy(mcol.rearrange("p a b -> p (a b)"), K.bank(("modT", 0))[:, 0:4 * KD]), ("modT", 0))
            K.wait_taken(dve, ("modT", 0))
            for t in range(T):
                name = ("n1", t, 1)
                K.wait_full(dve, name)
                for k in range(4):
                    ins = nc.vector.tensor_scalar(K.hT[:, 4 + k, t * P:(t + 1) * P], K.bank(name)[:, k * P:(k + 1) * P],
                                                  mcol[:, KD + 4 + k, min(t, 1):min(t, 1) + 1],
                                                  mcol[:, 4 + k, min(t, 1):min(t, 1) + 1], ALU.mult, ALU.add)
                K.took(ins, name)


def modulation_pe(K, pe, n):
    w = K.weights(("big", W_MOD + n), KD, 512)
    K.wait_weights(pe, ("big", W_MOD + n))
    K.wait_bank(pe, ("mod", n))
    for k in range(KD):
        for j in range(4):
            mm = K.nc.tensor.matmul(K.bank(("mod", n))[32 * j:32 * j + 2, 0:P], K.cT[:, k, :], w[:, k, j * P:(j + 1) * P],
                                    start=k == 0, stop=k == KD - 1)
    K.full(mm)


class LateModulation:

    def __init__(self, K, r, bias, gain):
        self.K, self.r, self.bias, self.gain = K, r, bias, gain

    @staticmethod
    def scales(n):
        return n in (8, 9)

    def load_bias(self, sp, l, n):
        K = self.K
        if n > FIRST:
            sp.wait_ge(K.S["mod_done"], n - FIRST)
        rows = K.io["mod_rows"]
        sp.dma_start(self.bias, rows[bass.ds(l, 1), n * 512:(n + 1) * 512].to_broadcast([2, 512])).then_inc(K.S["bias_landed"], 16)
        if self.scales(n):
            g = 7 * D + (n - 8) * 512
            sp.dma_start(self.gain, rows[bass.ds(l, 1), g:g + 512].to_broadcast([2, 512])).then_inc(K.S["bias_landed"], 16)

    def store(self, sp, n):
        K = self.K
        sp.wait_ge(K.S["mod_done"], n - FIRST + 1)
        sp.dma_start(K.io["mod_scratch"][:, n * 512:(n + 1) * 512], self.r).then_inc(K.S["mod_stored"], 16)

    def take(self, act, n):
        K = self.K
        K.wait_full(act, ("mod", n))
        if n > FIRST:
            act.wait_ge(K.S["mod_stored"], 16 * (n - FIRST))
        for j in range(4):
            piece, b = self.r[:, j * P:(j + 1) * P], K.bank(("mod", n))[32 * j:32 * j + 2, 0:P]
            ins = K.nc.scalar.activation(piece, b, ACT.Copy, bias=float(self.scales(n)))
        K.took(ins, ("mod", n))

    def finish(self, pool, n):
        K = self.K
        K.wait_taken(pool, ("mod", n))
        pool.wait_ge(K.S["bias_landed"], 16 * sum(1 + self.scales(i) for i in range(FIRST, n + 1)))
        ins = K.nc.gpsimd.tensor_tensor(self.r, self.r, self.bias, ALU.add)
        if self.scales(n):
            ins.then_inc(K.S["mod_biased"], 1)
            pool.wait_ge(K.S["mod_biased"], n - 7)
            ins = K.nc.gpsimd.tensor_tensor(self.r, self.r, self.gain, ALU.mult)
        ins.then_inc(K.S["mod_done"], 1)


def spread(io, v):
    t = io["mod_scratch"]
    return bass.AP(tensor=t.tensor, offset=v * D, ap=[[0, P], [6 * D, 2], [1, D]])


def norm_act_stats(K, act, sq, which, before=0):
    nc, S = K.nc, K.S
    for t in range(T):
        if t:
            act.wait_ge(S["stats_sq"], 3 * before + t)
        nc.scalar.activation(sq, K.x[:, t, :], ACT.Square,
                             accum_out=K.st[:, 8 * which + t:8 * which + t + 1]).then_inc(S["stats_sq"], 1)
    act.wait_ge(S["stats_var"], before + 1)
    nc.scalar.activation(K.st[:, 8 * which + 3:8 * which + 6], K.st[:, 8 * which:8 * which + 3],
                         ACT.Sqrt).then_inc(S["stats_sqrt"], 1)


def norm_stats_dve(K, dve, which, before=0):
    nc, S = K.nc, K.S
    s = K.st[:, 8 * which:8 * which + 3]
    dve.wait_ge(S["stats_sq"], 3 * before + 3)
    nc.vector.tensor_scalar(s, s, 1.0 / D, EPS, ALU.mult, ALU.add).then_inc(S["stats_var"], 1)
    dve.wait_ge(S["stats_sqrt"], before + 1)
    r = K.st[:, 8 * which + 3:8 * which + 6]
    dve.wait_ge(S["dve_step"], K.dve_steps(nc.vector.reciprocal(r, r)))


def norm_apply_dve(K, dve, mrow, srow, tiles):
    nc, S = K.nc, K.S
    for t in tiles:
        c = min(t, 1)
        n = K.dve_steps(nc.vector.scalar_tensor_tensor(out=K.h2(t), in0=K.x[:, t, :], scalar=K.st[:, 35 + t:36 + t],
                                                       in1=mrow[:, c, :], op0=ALU.mult, op1=ALU.mult))
        dve.wait_ge(S["dve_step"], n)
        nc.vector.tensor_tensor(K.h2(t), K.h2(t), srow[:, c, :], ALU.add).then_inc(S["h_ready"], 1)


def norm2_act_take(K, act, tiles):
    for t in tiles:
        for c in range(2):
            name = ("n2", t, c)
            K.wait_full(act, name)
            K.took(K.nc.scalar.copy(K.hT[:, 4 * c:4 * c + 4, t * P:(t + 1) * P],
                                    K.bank(name)[:, :].rearrange("p (k n) -> p k n", k=4)), name)


def norm2_pe(K, pe, tiles):
    for t in tiles:
        pe.wait_ge(K.S["h_ready"], T + t + 1)
        for c in range(2):
            name = ("n2", t, c)
            K.wait_bank(pe, name)
            for k in range(4):
                f = (4 * c + k) * P
                mm = K.nc.tensor.transpose(K.bank(name)[:, k * P:(k + 1) * P], K.h2(t)[:, f:f + P], K.ident)
            K.full(mm)


A_CQKV, A_KRDT, A_Z, A_XBC, A_UIN = 0, 1536, 1728, 4800, 9432
A_FREE = A_UIN + KD * UIN


def tokens(t, pad):
    a = [0, P + pad, 2 * P + pad][t]
    return slice(a, a + P)


def taps(K, dve, dst, src, wcol, bcol, width, length, m, done, ms):
    nc, S = K.nc, K.S
    before = {}
    for k in range(width):
        for j in ms:
            o, i = dst[:, j, :], src[:, j % m, k:k + length]
            w = K.vec[:, wcol + width * j + k:wcol + width * j + k + 1]
            if k:
                dve.wait_ge(S["dve_step"], before[j])
                ins = nc.vector.scalar_tensor_tensor(out=o, in0=i, scalar=w, in1=o, op0=ALU.mult, op1=ALU.add)
            elif bcol is None:
                ins = nc.vector.tensor_scalar(o, i, w, None, ALU.mult)
            else:
                ins = nc.vector.tensor_scalar(o, i, w, K.vec[:, bcol + j:bcol + j + 1], ALU.mult, ALU.add)
            if k < width - 1:
                before[j] = K.dve_steps(ins)
            else:
                ins.then_inc(S[done], 1)
            yield


def project_in(K, l):
    nc, S, io = K.nc, K.S, K.io
    cqkv, krdt, z = K.at(A_CQKV, T, 512), K.at(A_KRDT, T, 64), K.at(A_Z, T, D)
    xbc, uin = K.at(A_XBC, XC, XOUT), K.at(A_UIN, KD, UIN)
    xin = K.at(A_FREE, 6, XIN)
    sig = K.at(A_FREE + 6 * XIN, 2, TOK)
    steps = K.dve_steps
    with nc.Block() as block:
        @block.sync
        def _(sp):
            K.load_weights(sp, l, K.chunks.index(("big", W_GLU + 3)) + 4)

        @block.gpsimd
        def _(pool):
            for a, b in ((0, 2), (2 + P, 4 + P), (XIN - 2, XIN)):
                nc.gpsimd.memset(xin[:, :, a:b], 0.0)
            for a, b in ((0, 15), (15 + P, 30 + P), (UIN - 15, UIN)):
                last = nc.gpsimd.memset(uin[:, :, a:b], 0.0)
            last.then_inc(S["pads"], 1)

        @block.tensor
        def _(pe):
            def by_tokens(name, chunk, width, t):
                w = K.weights(chunk, KD, width)
                K.wait_bank(pe, name)
                for k in range(KD):
                    mm = nc.tensor.matmul(K.bank(name)[:, 0:width], K.hT[:, k, t * P:(t + 1) * P], w[:, k, :],
                                          start=k == 0, stop=k == KD - 1)
                K.full(mm)

            def by_features(name, chunk, m):
                w = K.weights(chunk, KD, 512)
                K.wait_weights(pe, chunk)
                K.wait_bank(pe, name)
                for k in range(KD):
                    mm = nc.tensor.matmul(K.bank(name)[:, 0:TOK], w[:, k, m * P:(m + 1) * P], K.hT[:, k, :],
                                          start=k == 0, stop=k == KD - 1)
                K.full(mm)

            K.wait_weights(pe, ("big", W_CQKV))
            for t in range(T):
                by_tokens(("cqkv", t), ("big", W_CQKV), 512, t)
            K.wait_weights(pe, ("small", 0))
            for t in range(T):
                by_tokens(("krdt", t), ("small", 0), 64, t)
            for h in range(2):
                K.wait_weights(pe, ("big", W_Z + h))
                for t in range(T):
                    by_tokens(("z", h, t), ("big", W_Z + h), 512, t)
            for m in range(XC):
                by_features(("xbc", m), ("big", W_XBC + m // 4), m % 4)
            for m in range(KD):
                by_features(("gt", m), ("big", W_GLU + 2 * (m // 4)), m % 4)
                by_features(("a", m), ("big", W_GLU + 2 * (m // 4) + 1), m % 4)

        @block.scalar
        def _(act):
            for t in range(T):
                K.wait_full(act, ("cqkv", t))
                K.took(nc.scalar.copy(cqkv[:, t, :], K.bank(("cqkv", t))[:, :]), ("cqkv", t))
            for t in range(T):
                K.wait_full(act, ("krdt", t))
                K.took(nc.scalar.copy(krdt[:, t, :], K.bank(("krdt", t))[:, 0:64]), ("krdt", t))
            for h in range(2):
                for t in range(T):
                    K.wait_full(act, ("z", h, t))
                    K.took(nc.scalar.activation(z[:, t, h * 512:(h + 1) * 512], K.bank(("z", h, t))[:, :],
                                                ACT.Silu), ("z", h, t))
            act.wait_ge(S["pads"], 1)

            def silu(m):
                act.wait_ge(S["x_conv_done"], m + 1)
                nc.scalar.activation(xbc[:, m, :], xbc[:, m, :], ACT.Silu,
                                     bias=K.vec[:, V_CB + m:V_CB + m + 1]).then_inc(S["x_silu"], 1)

            for m in range(XC):
                if m >= 6:
                    act.wait_ge(S["x_conv_done"], m - 5)
                K.wait_full(act, ("xbc", m))
                b = K.bank(("xbc", m))
                nc.scalar.copy(xin[:, m % 6, 2:2 + P], b[:, 0:P])
                K.took(nc.scalar.copy(xin[:, m % 6, 4 + P:4 + 3 * P], b[:, P:3 * P]), ("xbc", m))
                if m >= 3:
                    silu(m - 3)
            for m in range(XC - 3, XC):
                silu(m)
            for m in range(KD):
                if m >= 2:
                    K.wait_taken(act, ("a", m - 2))
                K.wait_full(act, ("gt", m))
                K.took(nc.scalar.activation(sig[:, m % 2, :], K.bank(("gt", m))[:, 0:TOK], ACT.Sigmoid), ("gt", m))

        @block.vector
        def _(dve):
            dve.wait_ge(S["pads"], 1)
            dve.wait_ge(S["loads2"], 32)
            for m in range(0, XC, 2):
                K.wait_taken(dve, ("xbc", m + 1))
                for _ in taps(K, dve, xbc, xin, V_CW, None, XW, XOUT, 6, "x_conv_done", (m, m + 1)):
                    pass
            for m in range(0, KD, 2):
                for j in (m, m + 1):
                    K.wait_full(dve, ("a", j))
                    K.wait_taken(dve, ("gt", j))
                    b = K.bank(("a", j))
                    steps(nc.vector.tensor_tensor(uin[:, j, 15:15 + P], b[:, 0:P], sig[:, j % 2, 0:P], ALU.mult))
                    K.took(nc.vector.tensor_tensor(uin[:, j, 30 + P:30 + 3 * P], b[:, P:3 * P], sig[:, j % 2, P:3 * P],
                                                   ALU.mult), ("a", j))


def attention(K, l):
    nc, S, io = K.nc, K.S, K.io
    cqkv, krdt = K.at(A_CQKV, T, 512), K.at(A_KRDT, T, 64)
    o = K.hn
    off = A_FREE
    cqT = K.at(off, KQ, TOK)
    ckvT = K.at(off + 1152, 512)
    krT = K.at(off + 1664, 512)
    q = K.at(off + 2176, T, HEADS * QK)
    v = K.at(off + 6784, 4, HEADS * VD)
    kT = K.at(off + 10880, 4, 512)
    qT = K.at(off + 12928, 2, TOK)
    pr = K.at(off + 13696, 2, 896)
    pT = K.at(off + 15504, 2, 896)
    krp = K.at(off + 10880, T, QK)
    tmp = K.at(off + 10880 + T * QK, HEADS * ROPE)
    mx = K.at(off + 15488, 2, 4)
    sm = K.at(off + 15496, 2, 4)
    steps = K.dve_steps
    st = K.st
    SC = QK ** -0.5
    late = LateModulation(K, *[K.hn[0:2, 0, 512 * i:512 * (i + 1)] for i in range(2)], K.hn[0:2, 1, 0:512])
    with nc.Block() as block:
        @block.gpsimd
        def _(pool):
            for n in LATE_ATTENTION:
                late.finish(pool, n)

        @block.sync
        def _(sp):
            late.load_bias(sp, l, LATE_ATTENTION[0])
            sp.dma_start(ckvT[:, P:2 * P], io["cache_kvT"][bass.ds(l, 1)].rearrange("a p n -> p (a n)")).then_inc(S["ctx_loads"], 16)
            sp.dma_start(krT[NOPE:QK, P:2 * P], io["cache_krT"][bass.ds(l, 1)].rearrange("a p n -> p (a n)")).then_inc(S["ctx_loads"], 16)
            sp.dma_start(io["new_krope"][bass.ds(l, 1)].rearrange("a p n -> p (a n)"), krdt[:, 0, 0:ROPE]).then_inc(S["stores"], 16)
            sp.wait_ge(S["kv_ready"], 3)
            sp.dma_start(io["new_ckv"][bass.ds(l, 1)].rearrange("a p n -> p (a n)"), cqkv[:, 0, Q_RANK:512]).then_inc(S["stores"], 16)
            for n in LATE_ATTENTION:
                K.load_weights(sp, l, K.chunks.index(("big", W_MOD + n)) + 4)
                late.store(sp, n)
                if n < LATE_ATTENTION[-1]:
                    late.load_bias(sp, l, n + 1)
            K.load_weights(sp, l, K.chunks.index(("ukv", 0)) + 4)
            sp.wait_ge(S["stores"], 32)

        @block.scalar
        def _(act):
            for t in range(T):
                nc.scalar.activation(q[:, t, 0:Q_RANK], cqkv[:, t, 0:Q_RANK], ACT.Square,
                                     accum_out=st[:, 16 + t:17 + t])
                nc.scalar.activation(q[:, t, Q_RANK:512], cqkv[:, t, Q_RANK:512], ACT.Square,
                                     accum_out=st[:, 19 + t:20 + t]).then_inc(S["sq_ready"], 1)
            act.wait_ge(S["lat_var"], 1)
            nc.scalar.activation(st[:, 16:22], st[:, 16:22], ACT.Sqrt).then_inc(S["ln_std"], 1)
            act.wait_ge(S["loads2"], 32)
            late.take(act, LATE_ATTENTION[0])
            for t in range(T):
                K.wait_full(act, ("cqT", t))
                for k in range(KQ):
                    ins = nc.scalar.activation(cqT[:, k, t * P:(t + 1) * P], K.bank(("cqT", t))[:, k * P:(k + 1) * P],
                                               ACT.Copy, scale=K.vec[:, V_GQ + k:V_GQ + k + 1])
                K.took(ins, ("cqT", t))
            K.wait_full(act, ("kvT", 0))
            b = K.bank(("kvT", 0))
            nc.scalar.copy(ckvT[:, 0:P], b[:, 0:P])
            K.took(nc.scalar.copy(ckvT[:, 2 * P:4 * P], b[:, P:3 * P]), ("kvT", 0))
            for n in LATE_ATTENTION[1:]:
                late.take(act, n)
            for c in range(3):
                for t in range(T):
                    K.wait_full(act, ("q", c, t))
                    K.took(nc.scalar.copy(q[:, t, c * 512:(c + 1) * 512], K.bank(("q", c, t))[:, :]), ("q", c, t))
            for step, h in attention_order():
                if step == "QT":
                    if h >= 2:
                        K.wait_full(act, ("SB", h - 2))
                    K.wait_full(act, (step, h))
                    K.took(nc.scalar.copy(qT[0:QK, h % 2, :], K.bank((step, h))[0:QK, 0:TOK]), (step, h))
                if step == "SB":
                    act.wait_ge(S["max_ready"], h + 1)
                    if h >= 2:
                        K.wait_full(act, ("PB", h - 2))
                        K.wait_taken(act, ("PV", h - 2))
                    pieces = [("SA", 0, P, 0), ("SA", P, 512, 1), ("SB", 0, TOK, 2)]
                    for name, a, z, j in pieces:
                        d = 0 if name == "SA" else 512
                        ins = nc.scalar.activation(pr[:, h % 2, d + a:d + z], K.bank((name, h))[:, a:z], ACT.Exp,
                                                   bias=mx[:, h % 2, j:j + 1], scale=SC,
                                                   accum_out=sm[:, h % 2, j:j + 1])
                        if j:
                            K.took(ins, (name, h))
                if step == "PB":
                    if h >= 2:
                        K.wait_full(act, ("PV", h - 2))
                    K.wait_full(act, (step, h))
                    K.took(nc.scalar.copy(pT[:, h % 2, 512:896], K.bank((step, h))[:, 0:TOK]), (step, h))

        @block.tensor
        def _(pe):
            modulation_pe(K, pe, LATE_ATTENTION[0])
            for t in range(T):
                pe.wait_ge(S["cq_ready"], t + 1)
                K.wait_bank(pe, ("cqT", t))
                for k in range(KQ):
                    mm = nc.tensor.transpose(K.bank(("cqT", t))[:, k * P:(k + 1) * P], cqkv[:, t, k * P:(k + 1) * P], K.ident)
                K.full(mm)
            pe.wait_ge(S["kv_ready"], 3)
            K.wait_bank(pe, ("kvT", 0))
            for t in range(T):
                mm = nc.tensor.transpose(K.bank(("kvT", 0))[:, t * P:(t + 1) * P], cqkv[:, t, Q_RANK:512], K.ident)
            K.full(mm)
            pe.wait_ge(S["kr_ready"], 1)
            K.wait_bank(pe, ("krT", 0))
            for t in range(T):
                mm = nc.tensor.transpose(K.bank(("krT", 0))[0:QK, t * P:(t + 1) * P], krp[:, t, :], K.ident)
            K.full(mm)
            for n in LATE_ATTENTION[1:]:
                modulation_pe(K, pe, n)
            K.wait_taken(pe, ("cqT", 2))
            for c in range(3):
                w = K.weights(("uq", c), KQ, 512)
                K.wait_weights(pe, ("uq", c))
                for t in range(T):
                    K.wait_bank(pe, ("q", c, t))
                    for k in range(KQ):
                        mm = nc.tensor.matmul(K.bank(("q", c, t))[:, :], cqT[:, k, t * P:(t + 1) * P], w[:, k, :],
                                              start=k == 0, stop=k == KQ - 1)
                    K.full(mm)
            wv = K.weights(("ukv", 0), HEADS, P)
            K.wait_weights(pe, ("ukv", 0))
            pe.wait_ge(S["ctx_loads"], 48)
            K.wait_taken(pe, ("kvT", 0))
            for kt in range(4):
                for c in range(2):
                    K.wait_bank(pe, ("v", kt, c))
                    K.full(nc.tensor.matmul(K.bank(("v", kt, c))[:, :], ckvT[:, kt * P:(kt + 1) * P],
                                            wv[:, 8 * c:8 * c + 8, NOPE:P], start=True, stop=True))
            for step, h in attention_order():
                b = K.bank((step, h))
                if step == "K":
                    K.wait_bank(pe, (step, h))
                    K.full(nc.tensor.matmul(b[0:NOPE, :], wv[:, h, 0:NOPE], ckvT[:, :], start=True, stop=True))
                if step == "QT":
                    if h == 0:
                        pe.wait_ge(S["q_roped"], 2)
                        K.wait_taken(pe, ("q", 2, 2))
                    K.wait_bank(pe, (step, h))
                    for t in range(T):
                        mm = nc.tensor.transpose(b[0:QK, t * P:(t + 1) * P], q[:, t, h * QK:(h + 1) * QK], K.ident)
                    K.full(mm)
                if step == "SA":
                    K.wait_taken(pe, ("K", h))
                    K.wait_taken(pe, ("QT", h))
                    if h == 0:
                        pe.wait_ge(S["rope_rows"], 1)
                    K.wait_bank(pe, (step, h))
                    nc.tensor.matmul(b[:, 0:P], qT[0:QK, h % 2, 0:P], kT[0:QK, h % 4, 0:P], start=True, stop=True)
                    K.full(nc.tensor.matmul(b[:, P:512], qT[0:QK, h % 2, P:2 * P], kT[0:QK, h % 4, P:512],
                                            start=True, stop=True))
                if step == "SB":
                    K.wait_bank(pe, (step, h))
                    K.full(nc.tensor.matmul(b[:, 0:TOK], qT[0:QK, h % 2, 2 * P:3 * P], kT[0:QK, h % 4, P:512],
                                            start=True, stop=True))
                if step in ("PA", "PB"):
                    K.wait_taken(pe, ("SB", h))
                    K.wait_bank(pe, (step, h))
                    d = 0 if step == "PA" else 512
                    for j in range(4 if step == "PA" else 3):
                        mm = nc.tensor.transpose(b[:, j * P:(j + 1) * P], pr[:, h % 2, d + j * P:d + (j + 1) * P], K.ident)
                    K.full(mm)
                if step == "PV":
                    K.wait_taken(pe, ("PA", h))
                    K.wait_taken(pe, ("PB", h))
                    K.wait_bank(pe, (step, h))
                    vh = v[:, :, h * VD:(h + 1) * VD]
                    nc.tensor.matmul(b[:, 0:VD], pT[:, h % 2, 0:P], vh[:, 0, :], start=True, stop=True)
                    for t in (1, 2):
                        for j in range(3):
                            a = ((1 if t == 1 else 4) + j) * P
                            mm = nc.tensor.matmul(b[:, t * VD:(t + 1) * VD], pT[:, h % 2, a:a + P], vh[:, 1 + j, :],
                                                  start=j == 0, stop=j == 2)
                    K.full(mm)

        @block.vector
        def _(dve):
            dve.wait_ge(S["sq_ready"], 3)
            n = steps(nc.vector.tensor_scalar(st[:, 16:19], st[:, 16:19], 1.0 / Q_RANK, EPS, ALU.mult, ALU.add))
            nc.vector.tensor_scalar(st[:, 19:22], st[:, 19:22], 1.0 / KV_RANK, EPS, ALU.mult, ALU.add).then_inc(S["lat_var"], 1)
            dve.wait_ge(S["ln_std"], 1)
            dve.wait_ge(S["dve_step"], steps(nc.vector.reciprocal(st[:, 16:22], st[:, 16:22])))
            dve.wait_ge(S["loads2"], 32)
            for t in range(T):
                nc.vector.tensor_scalar(cqkv[:, t, 0:Q_RANK], cqkv[:, t, 0:Q_RANK], st[:, 16 + t:17 + t], None,
                                        ALU.mult).then_inc(S["cq_ready"], 1)
                nc.vector.scalar_tensor_tensor(out=cqkv[:, t, Q_RANK:512], in0=cqkv[:, t, Q_RANK:512],
                                               scalar=st[:, 19 + t:20 + t], in1=K.row[:, R_GKV:R_GKV + P],
                                               op0=ALU.mult, op1=ALU.mult).then_inc(S["kv_ready"], 1)

            def rope(src, dst, scratch, heads, t, last=None):
                C = K.C[:, C_RC + 32 * (t - 1):C_RC + 32 * t].rearrange("p (a b n) -> p a b n", a=2, b=2)
                Z = K.C[:, C_RS + 32 * (t - 1):C_RS + 32 * t].rearrange("p (a b n) -> p a b n", a=2, b=2)
                for b in range(2):
                    for a in range(2):
                        s0 = src[:, :, 16 * a + 8 * (1 - b):16 * a + 8 * (1 - b) + 8]
                        o0 = scratch[:, :, 16 * a + 8 * b:16 * a + 8 * b + 8]
                        z0 = Z[:, a, b, :].unsqueeze(1).to_broadcast([P, heads, 8])
                        n = steps(nc.vector.tensor_tensor(o0, s0, z0, ALU.mult))
                cc = K.C[:, C_RC + 32 * (t - 1):C_RC + 32 * t].unsqueeze(1).to_broadcast([P, heads, ROPE])
                dve.wait_ge(S["dve_step"], n)
                n = steps(nc.vector.tensor_tensor(dst, src, cc, ALU.mult))
                dve.wait_ge(S["dve_step"], n)
                ins = nc.vector.tensor_tensor(dst, dst, scratch, ALU.add)
                if last:
                    ins.then_inc(S[last], 1)
                else:
                    steps(ins)

            steps(nc.vector.memset(krp[:, :, 0:NOPE], 0.0))
            steps(nc.vector.tensor_copy(krp[:, 0, NOPE:QK], krdt[:, 0, 0:ROPE]))
            for t in (1, 2):
                rope(krdt[:, t:t + 1, 0:ROPE], krp[:, t:t + 1, NOPE:QK],
                     tmp[:, 32 * t:32 * t + 32].unsqueeze(1), 1, t, "kr_ready" if t == 2 else None)
            K.wait_full(dve, ("krT", 0))
            b = K.bank(("krT", 0))
            steps(nc.vector.tensor_copy(krT[NOPE:QK, 0:P], b[NOPE:QK, 0:P]))
            K.took(nc.vector.tensor_copy(krT[NOPE:QK, 2 * P:4 * P], b[NOPE:QK, P:3 * P]), ("krT", 0))
            for t in (1, 2):
                K.wait_taken(dve, ("q", 2, t))
                if t == 2:
                    dve.wait_ge(S["q_roped"], 1)
                qr = q[:, t, :].rearrange("p (h n) -> p h n", h=HEADS)[:, :, NOPE:QK]
                rope(qr, qr, tmp.rearrange("p (h n) -> p h n", h=HEADS), HEADS, t, "q_roped")
            dve.wait_ge(S["q_roped"], 2)
            dve.wait_ge(S["ctx_loads"], 48)
            K.wait_taken(dve, ("krT", 0))
            nc.vector.tensor_copy(kT[NOPE:QK, :, :], krT[NOPE:QK, :].unsqueeze(1).to_broadcast([ROPE, 4, 512]))\
                .then_inc(S["rope_rows"], 1)
            for kt in range(4):
                for c in range(2):
                    K.wait_full(dve, ("v", kt, c))
                    K.took(nc.vector.tensor_copy(v[:, kt, c * 512:(c + 1) * 512], K.bank(("v", kt, c))[:, :]), ("v", kt, c))
            for step, h in attention_order():
                b = K.bank((step, h))
                if step == "K":
                    if h >= 4:
                        K.wait_full(dve, ("SB", h - 4))
                    K.wait_full(dve, (step, h))
                    K.took(nc.vector.tensor_copy(kT[0:NOPE, h % 4, :], b[0:NOPE, :]), (step, h))
                if step == "SB":
                    K.wait_full(dve, ("SB", h))
                    if h >= 2:
                        K.wait_taken(dve, ("SB", h - 2))
                    sa = K.bank(("SA", h))
                    steps(nc.vector.reduce_max(mx[:, h % 2, 0:1], sa[:, 0:P], AX.X))
                    steps(nc.vector.reduce_max(mx[:, h % 2, 1:2], sa[:, P:512], AX.X))
                    n = steps(nc.vector.reduce_max(mx[:, h % 2, 2:3], b[:, 0:TOK], AX.X))
                    dve.wait_ge(S["dve_step"], n)
                    nc.vector.tensor_scalar(mx[:, h % 2, 0:3], mx[:, h % 2, 0:3], -SC, None, ALU.mult)\
                        .then_inc(S["max_ready"], 1)
                if step == "PA":
                    if h >= 2:
                        K.wait_full(dve, ("PV", h - 2))
                    K.wait_full(dve, (step, h))
                    K.took(nc.vector.tensor_copy(pT[:, h % 2, 0:512], b[:, :]), (step, h))
                if step == "PV":
                    K.wait_taken(dve, ("SB", h))
                    n = steps(nc.vector.reciprocal(sm[:, h % 2, 0:3], sm[:, h % 2, 0:3]))
                    dve.wait_ge(S["dve_step"], n)
                    if h == 0:
                        dve.wait_ge(S["mod_stored"], 16 * len(LATE_ATTENTION))
                    K.wait_full(dve, (step, h))
                    K.took(nc.vector.tensor_tensor(
                        o[:, :, h * VD:(h + 1) * VD], b[:, 0:T * VD].rearrange("p (t n) -> p t n", t=T),
                        sm[:, h % 2, 0:3].unsqueeze(2).to_broadcast([P, T, VD]), ALU.mult), (step, h))


def ssd(K, l):
    nc, S, io = K.nc, K.S, K.io
    krdt = K.at(A_KRDT, T, 64)
    xbc = K.at(A_XBC, XC, XOUT)
    off = A_FREE
    xs = K.at(off, T, D)
    bt = K.at(off + 3072, T, 2 * SN)
    cbm = K.at(off + 3840, 2, 6 * P)
    y = K.at(off + 5376, T, D)
    H = K.at(off + 8448, 2, D)
    xdt = K.at(off + 10496, 2, 512)
    xw = K.at(off + 11520, 512)
    seg = K.at(off + 12032, 2, 512)
    M = K.at(off + 13056, 2, 512)
    tmp = K.at(off + 14080, 512)
    sm = off + 14592
    raw, dt, aA, ab, acum, tot = [K.at(sm + 96 * i, 96) for i in range(6)]
    ea, dend, etot = [K.at(sm + 96 * i, 96) for i in range(6, 9)]
    A = K.at(A_CQKV, 32)
    outs = K.at(A_CQKV + 64, 2, 512)
    steps = K.dve_steps
    units = [(t, d, g) for t, d in SSD_UNITS for g in range(SG)]

    def heads(a, u):
        t, d, g = u
        c = 32 * t + 16 * d + 8 * g
        return a[:, c:c + 8]

    def spread8(a, u):
        return heads(a, u).unsqueeze(2).to_broadcast([P, HG, SP_])

    def h8(v):
        return v.rearrange("p (h n) -> p h n", h=HG)

    late = LateModulation(K, *K.late_rows())
    with nc.Block() as block:
        @block.gpsimd
        def _(pool):
            late.finish(pool, LATE_SSD[0])
            n_xw = skips = 0
            for step, u in ssd_order():
                if step == "MOD":
                    late.finish(pool, u)
                    continue
                t, d, g = u
                i = units.index(u)
                if step == "AB0":
                    if i == 0:
                        pool.wait_ge(S["dta_ready"], 1)
                    if i >= 2:
                        K.wait_full(pool, ("YD", units[i - 2]))
                        if n_xw:
                            pool.wait_ge(S["xw_ready"], n_xw)
                    K.wait_taken(pool, ("xs", t, 1))
                    nc.gpsimd.tensor_tensor(h8(xdt[:, i % 2, :]), h8(xs[:, t, g * 512:(g + 1) * 512]), spread8(dt, u),
                                            ALU.mult).then_inc(S["xdt_ready"], 1)
                if step == "AB1" and state_of(u):
                    prev = [w for w in units[:i] if state_of(w)]
                    if prev:
                        K.wait_full(pool, ("CS", prev[-1]))
                    else:
                        pool.wait_ge(S["exps_ready"], 1)
                    pool.wait_ge(S["xdt_ready"], i + 1)
                    nc.gpsimd.tensor_tensor(h8(xw), h8(xdt[:, i % 2, :]), spread8(dend, u), ALU.mult).then_inc(S["xw_ready"], 1)
                    n_xw += 1
                if step == "AB1" and skips <= t:
                    for j in range(skips, t + 1):
                        nc.gpsimd.tensor_tensor(
                            y[:, j, :].rearrange("p (h n) -> p h n", h=SH), xs[:, j, :].rearrange("p (h n) -> p h n", h=SH),
                            K.row[:, R_D:R_D + SH].unsqueeze(2).to_broadcast([P, SH, SP_]), ALU.mult).then_inc(S["skip_ready"], 1)
                    skips = t + 1

        @block.sync
        def _(sp):
            def modulation(n):
                K.load_weights(sp, l, K.chunks.index(("big", W_MOD + n)) + 4)
                late.store(sp, n)
                late.load_bias(sp, l, n + 1)

            late.load_bias(sp, l, LATE_SSD[0])
            sp.dma_start(H, io["h0T"][bass.ds(l, 1)].rearrange("a p n -> p (a n)").rearrange("p (d n) -> p d n", d=2)).then_inc(S["ctx_loads"], 16)
            modulation(LATE_SSD[0])
            for step, u in ssd_order():
                if step == "MOD":
                    modulation(u)
                if step == "CS" and u[0] == 0:
                    K.wait_taken(sp, ("CS", u))
                    dst = io["new_state"][bass.ds(l, 1), u[1]].rearrange("a p n -> p (a n)")[:, u[2] * 512:(u[2] + 1) * 512]
                    sp.dma_start(dst, outs[:, u[2], :]).then_inc(S["stores"], 16)
            sp.wait_ge(S["stores"], 32 + 64)

        @block.scalar
        def _(act):
            act.wait_ge(S["dt_abs"], 1)
            nc.scalar.activation(ab, ab, ACT.Exp, scale=-1.0).then_inc(S["act_step"], 1)
            nc.scalar.activation(A, K.row[:, R_ALOG:R_ALOG + 32], ACT.Exp).then_inc(S["act_step"], 1)
            act.wait_ge(S["act_step"], 1)
            nc.scalar.activation(ab, ab, ACT.Ln, bias=K.one).then_inc(S["dt_ln"], 1)
            late.take(act, LATE_SSD[0])
            for t in range(T):
                for c in range(2):
                    K.wait_full(act, ("xs", t, c))
                    K.took(nc.scalar.copy(xs[:, t, c * 512:(c + 1) * 512], K.bank(("xs", t, c))[:, :]), ("xs", t, c))
            for g in range(SG):
                K.wait_full(act, ("bt", g))
                K.took(nc.scalar.copy(bt[:, :, g * SN:(g + 1) * SN],
                                      K.bank(("bt", g))[:, 0:TOK].rearrange("p (t n) -> p t n", t=T)), ("bt", g))
            act.wait_ge(S["cum_ready"], 1)
            nc.scalar.activation(ea, acum, ACT.Exp)
            nc.scalar.activation(dend, dend, ACT.Exp)
            nc.scalar.activation(etot, tot, ACT.Exp).then_inc(S["exps_ready"], 1)
            for i in range(2 * len(units)):
                if i % 2 == 0 and i // 2 - 1 in LATE_UNITS:
                    late.take(act, LATE_SSD[1 + LATE_UNITS.index(i // 2 - 1)])
                K.wait_taken(act, (f"AB{i % 2}", units[i // 2]))
                if i >= 2:
                    act.wait_ge(S["m_ready"], i - 1)
                nc.scalar.activation(seg[:, i % 2, :], seg[:, i % 2, :], ACT.Exp).then_inc(S["exp_seg"], 1)

        @block.tensor
        def _(pe):
            modulation_pe(K, pe, LATE_SSD[0])
            pe.wait_ge(S["dta_ready"], 1)
            K.wait_bank(pe, ("cum", 0))
            b = K.bank(("cum", 0))
            for t in range(T):
                for d in range(2):
                    c = 32 * t + 16 * d
                    nc.tensor.matmul(b[:, c:c + 16], K.tri[d], aA[:, c:c + 16], start=True, stop=True)
            K.full(nc.tensor.matmul(b[:, 96:192], K.ones, aA, start=True, stop=True))
            for t in range(T):
                for c in range(2):
                    K.wait_bank(pe, ("xs", t, c))
                    for k in range(4):
                        mm = nc.tensor.transpose(K.bank(("xs", t, c))[:, k * P:(k + 1) * P],
                                                 xbc[:, 4 * c + k, tokens(t, 2)], K.ident)
                    K.full(mm)
            for g in range(SG):
                K.wait_bank(pe, ("bt", g))
                for t in range(T):
                    mm = nc.tensor.transpose(K.bank(("bt", g))[:, t * P:(t + 1) * P], xbc[:, 8 + g, tokens(t, 2)], K.ident)
                K.full(mm)
            for j in range(2):
                K.wait_bank(pe, ("cb", j))
                for i in range(4 * j, min(4 * j + 4, 6)):
                    t, g = i // 2, i % 2
                    mm = nc.tensor.matmul(K.bank(("cb", j))[:, (i % 4) * P:(i % 4 + 1) * P], xbc[:, 8 + g, tokens(t, 2)],
                                          xbc[:, 10 + g, tokens(t, 2)], start=True, stop=True)
                K.full(mm)
            n_xw = 0
            pe.wait_ge(S["ctx_loads"], 64)
            for step, u in ssd_order():
                if step == "MOD":
                    modulation_pe(K, pe, u)
                    continue
                t, d, g = u
                i = units.index(u)
                name = (step, u)
                b = K.bank(name)
                if step in ("AB0", "AB1"):
                    K.wait_bank(pe, name)
                    for j in range(4):
                        c = 32 * t + 16 * d + 8 * g + 4 * (step == "AB1") + j
                        mm = nc.tensor.matmul(b[:, j * P:(j + 1) * P], aA[:, c:c + 1].to_broadcast([P, P]), K.tri[d],
                                              start=True, stop=True)
                    K.full(mm)
                if step == "YD":
                    pe.wait_ge(S["xdt_ready"], i + 1)
                    K.wait_bank(pe, name)
                    for j in range(HG):
                        if j % 4 == 0:
                            pe.wait_ge(S["m_ready"], 2 * i + j // 4 + 1)
                        mm = nc.tensor.matmul(b[:, j * SP_:(j + 1) * SP_], M[:, j // 4, (j % 4) * P:(j % 4 + 1) * P],
                                              xdt[:, i % 2, j * SP_:(j + 1) * SP_], start=True, stop=True)
                    K.full(mm)
                if step == "YO":
                    if (t, d) in ((2, 0), (1, 1)):
                        K.wait_taken(pe, ("CS", (3 - t, d, g)))
                    K.wait_bank(pe, name)
                    K.full(nc.tensor.matmul(b[:, :], xbc[:, 10 + g, tokens(t, 2)], H[:, d, g * 512:(g + 1) * 512],
                                            start=True, stop=True))
                if step == "CS":
                    n_xw += 1
                    pe.wait_ge(S["xw_ready"], n_xw)
                    K.wait_bank(pe, name)
                    K.full(nc.tensor.matmul(b[:, :], bt[:, t, g * SN:(g + 1) * SN], xw, start=True, stop=True))

        @block.vector
        def _(dve):
            r3 = raw.rearrange("p (t n) -> p t n", t=T)
            n = steps(nc.vector.tensor_tensor(r3, krdt[:, :, 32:64],
                                              K.row[:, R_DTB:R_DTB + 32].unsqueeze(1).to_broadcast([P, T, 32]), ALU.add))
            dve.wait_ge(S["dve_step"], n)
            nc.vector.scalar_tensor_tensor(out=ab, in0=raw, scalar=-1.0, in1=raw, op0=ALU.mult, op1=ALU.max).then_inc(S["dt_abs"], 1)
            n = steps(nc.vector.tensor_scalar(dt, raw, 0.0, None, ALU.max))
            dve.wait_ge(S["dve_step"], n)
            dve.wait_ge(S["dt_ln"], 1)
            n = steps(nc.vector.tensor_tensor(dt, dt, ab, ALU.add))
            dve.wait_ge(S["dve_step"], n)
            dve.wait_ge(S["act_step"], 2)
            nc.vector.scalar_tensor_tensor(out=aA.rearrange("p (t n) -> p t n", t=T), in0=dt.rearrange("p (t n) -> p t n", t=T),
                                           scalar=-1.0, in1=A.unsqueeze(1).to_broadcast([P, T, 32]),
                                           op0=ALU.mult, op1=ALU.mult).then_inc(S["dta_ready"], 1)
            K.wait_full(dve, ("cum", 0))
            b = K.bank(("cum", 0))
            steps(nc.vector.tensor_copy(acum, b[:, 0:96]))
            K.took(nc.vector.tensor_copy(tot, b[:, 96:192]), ("cum", 0))
            K.wait_taken(dve, ("cum", 0))
            nc.vector.tensor_tensor(dend, tot, acum, ALU.subtract).then_inc(S["cum_ready"], 1)
            for j in range(2):
                K.wait_full(dve, ("cb", j))
                cnt = 4 if j == 0 else 2
                src = K.bank(("cb", j))[:, 0:cnt * P].rearrange("p (a n) -> p a n", a=cnt)
                for d in range(2):
                    dst = cbm[:, d, 4 * j * P:(4 * j + cnt) * P].rearrange("p (a n) -> p a n", a=cnt)
                    ins = nc.vector.tensor_tensor(dst, src, K.tri[d].unsqueeze(1).to_broadcast([P, cnt, P]), ALU.mult)
                    if d:
                        K.took(ins, ("cb", j))
            K.wait_taken(dve, ("cb", 1))
            dve.wait_ge(S["exps_ready"], 1)
            n_out = 0
            y_last = {}
            for step, u in ssd_order():
                if step == "MOD":
                    continue
                t, d, g = u
                i = units.index(u)
                name = (step, u)
                b = K.bank(name)
                yv = y[:, t, g * 512:(g + 1) * 512]
                if step in ("AB0", "AB1"):
                    k = 2 * i + (step == "AB1")
                    K.wait_full(dve, name)
                    if k >= 2:
                        dve.wait_ge(S["m_ready"], k - 1)
                    for j in range(4):
                        c = 32 * t + 16 * d + 8 * g + 4 * (step == "AB1") + j
                        ins = nc.vector.tensor_scalar(seg[:, k % 2, j * P:(j + 1) * P], b[:, j * P:(j + 1) * P],
                                                      acum[:, c:c + 1], 0.0, ALU.subtract, ALU.min)
                        if j < 3:
                            steps(ins)
                    K.took(ins, name)
                if step == "AB1":
                    for k in (2 * i, 2 * i + 1):
                        dve.wait_ge(S["exp_seg"], k + 1)
                        if i >= 1:
                            K.wait_full(dve, ("YD", units[i - 1]))
                        cb = cbm[:, d, (2 * t + g) * P:(2 * t + g + 1) * P].unsqueeze(1).to_broadcast([P, 4, P])
                        nc.vector.tensor_tensor(M[:, k % 2, :].rearrange("p (a n) -> p a n", a=4),
                                                seg[:, k % 2, :].rearrange("p (a n) -> p a n", a=4), cb,
                                                ALU.mult).then_inc(S["m_ready"], 1)
                if step == "YD":
                    dve.wait_ge(S["skip_ready"], t + 1)
                    if (t, g) in y_last:
                        dve.wait_ge(S["dve_step"], y_last[(t, g)])
                    K.wait_full(dve, name)
                    K.took(nc.vector.tensor_tensor(yv, yv, b[:, :], ALU.add), name)
                    K.wait_taken(dve, name)
                if step == "YO":
                    K.wait_full(dve, name)
                    K.took(nc.vector.tensor_tensor(h8(tmp), h8(b[:, :]), spread8(ea, u), ALU.mult), name)
                    K.wait_taken(dve, name)
                    y_last[(t, g)] = steps(nc.vector.tensor_tensor(yv, yv, tmp, ALU.add))
                if step == "CS":
                    K.wait_full(dve, name)
                    if t == 0:
                        if n_out >= 2:
                            dve.wait_ge(S["stores"], 32 + 32)
                        K.took(nc.vector.tensor_copy(outs[:, g, :], b[:, :]), name)
                        n_out += 1
                    else:
                        if ("YO", u) in K.G.names:
                            K.wait_full(dve, ("YO", u))
                        dve.wait_ge(S["ctx_loads"], 64)
                        Hs = H[:, d, g * 512:(g + 1) * 512]
                        n = steps(nc.vector.tensor_tensor(h8(Hs), h8(Hs), spread8(etot, u), ALU.mult))
                        dve.wait_ge(S["dve_step"], n)
                        K.took(nc.vector.tensor_tensor(Hs, Hs, b[:, :], ALU.add), name)


def branches(K, l):
    nc, S, io = K.nc, K.S, K.io
    z, uin = K.at(A_Z, T, D), K.at(A_UIN, KD, UIN)
    off = A_FREE
    y = K.at(off + 5376, T, D)
    oT = K.at(off, KD, TOK)
    yT = K.at(A_XBC, KD, TOK)
    uT = K.at(A_UIN, KD, TOK)
    merged = K.hn[:, :, :].rearrange("p t n -> p (t n)").rearrange("p (k n) -> p k n", k=KD)
    mean = K.at(A_CQKV, UOUT)
    std = K.at(A_CQKV + 400, UOUT)
    gs = K.at(A_CQKV + 800, 2, TOK)
    tmp = K.at(off + 3072, 2, 512)
    sqt = K.at(off + 4096, D)
    gt = K.at(A_Z, 2, D)
    uc = K.at(off + 8448, KD, UOUT)
    squ = K.at(off + 11640, KD, UOUT)
    steps = K.dve_steps
    st = K.st
    srcs = [oT, yT, uT]
    late = LateModulation(K, *K.late_rows())
    with nc.Block() as block:
        @block.gpsimd
        def _(pool):
            for t in range(T):
                nc.gpsimd.tensor_tensor(y[:, t, :], y[:, t, :], z[:, t, :], ALU.mult).then_inc(S["y_ready"], 1)
            for n in LATE_BRANCHES:
                late.finish(pool, n)

        @block.sync
        def _(sp):
            sp.wait_ge(S["y_ready"], 3)
            sp.dma_start(gt, spread(io, 2)).then_inc(S["loads3"], 16)
            for n in LATE_BRANCHES:
                K.load_weights(sp, l, K.chunks.index(("big", W_MOD + n)) + 4)
                late.store(sp, n)
            K.load_weights(sp, l, K.chunks.index(("big", W_BR + 11)) + 1)
            sp.wait_ge(S["mod_stored"], 16 * (12 - FIRST))
            K.wait_full(sp, ("yT", KD - 1))
            sp.wait_ge(S["uT_ready"], 1)
            for v, dst in zip((4, 3), norm2_rows(K)):
                sp.dma_start(dst, spread(io, v)).then_inc(S["norm_rows"], 16)
            K.load_weights(sp, l, len(K.chunks) - 1)

        @block.scalar
        def _(act):
            for k in range(KD):
                K.wait_full(act, ("oT", k))
                K.took(nc.scalar.copy(oT[:, k, :], K.bank(("oT", k))[:, 0:TOK]), ("oT", k))
            for t in range(T):
                act.wait_ge(S["y_ready"], t + 1)
                act.wait_ge(S["stats_sq"], 3 + t)
                nc.scalar.activation(sqt, y[:, t, :], ACT.Square, accum_out=st[:, 24 + t:25 + t]).then_inc(S["stats_sq"], 1)
            for n in LATE_BRANCHES:
                late.take(act, n)
            for i, (br, h, m) in enumerate(BRANCH_ORDER):
                if i == 2:
                    act.wait_ge(S["stats_var"], 2)
                    nc.scalar.activation(st[:, 27:30], st[:, 24:27], ACT.Sqrt).then_inc(S["stats_sqrt"], 1)
                for k in range(KD) if (br, h, m) == (1, 0, 0) else ():
                    K.wait_full(act, ("yT", k))
                    K.took(nc.scalar.activation(yT[:, k, :], K.bank(("yT", k))[:, 0:TOK], ACT.Copy,
                                                scale=K.vec[:, V_GS + k:V_GS + k + 1]), ("yT", k))
                name = ("gate", br, h, m)
                if i >= 2:
                    K.wait_taken(act, ("br", *BRANCH_ORDER[i - 2]))
                K.wait_full(act, name)
                c = V_BG + 8 * br + 4 * h + m
                K.took(nc.scalar.activation(gs[:, i % 2, :], K.bank(name)[:, 0:TOK], ACT.Sigmoid,
                                            bias=K.vec[:, c:c + 1]), name)
                if LN_AFTER.get((br, h, m)) == "mu":
                    K.wait_full(act, ("mu", 0))
                    K.took(nc.scalar.mul(mean, K.bank(("mu", 0))[:, 0:UOUT], 1.0 / D), ("mu", 0))
                    act.wait_ge(S["uc_ready"], 1)
                    for k in range(KD):
                        nc.scalar.activation(squ[:, k, :], uc[:, k, :], ACT.Square).then_inc(S["squares"], 1)
                if LN_AFTER.get((br, h, m)) == "var":
                    K.wait_full(act, ("var", 0))
                    K.took(nc.scalar.activation(std, K.bank(("var", 0))[:, 0:UOUT], ACT.Sqrt, scale=1.0 / D, bias=K.eps), ("var", 0))
                    act.wait_ge(S["ln_ready"], 1)
                    for k in range(KD):
                        for a, e, b0 in ((0, P, 0), (P + 15, UOUT, P)):
                            ins = nc.scalar.activation(uT[:, k, b0:b0 + e - a], uc[:, k, a:e], ACT.Silu,
                                                       scale=K.vec[:, V_LG + k:V_LG + k + 1], bias=K.vec[:, V_LB + k:V_LB + k + 1])
                    ins.then_inc(S["uT_ready"], 1)
            for t in range(T):
                act.wait_ge(S["x_added"], 2 * (t + 1))
                act.wait_ge(S["stats_sq"], 6 + t)
                nc.scalar.activation(sqt, K.x[:, t, :], ACT.Square, accum_out=st[:, 32 + t:33 + t]).then_inc(S["stats_sq"], 1)
                act.wait_ge(S["stats_var"], 3 + t)
                nc.scalar.activation(st[:, 35 + t:36 + t], st[:, 32 + t:33 + t], ACT.Sqrt).then_inc(S["stats_sqrt"], 1)
            norm2_act_take(K, act, (0,))

        @block.tensor
        def _(pe):
            for k in range(KD):
                K.wait_bank(pe, ("oT", k))
                for t in range(T):
                    mm = nc.tensor.transpose(K.bank(("oT", k))[:, t * P:(t + 1) * P], K.hn[:, t, k * P:(k + 1) * P], K.ident)
                K.full(mm)
            for n in LATE_BRANCHES:
                modulation_pe(K, pe, n)
            for br, h, m in BRANCH_ORDER:
                for k in range(KD) if (br, h, m) == (1, 0, 0) else ():
                    pe.wait_ge(S["yn_ready"], 3)
                    K.wait_bank(pe, ("yT", k))
                    for t in range(T):
                        mm = nc.tensor.transpose(K.bank(("yT", k))[:, t * P:(t + 1) * P], y[:, t, k * P:(k + 1) * P], K.ident)
                    K.full(mm)
                for what, name, src in (("g", ("gate", br, h, m), K.hT), ("o", ("br", br, h, m), srcs[br])):
                    chunk = ("big", W_BR + 4 * br + 2 * h + (what == "o"))
                    w = K.weights(chunk, KD, 512)
                    K.wait_weights(pe, chunk)
                    if what == "o" and h == 0 and m == 0:
                        if br == 0:
                            K.wait_taken(pe, ("oT", KD - 1))
                        if br == 1:
                            K.wait_taken(pe, ("yT", KD - 1))
                        if br == 2:
                            pe.wait_ge(S["uT_ready"], 1)
                    K.wait_bank(pe, name)
                    for k in range(KD):
                        mm = nc.tensor.matmul(K.bank(name)[:, 0:TOK], w[:, k, m * P:(m + 1) * P], src[:, k, :],
                                              start=k == 0, stop=k == KD - 1)
                    K.full(mm)
                if (br, h, m) in LN_AFTER:
                    name = (LN_AFTER[br, h, m], 0)
                    K.wait_bank(pe, name)
                    if name[0] == "mu":
                        pe.wait_ge(S["u_conv_done"], KD)
                    for k in range(KD):
                        if name[0] == "var":
                            pe.wait_ge(S["squares"], k + 1)
                        mm = nc.tensor.matmul(K.bank(name)[:, 0:UOUT], K.ones, (uc if name[0] == "mu" else squ)[:, k, :],
                                              start=k == 0, stop=k == KD - 1)
                    K.full(mm)
            pe.wait_ge(S["merged"], 16)
            for t in range(T):
                for h in range(2):
                    w = K.weights(("big", W_OUT + h), KD, 512)
                    K.wait_weights(pe, ("big", W_OUT + h))
                    K.wait_bank(pe, ("out", h, t))
                    for k in range(KD):
                        mm = nc.tensor.matmul(K.bank(("out", h, t))[:, :], merged[:, k, t * P:(t + 1) * P], w[:, k, :],
                                              start=k == 0, stop=k == KD - 1)
                    K.full(mm)
            norm2_pe(K, pe, (0,))

        @block.vector
        def _(dve):

            def convolution():
                for m in range(0, KD, 2):
                    yield from taps(K, dve, uc, uin, V_UW, V_UB, CW, UOUT, KD, "u_conv_done", (m, m + 1))

            conv = convolution()
            per_block = -(-CW * KD // (BRANCH_ORDER.index((1, 1, 0)) + 1))
            for i, (br, h, m) in enumerate(BRANCH_ORDER):
                if i == 1:
                    dve.wait_ge(S["stats_sq"], 6)
                    nc.vector.tensor_scalar(st[:, 24:27], st[:, 24:27], 1.0 / D, EPS, ALU.mult, ALU.add).then_inc(S["stats_var"], 1)
                if i == 4:
                    dve.wait_ge(S["stats_sqrt"], 2)
                    dve.wait_ge(S["dve_step"], steps(nc.vector.reciprocal(st[:, 27:30], st[:, 27:30])))
                    for t in range(T):
                        nc.vector.tensor_scalar(y[:, t, :], y[:, t, :], st[:, 27 + t:28 + t], None, ALU.mult).then_inc(S["yn_ready"], 1)
                for _ in range(per_block):
                    next(conv, None)
                mo = merged[:, 4 * h + m, :]
                name = ("br", br, h, m)
                K.wait_full(dve, name)
                K.wait_taken(dve, ("gate", br, h, m))
                b = K.bank(name)[:, 0:TOK]
                if br == 0:
                    K.took(nc.vector.tensor_tensor(mo, b, gs[:, i % 2, :], ALU.mult), name)
                else:
                    n = i - 8
                    if n >= 2:
                        dve.wait_ge(S["merged"], n - 1)
                    K.took(nc.vector.tensor_tensor(tmp[:, i % 2, 0:TOK], b, gs[:, i % 2, :], ALU.mult), name)
                    K.wait_taken(dve, name)
                    if br == 2:
                        dve.wait_ge(S["merged"], n - 7)
                    nc.vector.tensor_tensor(mo, mo, tmp[:, i % 2, 0:TOK], ALU.add).then_inc(S["merged"], 1)
                if (br, h, m) in LN_AFTER:
                    K.wait_taken(dve, (LN_AFTER[br, h, m], 0))
                    if LN_AFTER[br, h, m] == "mu":
                        nc.vector.tensor_tensor(uc, uc, mean.unsqueeze(1).to_broadcast([P, KD, UOUT]), ALU.subtract)\
                            .then_inc(S["uc_ready"], 1)
                    else:
                        dve.wait_ge(S["dve_step"], steps(nc.vector.reciprocal(std, std)))
                        dve.wait_ge(S["squares"], KD)
                        nc.vector.tensor_tensor(uc, uc, std.unsqueeze(1).to_broadcast([P, KD, UOUT]), ALU.mult)\
                            .then_inc(S["ln_ready"], 1)
            dve.wait_ge(S["loads3"], 16)
            for t in range(T):
                for h in range(2):
                    i = 2 * t + h
                    if i >= 2:
                        dve.wait_ge(S["x_added"], i - 1)
                    else:
                        dve.wait_ge(S["merged"], 16)
                    K.wait_full(dve, ("out", h, t))
                    K.took(nc.vector.tensor_tensor(tmp[:, i % 2, :], K.bank(("out", h, t))[:, :], gt[:, min(t, 1), h * 512:(h + 1) * 512],
                                                   ALU.mult), ("out", h, t))
                    K.wait_taken(dve, ("out", h, t))
                    xv = K.x[:, t, h * 512:(h + 1) * 512]
                    nc.vector.tensor_tensor(xv, xv, tmp[:, i % 2, :], ALU.add).then_inc(S["x_added"], 1)
                s = st[:, 32 + t:33 + t]
                dve.wait_ge(S["stats_sq"], 7 + t)
                nc.vector.tensor_scalar(s, s, 1.0 / D, EPS, ALU.mult, ALU.add).then_inc(S["stats_var"], 1)
                dve.wait_ge(S["stats_sqrt"], 3 + t)
                dve.wait_ge(S["dve_step"], steps(nc.vector.reciprocal(st[:, 35 + t:36 + t], st[:, 35 + t:36 + t])))
                if t == 0:
                    dve.wait_ge(S["norm_rows"], 32)
                    norm_apply_dve(K, dve, *norm2_rows(K), (0,))


def norm2_rows(K):
    return K.at(B_ROUTE + 15360, 2, D), K.at(B_ROUTE + 17408, 2, D)


U = 8
TRIPS = SLOTS // (2 * U)
B_ROUTE = CHUNK


def experts(K, l):
    nc, S, io = K.nc, K.S, K.io
    o = B_ROUTE
    gw, ei = K.at(o, T * SLOTS), K.at(o + 384, T * SLOTS).bitcast(U32)
    g2 = K.at(o + 768, 2, D)
    qT = K.at(o + 2816, 16, TOK)
    keys = K.at(o + 8960, 2, P)
    s = K.at(o + 9216, 16 * NKEYS)
    cand = K.at(o + 13312, PH, 256)
    mrow, srow = norm2_rows(K)
    acc, junk = K.at(o + 15360, D), K.at(o + 16384, D)
    hot = K.at(o + 17408, SLOTS, TOPK)
    o2 = o + 19456
    v1 = K.at(o2, 16, TOPK)
    x1 = K.at(o2 + 256, 16, TOPK).bitcast(U32)
    f1 = K.at(o2 + 512, 16, TOPK)
    v2 = K.at(o2 + 768, PH, TOPK)
    x2 = K.at(o2 + 896, PH, TOPK).bitcast(U32)
    hi, lo = K.at(o2 + 1024, SLOTS).bitcast(U32), K.at(o2 + 1152, SLOTS).bitcast(U32)
    hf, lf = K.at(o2 + 1280, SLOTS), K.at(o2 + 1408, SLOTS)
    e1, e2 = K.at(o2 + 1536, SLOTS), K.at(o2 + 1664, SLOTS)
    ex, sm = K.at(o2 + 1792, PH, TOPK), K.at(o2 + 1920, PH)
    o3 = o2 + 1936
    stage = K.at(o3, 2, U).bitcast(U32)
    dots, gel, wgt, gws = [K.at(o3 + 16 + 16 * i, 2, U) for i in range(4)]
    tick = K.at(o3 + 80, 1 + 2 * U)
    spare = [K.at(o + 11264, 2 * D), K.at(K.pool_n - 2 * D, 2 * D)]

    def row(k):
        if k < 2:
            return spare[k]
        a = K.place(("big", W_PQ + k // 2 - 1)) + k % 2 * 2 * D
        return K.arena[:, a:a + 2 * D]

    steps = K.dve_steps
    with nc.Block() as block:
        @block.sync
        def _(sp):
            K.load_weights(sp, l, len(K.chunks))
            sp.dma_start(keys, io["keysT"][bass.ds(l, 1)].rearrange("a p n -> p (a n)").rearrange("p (d n) -> p d n", d=2)).then_inc(S["key_loads"], 16)
            sp.dma_start(g2, spread(io, 5)).then_inc(S["key_loads"], 16)

        @block.gpsimd
        def _(pool):
            def pass_wait(n):
                nc.gpsimd.tensor_tensor(tick[:, 1 + n:2 + n], tick[:, 0:1], tick[:, 0:1], ALU.add)

            nc.gpsimd.memset(tick[:, 0:1], 0.0).then_inc(S["pool_step"], 1)
            pool.wait_ge(S["pool_step"], 1)
            for t, half in [(t, half) for t in range(T) for half in range(2)]:
                first, last = half * TRIPS // 2, (half + 1) * TRIPS // 2
                pool.wait_ge(S["routed"], 2 * t + half + 1)
                with pool.Fori(first, last) as i:
                    for r in range(2):
                        nc.gpsimd.tensor_copy(stage[:, r, :], ei[:, bass.ds(i * (2 * U) + (t * SLOTS + r * U), U)])\
                            .then_inc(S["staged"], 1)
                        for k in range(U):
                            if k == 0:
                                pool.wait_ge(S["staged"], i * 2 + (2 * t * TRIPS + r + 1))
                            if k >= 2 and (t, half) == (0, 0):
                                K.wait_full(pool, ("pq", 4 * (k // 2 - 1) + 3))
                            pool.wait_ge(S["slot_done"], i * (2 * U) + (t * SLOTS + r * U + k + 1))
                            pass_wait(r * U + k)
                            nc.gpsimd.indirect_dma_start(row(k), None, io["experts"],
                                                         bass.IndirectOffsetOnAxis(ap=stage[:, r, k:k + 1], axis=0))\
                                .then_inc(K.gathered[k], 16)

        @block.scalar
        def _(act):
            def soft(t):
                act.wait_ge(S["soft_in"], t + 1)
                nc.scalar.activation(ex, ex, ACT.Exp).then_inc(S["soft_exp"], 1)

            for half in range(2):
                cs = (2 * half, 2 * half + 1)
                for c in cs:
                    K.wait_full(act, ("pq0", c))
                    K.took(nc.scalar.copy(qT[:, 4 * c:4 * c + 4, 0:P],
                                          K.bank(("pq0", c))[:, :].rearrange("p (k n) -> p k n", k=4)), ("pq0", c))
                for c in cs:
                    K.wait_full(act, ("ps", 0, c))
                    K.took(nc.scalar.copy(s[:, c * 512:(c + 1) * 512], K.bank(("ps", 0, c))[:, :]), ("ps", 0, c))
            norm2_act_take(K, act, (1, 2))
            for m in range(8):
                K.wait_full(act, ("pq", m))
                K.took(nc.scalar.copy(qT[:, m, P:TOK], K.bank(("pq", m))[:, 0:2 * P]), ("pq", m))
            for t in range(T):
                soft(t)
                act.wait_ge(S["gates_ready"], t + 1)
                with act.Fori(0, TRIPS) as i:
                    nc.scalar.copy(gws.rearrange("p a b -> p (a b)"), gw[:, bass.ds(i * (2 * U) + t * SLOTS, 2 * U)])\
                        .then_inc(S["gw_staged"], 1)
                    act.wait_ge(S["gw_staged"], i + (t * TRIPS + 1))
                    for n in range(2 * U):
                        r, k = n // U, n % U
                        act.wait_ge(S["dot_done"], i * (2 * U) + (t * SLOTS + n + 1))
                        nc.scalar.activation(gel[:, r, k:k + 1], dots[:, r, k:k + 1], ACT.Gelu).then_inc(S["gelu_done"], 1)
                        act.wait_ge(S["gelu_done"], i * (2 * U) + (t * SLOTS + n + 1))
                        nc.scalar.activation(wgt[:, r, k:k + 1], gel[:, r, k:k + 1], ACT.Copy,
                                             scale=gws[:, r, k:k + 1]).then_inc(S["weight_done"], 1)
                    act.wait_ge(S["weight_done"], i * (2 * U) + (t * SLOTS + 2 * U))

        @block.tensor
        def _(pe):
            def scores(t, cs=range(4)):
                for c in cs:
                    K.wait_bank(pe, ("ps", t, c))
                    for j in range(4):
                        m = 4 * c + j
                        mm = nc.tensor.matmul(K.bank(("ps", t, c))[:, j * P:(j + 1) * P], qT[:, m, t * P:(t + 1) * P],
                                              keys[:, m % 2, :], start=True, stop=True)
                    K.full(mm)

            K.wait_taken(pe, ("n2", 0, 1))
            for half in range(2):
                cs = (2 * half, 2 * half + 1)
                for c in cs:
                    chunk = ("big", W_PQ + c)
                    wt = K.weights(chunk, KD, 512)
                    K.wait_weights(pe, chunk)
                    K.wait_bank(pe, ("pq0", c))
                    for j in range(4):
                        for k in range(KD):
                            mm = nc.tensor.matmul(K.bank(("pq0", c))[:, j * P:(j + 1) * P], wt[:, k, j * P:(j + 1) * P],
                                                  K.hT[:, k, 0:P], start=k == 0, stop=k == KD - 1)
                    K.full(mm)
                pe.wait_ge(S["key_loads"], 32)
                K.wait_taken(pe, ("pq0", cs[1]))
                scores(0, cs)
            norm2_pe(K, pe, (1, 2))
            K.wait_taken(pe, ("n2", 2, 1))
            for m in range(16):
                wt = K.weights(("big", W_PQ + m // 4), KD, 512)
                K.wait_bank(pe, ("pq", m))
                for k in range(KD):
                    mm = nc.tensor.matmul(K.bank(("pq", m))[:, 0:2 * P], wt[:, k, (m % 4) * P:(m % 4 + 1) * P],
                                          K.hT[:, k, P:TOK], start=k == 0, stop=k == KD - 1)
                K.full(mm)
            K.wait_taken(pe, ("pq", 7))
            K.wait_taken(pe, ("pq", 15))
            scores(1)
            scores(2)

        @block.vector
        def _(dve):
            norm_apply_dve(K, dve, mrow, srow, (1, 2))
            dve.wait_ge(S["h_ready"], 6)

            def top16(src, vals, idx, ms):
                for m in ms:
                    k = steps(nc.vector.max(out=vals[:, m, 0:8], in_=src[:, m, :]))
                dve.wait_ge(S["dve_step"], k)
                for m in ms:
                    k = steps(nc.vector.max_index(idx[:, m, 0:8], vals[:, m, 0:8], src[:, m, :]))
                dve.wait_ge(S["dve_step"], k)
                for m in ms:
                    k = steps(nc.vector.match_replace(out=src[:, m, :], in_to_replace=vals[:, m, 0:8],
                                                      in_values=src[:, m, :], imm_value=NEG))
                dve.wait_ge(S["dve_step"], k)
                for m in ms:
                    k = steps(nc.vector.max(out=vals[:, m, 8:16], in_=src[:, m, :]))
                dve.wait_ge(S["dve_step"], k)
                for m in ms:
                    k = steps(nc.vector.max_index(idx[:, m, 8:16], vals[:, m, 8:16], src[:, m, :]))
                dve.wait_ge(S["dve_step"], k)

            def chosen(places, ids, out, heads):
                n = len(heads) * TOPK
                a = heads[0] * TOPK
                iota = K.C[:, C_IOTA:C_IOTA + TOPK].unsqueeze(1).to_broadcast([P, n, TOPK])
                some = hot[:, a:a + n, :]
                k = steps(nc.vector.tensor_tensor(some, places[:, a:a + n].unsqueeze(2).to_broadcast([P, n, TOPK]), iota,
                                                  ALU.is_equal))
                dve.wait_ge(S["dve_step"], k)
                for h in heads:
                    hv = hot[:, h * TOPK:(h + 1) * TOPK, :]
                    k = steps(nc.vector.tensor_tensor(hv, hv, ids[:, 2 * h, :].unsqueeze(1).to_broadcast([P, TOPK, TOPK]), ALU.mult))
                dve.wait_ge(S["dve_step"], k)
                return steps(nc.vector.tensor_reduce(out[:, a:a + n], some, AX.X, ALU.add))

            def route_keys(t, half):
                for c in (2 * half, 2 * half + 1) if t else ():
                    K.wait_full(dve, ("ps", t, c))
                    K.took(nc.vector.tensor_copy(s[:, c * 512:(c + 1) * 512], K.bank(("ps", t, c))[:, :]), ("ps", t, c))
                K.wait_taken(dve, ("ps", t, 2 * half + 1))
                sv = s.rearrange("p (m n) -> p m n", m=16)
                top16(sv, v1, x1, range(8 * half, 8 * half + 8))
                k = steps(nc.vector.tensor_copy(f1[:, 8 * half:8 * half + 8, :], x1[:, 8 * half:8 * half + 8, :]))
                dve.wait_ge(S["dve_step"], k)

            def route_experts(t, heads):
                a, e = heads[0] * TOPK, (heads[-1] + 1) * TOPK
                hs = slice(heads[0], heads[-1] + 1)
                for h in heads:
                    k = steps(nc.vector.tensor_tensor(
                        cand[:, h, :].rearrange("p (a b) -> p a b", a=TOPK),
                        v1[:, 2 * h, :].unsqueeze(2).to_broadcast([P, TOPK, TOPK]),
                        v1[:, 2 * h + 1, :].unsqueeze(1).to_broadcast([P, TOPK, TOPK]), ALU.add))
                dve.wait_ge(S["dve_step"], k)
                top16(cand, v2, x2, heads)
                diff = nc.vector.tensor_tensor(ex[:, hs, :], v2[:, hs, :], v2[:, hs, 0:1].to_broadcast([P, len(heads), TOPK]),
                                               ALU.subtract)
                if e == SLOTS:
                    diff.then_inc(S["soft_in"], 1)
                else:
                    steps(diff)
                xf = x2.rearrange("p a b -> p (a b)")[:, a:e]
                steps(nc.vector.tensor_scalar(hi[:, a:e], xf, 4, None, ALU.logical_shift_right))
                k = steps(nc.vector.tensor_scalar(lo[:, a:e], xf, 15, None, ALU.bitwise_and))
                dve.wait_ge(S["dve_step"], k)
                steps(nc.vector.tensor_copy(hf[:, a:e], hi[:, a:e]))
                k = steps(nc.vector.tensor_copy(lf[:, a:e], lo[:, a:e]))
                dve.wait_ge(S["dve_step"], k)
                k = chosen(hf, f1, e1, heads)
                dve.wait_ge(S["dve_step"], k)
                k = chosen(lf, f1[:, 1:16, :], e2, heads)
                dve.wait_ge(S["dve_step"], k)
                k = steps(nc.vector.scalar_tensor_tensor(out=e1[:, a:e], in0=e1[:, a:e], scalar=float(NKEYS), in1=e2[:, a:e],
                                                         op0=ALU.mult, op1=ALU.add))
                dve.wait_ge(S["dve_step"], k)
                k = steps(nc.vector.tensor_scalar(e1[:, a:e], e1[:, a:e], K.row[:, R_BASE:R_BASE + 1], None, ALU.add))
                dve.wait_ge(S["dve_step"], k)
                copy = nc.vector.tensor_copy(ei[:, t * SLOTS + a:t * SLOTS + e], e1[:, a:e])
                if e % (SLOTS // 2) == 0:
                    copy.then_inc(S["routed"], 1)
                    dve.wait_ge(S["routed"], 2 * t + e // (SLOTS // 2))
                else:
                    dve.wait_ge(S["dve_step"], steps(copy))

            def route_gates(t):
                dve.wait_ge(S["soft_exp"], t + 1)
                k = steps(nc.vector.tensor_reduce(sm, ex, AX.X, ALU.add))
                dve.wait_ge(S["dve_step"], k)
                k = steps(nc.vector.reciprocal(sm, sm))
                dve.wait_ge(S["dve_step"], k)
                nc.vector.tensor_tensor(gw[:, t * SLOTS:(t + 1) * SLOTS].rearrange("p (a b) -> p a b", a=PH), ex,
                                        sm.unsqueeze(2).to_broadcast([P, PH, TOPK]), ALU.mult).then_inc(S["gates_ready"], 1)
                dve.wait_ge(S["gates_ready"], t + 1)

            def dot(t, i, n):
                r, k = n // U, n % U
                dve.wait_ge(K.gathered[k], (l * (2 * T * TRIPS) + i * 2) * 16 + 16 * (2 * t * TRIPS + r + 1))
                if n:
                    dve.wait_ge(S["dot_done"], i * (2 * U) + (t * SLOTS + n))
                nc.vector.tensor_tensor_reduce(out=junk, in0=row(k)[:, 0:D], in1=K.h2(t), scale=1.0, scalar=0.0,
                                               op0=ALU.mult, op1=ALU.add, accum_out=dots[:, r, k:k + 1]).then_inc(S["dot_done"], 1)

            def add(t, i, n):
                r, k = n // U, n % U
                dve.wait_ge(S["weight_done"], i * (2 * U) + (t * SLOTS + n + 1))
                dve.wait_ge(S["slot_done"], i * (2 * U) + (t * SLOTS + n + U))
                nc.vector.scalar_tensor_tensor(out=acc, in0=row(k)[:, D:2 * D], scalar=wgt[:, r, k:k + 1], in1=acc,
                                               op0=ALU.mult, op1=ALU.add).then_inc(S["slot_done"], 1)

            def trip(t, i, beside=None):
                for n in range(2 * U):
                    dot(t, i, n)
                    if beside:
                        beside(n)
                    if n:
                        add(t, i, n - 1)
                dve.wait_ge(S["dot_done"], i * (2 * U) + (t * SLOTS + 2 * U))
                add(t, i, 2 * U - 1)

            def slots(t, first, last):
                with dve.Fori(first, last) as i:
                    trip(t, i)

            def take_queries(n):
                if n < 8:
                    K.wait_full(dve, ("pq", 8 + n))
                    K.took(nc.vector.tensor_copy(qT[:, 8 + n, P:TOK], K.bank(("pq", 8 + n))[:, 0:2 * P]), ("pq", 8 + n))

            nc.vector.memset(acc, 0.0).then_inc(S["slot_done"], U)
            for half in range(2):
                route_keys(0, half)
                route_experts(0, range(4 * half, 4 * half + 4))
            route_gates(0)
            dve.wait_ge(S["key_loads"], 32)
            for t in range(T):
                if t < T - 1:
                    if t == 0:
                        trip(0, 0, take_queries)
                    else:
                        slots(t, 0, 1)
                    route_keys(t + 1, 0)
                    slots(t, 1, 2)
                    route_keys(t + 1, 1)
                    for i, (first, last) in enumerate(((2, 4), (4, 5), (5, 6), (6, 7))):
                        slots(t, first, last)
                        route_experts(t + 1, range(2 * i, 2 * i + 2))
                    slots(t, 7, TRIPS)
                else:
                    slots(t, 0, TRIPS)
                dve.wait_ge(S["slot_done"], (t + 1) * SLOTS + U)
                k = steps(nc.vector.tensor_tensor(junk, acc, g2[:, min(t, 1), :], ALU.mult))
                dve.wait_ge(S["dve_step"], k)
                k = steps(nc.vector.tensor_tensor(K.x[:, t, :], K.x[:, t, :], junk, ALU.add))
                if t < T - 1:
                    k = steps(nc.vector.memset(acc, 0.0))
                    dve.wait_ge(S["dve_step"], k)
                    route_gates(t + 1)


def trunk_kernel(nc, io):
    K = Kernel(nc, io)
    S = K.S
    with nc.Block() as block:
        @block.sync
        def _(sp):
            sp.dma_start(K.x[:, :, :], io["x"].rearrange("(t p) n -> p t n", p=P)).then_inc(S["loads"], 16)
            sp.dma_start(K.C[:, :], io["consts"]).then_inc(S["loads"], 16)
            sp.wait_ge(S["loads"], 32)
    nc.all_engine_barrier(sems_to_clear=S.span())
    with nc.Fori(0, DEPTH) as l:
        K.loaded, K.pe_at, K.takes = 0, 0, {"act": 0, "dve": 0, "norm": 0}
        modulate_and_norm(K, l)
        project_in(K, l)
        attention(K, l)
        ssd(K, l)
        branches(K, l)
        experts(K, l)
        assert K.loaded == len(K.chunks) and K.pe_at == len(K.G.names)
        nc.all_engine_barrier(sems_to_clear=S.span())
    final_norm(K)


def final_norm(K):
    nc, S, io = K.nc, K.S, K.io
    gf = K.at(0, D)
    sq = K.at(D, D)
    y = K.at(2 * D, T, D)
    K.dve_steps = Steps(S["dve_step"])
    with nc.Block() as block:
        @block.sync
        def _(sp):
            sp.dma_start(gf, io["g_final"].to_broadcast([P, D])).then_inc(S["loads"], 16)
            for t in range(T):
                sp.wait_ge(S["h_ready"], t + 1)
                sp.dma_start(io["y"][t * P:(t + 1) * P, :], y[:, t, :]).then_inc(S["stores"], 16)
            sp.wait_ge(S["stores"], 16 * T)

        @block.scalar
        def _(act):
            norm_act_stats(K, act, sq, 0)

        @block.vector
        def _(dve):
            norm_stats_dve(K, dve, 0)
            dve.wait_ge(S["loads"], 16)
            for t in range(T):
                nc.vector.scalar_tensor_tensor(out=y[:, t, :], in0=K.x[:, t, :], scalar=K.st[:, 3 + t:4 + t], in1=gf,
                                               op0=ALU.mult, op1=ALU.mult).then_inc(S["h_ready"], 1)


def kernel(**a):
    import concourse.bacc as _bacc
    from concourse.bass_utils import run_bass_kernel_spmd as _run

    a = {k: np.ascontiguousarray(v) for k, v in a.items()}
    L = DEPTH

    def big(w, cols):
        w = w[:, :, cols]
        n = w.shape[2] // 512
        return w.reshape(L, KD, P, n, 512).transpose(0, 3, 2, 1, 4).reshape(L, n, P, CHUNK)

    OKR, OZ, OX, ODT, OG = 512, 544, 1568, 3104, 3136
    w_in = a["w_in"]
    glu = big(w_in, slice(OG, OG + 2 * D))
    parts = [big(a["w_mod"], slice(None)), big(w_in, slice(0, 512)), big(w_in, slice(OZ, OZ + D)),
             big(w_in, slice(OX, OX + XC * P)), glu[:, 2:3], glu[:, 0:1], glu[:, 3:4], glu[:, 1:2]]
    gate = big(a["w_gate"], slice(None))
    for b, name in enumerate(("w_attn_out", "w_ssd_out", "w_cv_pw2")):
        w = big(a[name], slice(None))
        for h in range(2):
            parts += [gate[:, 2 * b + h:2 * b + h + 1], w[:, h:h + 1]]
    parts += [big(a["w_out"], slice(None)), big(a["w_peer_q"], slice(None))]
    w_big = np.concatenate(parts, axis=1)
    small = np.concatenate([w_in[:, :, OKR:OZ], w_in[:, :, ODT:OG]], axis=2)
    w_small = small.reshape(L, 1, KD, P, 64).transpose(0, 1, 3, 2, 4).reshape(L, 1, P, KD * 64)
    w_uq = a["w_uq"].reshape(L, KQ, P, 3, 512).transpose(0, 3, 2, 1, 4).reshape(L, 3, P, KQ * 512)
    w_ukv = a["w_ukv"].reshape(L, 1, P, 2048)

    def cols(v):
        return v.reshape(L, -1, P).transpose(0, 2, 1)

    def taps(w, n):
        return w.reshape(L, w.shape[1], n, P).transpose(0, 3, 2, 1).reshape(L, P, -1)

    vecs = np.concatenate([cols(a["g_q_norm"]), taps(a["ssd_conv_w"], XC), cols(a["ssd_conv_b"]), taps(a["cv_dw_w"], KD),
                           cols(a["cv_dw_b"]), cols(a["cv_ln_g"]), cols(a["cv_ln_b"]), cols(a["g_ssd_norm"]),
                           cols(a["b_gate"])], axis=2)
    base = (np.arange(L) * NKEYS * NKEYS).astype(np.float32)[:, None]
    rows = np.concatenate([a["g_kv_norm"], a["ssd_dt_bias"].reshape(L, 32), a["ssd_a_log"].reshape(L, 32), a["ssd_d"], base], axis=1)

    consts = np.zeros((P, N_CONST), np.float32)
    i = np.arange(P)
    consts[:, C_ID:C_ID + P] = np.eye(P)
    consts[:, C_TF:C_TF + P] = i[:, None] <= i[None, :]
    consts[:, C_TB:C_TB + P] = i[:, None] >= i[None, :]
    consts[:, C_ONE:C_ONE + P] = 1.0
    inv = (np.float32(10000.0) ** (-np.arange(8, dtype=np.float32) / np.float32(8))).astype(np.float32)
    for t in range(2):
        tok = t * P + i
        for ax, pos in enumerate((tok // 64, tok % 64)):
            ang = pos.astype(np.float32)[:, None] * inv
            for half in range(2):
                c = 32 * t + 16 * ax + 8 * half
                consts[:, C_RC + c:C_RC + c + 8] = np.cos(ang)
                consts[:, C_RS + c:C_RS + c + 8] = np.sin(ang) if half else -np.sin(ang)
    consts[:, C_IOTA:C_IOTA + TOPK] = np.arange(TOPK)
    consts[:, C_EPS] = EPS
    consts[:, C_EPS + 1] = 1.0

    h0 = np.stack([a["state_ssd_fwd"][0], a["state_ssd_bwd"][0]], axis=1)
    arrays = {
        "x": np.concatenate([a["x_prompt"][0], a["x_sample"][0]], axis=0),
        "c_rows": np.stack([a["c_ctx"].reshape(KD, P), a["c"][0].reshape(KD, P)], axis=2).transpose(1, 0, 2).reshape(P, KD * 2),
        "w_big": w_big, "w_small": w_small, "w_uq": w_uq, "w_ukv": w_ukv,
        "mod_rows": np.concatenate([a["b_mod"], a["g_norm1"], a["g_norm2"]], axis=1),
        "vecs": vecs, "rows": rows, "consts": consts,
        "cache_kvT": a["cache_ckv"][0].transpose(0, 2, 1), "cache_krT": a["cache_krope"][0].transpose(0, 2, 1),
        "h0T": h0.transpose(0, 4, 1, 2, 3).reshape(L, P, 2 * D),
        "keysT": a["peer_keys"].transpose(0, 3, 1, 2).reshape(L, P, 2 * P),
        "experts": np.concatenate([a["peer_u"], a["peer_v"]], axis=2).reshape(L * NKEYS * NKEYS, 2 * D),
        "g_final": a["g_final"].reshape(1, D),
    }
    outs = {"y": (TOK, D), "new_ckv": (L, P, KV_RANK), "new_krope": (L, P, ROPE), "new_state": (L, 2, P, D)}
    nc = _bacc.Bacc("TRN2", target_bir_lowering=False, num_devices=1)
    io = {}
    for name in arrays:
        arrays[name] = np.ascontiguousarray(arrays[name])
        io[name] = nc.dram_tensor(f"in_{name}_dram", arrays[name].shape, F32, kind="ExternalInput").ap()
    for name, shape in outs.items():
        io[name] = nc.dram_tensor(f"out_{name}_dram", shape, F32, kind="ExternalOutput").ap()
    io["mod_scratch"] = nc.dram_tensor("mod_scratch", (2, 6 * D), F32, kind="Internal").ap()
    trunk_kernel(nc, io)
    r = _run(nc, [{f"in_{k}_dram": v for k, v in arrays.items()}], core_ids=[0]).results[0]
    y = r["out_y_dram"]
    s = r["out_new_state_dram"].reshape(L, 2, P, SH, SP_).transpose(1, 0, 3, 4, 2)[:, None]
    s = np.ascontiguousarray(s)
    return (y[None, :P], y[None, P:], r["out_new_ckv_dram"][None], r["out_new_krope_dram"][None], s[0], s[1])
```
